# Optimizing a Trainium2 kernel written in Bass

```python
import jax, jax.numpy as jnp
from jax import lax
import numpy as np

D_MODEL = 1024
BATCH = 1
SEQ = 512
DEPTH = 2

ROPE_THETA = 500000.0
NORM_EPS = 1e-6
Q_BLOCK = 128
NEG_INF = -1e30

MLA_HEADS = 8
MLA_Q_RANK = 256
MLA_KV_RANK = 128
MLA_NOPE_DIM = 64
MLA_ROPE_DIM = 32
MLA_V_DIM = 64
MLA_QK_DIM = MLA_NOPE_DIM + MLA_ROPE_DIM

NSA_HEADS = 8
NSA_KV_HEADS = 2
NSA_GROUP = NSA_HEADS // NSA_KV_HEADS
NSA_HEAD_DIM = 64
NSA_ROT_DIM = NSA_HEAD_DIM // 4
NSA_BRANCHES = 3
CMP_LEN = 32
CMP_STRIDE = 16
CMP_HIDDEN = 128
SLC_LEN = 64
SLC_TOPK = 16
WINDOW = 512
FORCE_SCORE = 1e6

D_MIX = MLA_HEADS * MLA_V_DIM + NSA_HEADS * NSA_HEAD_DIM
D_FF = 2816
CONV_WIDTH = 3

IN_SPLITS = (MLA_Q_RANK, MLA_KV_RANK, MLA_ROPE_DIM, NSA_HEADS * NSA_HEAD_DIM,
             NSA_BRANCHES * 2 * NSA_KV_HEADS * NSA_HEAD_DIM, NSA_HEADS * NSA_BRANCHES)
IN_COLS = sum(IN_SPLITS)
SPLIT_POINTS = tuple(int(v) for v in np.cumsum(IN_SPLITS)[:-1])

kernel_name = 'hybrid_mla_nsa_convffn'

def rms_norm(x, g):
    xf = x.astype(jnp.float32)
    y = xf * lax.rsqrt(jnp.mean(xf * xf, axis=-1, keepdims=True) + NORM_EPS)
    return (y * g.astype(jnp.float32)).astype(x.dtype)

def rope_tables(seq, dim):
    inv = ROPE_THETA ** (-jnp.arange(0, dim, 2, dtype=jnp.float32) / dim)
    ang = jnp.arange(seq, dtype=jnp.float32)[:, None] * inv[None, :]
    return jnp.cos(ang), jnp.sin(ang)

def apply_rope(x, cos, sin):
    half = x.shape[-1] // 2
    x1, x2 = x[..., :half], x[..., half:]
    c = cos[None, :, None, :].astype(x.dtype)
    s = sin[None, :, None, :].astype(x.dtype)
    return jnp.concatenate([x1 * c - x2 * s, x1 * s + x2 * c], axis=-1)

def partial_rope(x, cos, sin):
    return jnp.concatenate([apply_rope(x[..., :NSA_ROT_DIM], cos, sin), x[..., NSA_ROT_DIM:]], axis=-1)

def masked_softmax(logits, mask):
    p = jax.nn.softmax(jnp.where(mask, logits.astype(jnp.float32), NEG_INF), axis=-1)
    return jnp.where(mask, p, 0.0)

def to_blocks(t):
    b, s = t.shape[:2]
    t = t.reshape((b, s // Q_BLOCK, Q_BLOCK) + t.shape[2:])
    return jnp.moveaxis(t, 1, 0)

def from_blocks(t):
    t = jnp.moveaxis(t, 0, 1)
    return t.reshape((t.shape[0], t.shape[1] * t.shape[2]) + t.shape[3:])

def mla_attention(q_lat, kv_lat, k_rope, q_norm, kv_norm, w_uq, w_ukv, cos, sin):
    b, s, _ = q_lat.shape
    q = (rms_norm(q_lat, q_norm) @ w_uq).reshape(b, s, MLA_HEADS, MLA_QK_DIM)
    q = jnp.concatenate([q[..., :MLA_NOPE_DIM], apply_rope(q[..., MLA_NOPE_DIM:], cos, sin)], axis=-1)
    kv = (rms_norm(kv_lat, kv_norm) @ w_ukv).reshape(b, s, MLA_HEADS, MLA_NOPE_DIM + MLA_V_DIM)
    k_pe = apply_rope(k_rope[:, :, None, :], cos, sin)
    k = jnp.concatenate([kv[..., :MLA_NOPE_DIM],
                         jnp.broadcast_to(k_pe, (b, s, MLA_HEADS, MLA_ROPE_DIM))], axis=-1)
    v = kv[..., MLA_NOPE_DIM:]
    scale = MLA_QK_DIM ** -0.5
    kpos = jnp.arange(s)

    def block(args):
        i, qi = args
        qpos = i * Q_BLOCK + jnp.arange(Q_BLOCK)
        logits = jnp.einsum('bqhd,bkhd->bhqk', qi, k) * scale
        p = masked_softmax(logits, kpos[None, :] <= qpos[:, None])
        return jnp.einsum('bhqk,bkhd->bqhd', p.astype(v.dtype), v)

    o = lax.map(block, (jnp.arange(s // Q_BLOCK), to_blocks(q)))
    return from_blocks(o).reshape(b, s, MLA_HEADS * MLA_V_DIM)

def compress(t, pos, w1, b1, w2):
    b, s, g, d = t.shape
    n_c = (s - CMP_LEN) // CMP_STRIDE + 1
    idx = jnp.arange(n_c)[:, None] * CMP_STRIDE + jnp.arange(CMP_LEN)[None, :]
    blocks = t[:, idx] + pos[None, None, :, None, :]
    flat = jnp.moveaxis(blocks, 3, 2).reshape(b, n_c, g, CMP_LEN * d)
    return jax.nn.gelu(flat @ w1 + b1) @ w2

def nsa_attention(q, kv, gate_logits, gate_bias, cmp_pos, cmp_w1, cmp_b1, cmp_w2, cos, sin):
    b, s = q.shape[:2]
    q = partial_rope(q, cos, sin)
    k_cmp = compress(partial_rope(kv[:, :, 0, 0], cos, sin), cmp_pos[0], cmp_w1[0], cmp_b1[0], cmp_w2[0])
    v_cmp = compress(kv[:, :, 0, 1], cmp_pos[1], cmp_w1[1], cmp_b1[1], cmp_w2[1])
    k_slc = jnp.moveaxis(partial_rope(kv[:, :, 1, 0], cos, sin), 2, 1)
    v_slc = jnp.moveaxis(kv[:, :, 1, 1], 2, 1)
    pad = ((0, 0), (WINDOW, 0), (0, 0), (0, 0))
    k_win = jnp.pad(partial_rope(kv[:, :, 2, 0], cos, sin), pad)
    v_win = jnp.pad(kv[:, :, 2, 1], pad)
    gates = jax.nn.sigmoid((gate_logits + gate_bias).astype(jnp.float32)).astype(q.dtype)
    gates = gates.reshape(b, s, NSA_KV_HEADS, NSA_GROUP, NSA_BRANCHES)

    n_c = k_cmp.shape[1]
    n_s = s // SLC_LEN
    top = min(SLC_TOPK, n_s)
    cmp_start = jnp.arange(n_c) * CMP_STRIDE
    cmp_end = cmp_start + CMP_LEN - 1
    slc_start = jnp.arange(n_s) * SLC_LEN
    overlap = ((cmp_start[:, None] <= slc_start[None, :] + SLC_LEN - 1)
               & (cmp_end[:, None] >= slc_start[None, :])).astype(jnp.float32)
    blk_id = jnp.arange(n_s)
    tok_off = jnp.arange(SLC_LEN)
    b_ix = jnp.arange(b)[:, None, None]
    g_ix = jnp.arange(NSA_KV_HEADS)[None, :, None]
    scale = NSA_HEAD_DIM ** -0.5

    def block(args):
        i, qi, gi = args
        qpos = i * Q_BLOCK + jnp.arange(Q_BLOCK)
        qg = qi.reshape(b, Q_BLOCK, NSA_KV_HEADS, NSA_GROUP, NSA_HEAD_DIM)
        lc = jnp.einsum('bqghd,bcgd->bghqc', qg, k_cmp) * scale
        pc = masked_softmax(lc, cmp_end[None, :] <= qpos[:, None])
        o_cmp = jnp.einsum('bghqc,bcgd->bqghd', pc.astype(v_cmp.dtype), v_cmp)
        imp = jnp.einsum('bghqc,cs->bgqs', pc, overlap)
        cur = (qpos // SLC_LEN)[:, None]
        forced = (blk_id[None, :] == 0) | (blk_id[None, :] == cur) | (blk_id[None, :] == cur - 1)
        score = jnp.where(forced, FORCE_SCORE, jnp.where(blk_id[None, :] <= cur, imp, -1.0))
        top_val, top_idx = lax.top_k(score, top)
        tok = top_idx[..., None] * SLC_LEN + tok_off
        tok_mask = ((top_val >= 0.0)[..., None] & (tok <= qpos[:, None, None]))
        tok_mask = tok_mask.reshape(b, NSA_KV_HEADS, Q_BLOCK, top * SLC_LEN)
        flat_idx = tok.reshape(b, NSA_KV_HEADS, Q_BLOCK * top * SLC_LEN)
        k_sel = k_slc[b_ix, g_ix, flat_idx].reshape(b, NSA_KV_HEADS, Q_BLOCK, top * SLC_LEN, NSA_HEAD_DIM)
        v_sel = v_slc[b_ix, g_ix, flat_idx].reshape(b, NSA_KV_HEADS, Q_BLOCK, top * SLC_LEN, NSA_HEAD_DIM)
        ls = jnp.einsum('bqghd,bgqnd->bghqn', qg, k_sel) * scale
        ps = masked_softmax(ls, tok_mask[:, :, None])
        o_slc = jnp.einsum('bghqn,bgqnd->bqghd', ps.astype(v_sel.dtype), v_sel)
        kw = lax.dynamic_slice_in_dim(k_win, i * Q_BLOCK, Q_BLOCK + WINDOW, axis=1)
        vw = lax.dynamic_slice_in_dim(v_win, i * Q_BLOCK, Q_BLOCK + WINDOW, axis=1)
        kpos = i * Q_BLOCK - WINDOW + jnp.arange(Q_BLOCK + WINDOW)
        mw = ((kpos[None, :] >= 0) & (kpos[None, :] <= qpos[:, None])
              & (kpos[None, :] > qpos[:, None] - WINDOW))
        lw = jnp.einsum('bqghd,bkgd->bghqk', qg, kw) * scale
        pw = masked_softmax(lw, mw)
        o_win = jnp.einsum('bghqk,bkgd->bqghd', pw.astype(vw.dtype), vw)
        o = gi[..., 0:1] * o_cmp + gi[..., 1:2] * o_slc + gi[..., 2:3] * o_win
        return o.reshape(b, Q_BLOCK, NSA_HEADS * NSA_HEAD_DIM)

    o = lax.map(block, (jnp.arange(s // Q_BLOCK), to_blocks(q), to_blocks(gates)))
    return from_blocks(o)

def conv_ffn(x, w_up, conv_w, conv_b, w_down):
    h = x @ w_up
    c = h.shape[-1]
    h = lax.conv_general_dilated(h, conv_w[:, None, :].astype(h.dtype), window_strides=(1,),
                                 padding=((CONV_WIDTH - 1, 0),),
                                 dimension_numbers=('NWC', 'WIO', 'NWC'),
                                 feature_group_count=c) + conv_b
    u, v = jnp.split(h, 2, axis=-1)
    return (jax.nn.silu(u) * v) @ w_down

def setup_inputs(seed: int = 0) -> dict:
    key = jax.random.key(seed)
    ks = jax.random.split(key, 20)

    def nrm(k, shape, scale):
        return jax.random.normal(k, shape, jnp.float32) * scale

    return {
        'x': nrm(ks[0], (BATCH, SEQ, D_MODEL), 1.0),
        'attn_norm': 1.0 + nrm(ks[1], (DEPTH, D_MODEL), 0.02),
        'w_in': nrm(ks[2], (DEPTH, D_MODEL, IN_COLS), D_MODEL ** -0.5),
        'mla_q_norm': 1.0 + nrm(ks[3], (DEPTH, MLA_Q_RANK), 0.02),
        'mla_kv_norm': 1.0 + nrm(ks[4], (DEPTH, MLA_KV_RANK), 0.02),
        'mla_w_uq': nrm(ks[5], (DEPTH, MLA_Q_RANK, MLA_HEADS * MLA_QK_DIM), MLA_Q_RANK ** -0.5),
        'mla_w_ukv': nrm(ks[6], (DEPTH, MLA_KV_RANK, MLA_HEADS * (MLA_NOPE_DIM + MLA_V_DIM)), MLA_KV_RANK ** -0.5),
        'nsa_gate_bias': nrm(ks[7], (DEPTH, NSA_HEADS * NSA_BRANCHES), 0.02),
        'nsa_cmp_pos': nrm(ks[8], (DEPTH, 2, CMP_LEN, NSA_HEAD_DIM), 0.1),
        'nsa_cmp_w1': nrm(ks[9], (DEPTH, 2, CMP_LEN * NSA_HEAD_DIM, CMP_HIDDEN), (CMP_LEN * NSA_HEAD_DIM) ** -0.5),
        'nsa_cmp_b1': nrm(ks[10], (DEPTH, 2, CMP_HIDDEN), 0.02),
        'nsa_cmp_w2': nrm(ks[11], (DEPTH, 2, CMP_HIDDEN, NSA_HEAD_DIM), CMP_HIDDEN ** -0.5),
        'w_out': nrm(ks[12], (DEPTH, D_MIX, D_MODEL), D_MIX ** -0.5),
        'ffn_norm': 1.0 + nrm(ks[13], (DEPTH, D_MODEL), 0.02),
        'ffn_w_up': nrm(ks[14], (DEPTH, D_MODEL, 2 * D_FF), D_MODEL ** -0.5),
        'ffn_conv_w': nrm(ks[15], (DEPTH, CONV_WIDTH, 2 * D_FF), CONV_WIDTH ** -0.5),
        'ffn_conv_b': nrm(ks[16], (DEPTH, 2 * D_FF), 0.02),
        'ffn_w_down': nrm(ks[17], (DEPTH, D_FF, D_MODEL), D_FF ** -0.5),
        'final_norm': 1.0 + nrm(ks[18], (D_MODEL,), 0.02),
    }

def reference(x, attn_norm, w_in, mla_q_norm, mla_kv_norm, mla_w_uq, mla_w_ukv, nsa_gate_bias,
              nsa_cmp_pos, nsa_cmp_w1, nsa_cmp_b1, nsa_cmp_w2, w_out, ffn_norm, ffn_w_up,
              ffn_conv_w, ffn_conv_b, ffn_w_down, final_norm):
    b, s, _ = x.shape
    cos_mla, sin_mla = rope_tables(s, MLA_ROPE_DIM)
    cos_nsa, sin_nsa = rope_tables(s, NSA_ROT_DIM)
    for l in range(DEPTH):
        h = rms_norm(x, attn_norm[l])
        proj = h @ w_in[l]
        q_lat, kv_lat, k_rope, nsa_q, nsa_kv, gate_logits = jnp.split(proj, SPLIT_POINTS, axis=-1)
        o_mla = mla_attention(q_lat, kv_lat, k_rope, mla_q_norm[l], mla_kv_norm[l],
                              mla_w_uq[l], mla_w_ukv[l], cos_mla, sin_mla)
        o_nsa = nsa_attention(nsa_q.reshape(b, s, NSA_HEADS, NSA_HEAD_DIM),
                              nsa_kv.reshape(b, s, NSA_BRANCHES, 2, NSA_KV_HEADS, NSA_HEAD_DIM),
                              gate_logits, nsa_gate_bias[l], nsa_cmp_pos[l], nsa_cmp_w1[l],
                              nsa_cmp_b1[l], nsa_cmp_w2[l], cos_nsa, sin_nsa)
        x = x + jnp.concatenate([o_mla, o_nsa], axis=-1) @ w_out[l]
        h = rms_norm(x, ffn_norm[l])
        x = x + conv_ffn(h, ffn_w_up[l], ffn_conv_w[l], ffn_conv_b[l], ffn_w_down[l])
    return rms_norm(x, final_norm)


_drawn_inputs = setup_inputs


def setup_inputs(seed=0):
    import zlib

    import numpy as np

    out = dict(_drawn_inputs(seed))
    spreads = {}
    factors = {'attn_norm': 6.397,
     'mla_q_norm': 8.0,
     'mla_kv_norm': 8.0,
     'nsa_gate_bias': 8.0,
     'nsa_cmp_b1': 8.0,
     'ffn_conv_b': 2.718,
     'final_norm': 8.37,
     'ffn_norm': 3.126}
    for name, (base, spread) in spreads.items():
        noise = np.random.default_rng([zlib.crc32(name.encode()), seed]).standard_normal(out[name].shape)
        drawn = base * np.exp(spread * noise) if base else spread * noise
        out[name] = __import__('jax').numpy.asarray(drawn.astype(out[name].dtype))
    for name, factor in factors.items():
        out[name] = (out[name] * factor).astype(out[name].dtype)
    return out
```

```python
from contextlib import ExitStack

import numpy as np

import concourse.bass as bass
from concourse import mybir

F32 = mybir.dt.float32
F32R = mybir.dt.float32r
ALU = mybir.AluOpType
ACT = mybir.ActivationFunctionType
AX = mybir.AxisListType.X

P = 128
D = 1024
S = 512
L = 2
T = S // P
KD = D // P
EPS = 1e-6
NEG = -1e30
THETA = 500000.0

H = 8
QR, KVR, ROPE, NOPE, VD = 256, 128, 32, 64, 64
QK = NOPE + ROPE
HD = 64
ROT = HD // 4
G = 2
BR = 3
GROUP = H // G
CLEN, CSTRIDE, CHID = 32, 16, 128
NC = (S - CLEN) // CSTRIDE + 1
NCP = NC + 1
DFF = 2816
FT = DFF // P
TAPS = 3

COL_Q = QR + KVR + ROPE
COL_KV = COL_Q + H * HD
COL_GATE = COL_KV + BR * 2 * G * HD
COLS = COL_GATE + H * BR
CH = 4
CW = COLS // CH
HALF = D // 2
MT = CLEN * HD // P
LAT = KD // 2
U_MLA = (H // 2) * T
U_NSA = H * T
U = U_MLA + U_NSA

C_TAP, C_CB = 0, TAPS * 2 * FT
C_POS = C_CB + 2 * FT
C_B1 = C_POS + 2 * MT
C_END = C_B1 + 2

SLOTS = 4
POS_WIN = 2
POS_UKV = POS_WIN + CH * KD // 2
POS_UQ = POS_UKV + 1
POS_CMP = POS_UQ + 2
POS_WOUT = -(-(POS_CMP + 4) // SLOTS) * SLOTS
POS_UP = POS_WOUT + KD
POS_DOWN = POS_UP + 2 * FT
POS_END = POS_DOWN + FT
PERIOD = -(-POS_END // SLOTS) * SLOTS
DOWN_TURNS = FT // SLOTS - 2
assert POS_WOUT % SLOTS == 0 and POS_UP % SLOTS == 0 and POS_DOWN % SLOTS == 0
RAW_POS = [p for p in range(POS_WIN, POS_END) if not POS_CMP + 4 <= p < POS_WOUT]
SPLIT_POS = [p for p in RAW_POS if not POS_CMP <= p < POS_CMP + 4]
MLA_POS = [POS_UKV, POS_UQ, POS_UQ + 1]
USED_POS = [p for p in SPLIT_POS if p not in MLA_POS]
CMP_POS = list(range(POS_CMP, POS_CMP + 4))
LOADS_PER_SLOT = [sum(p % SLOTS == s for p in RAW_POS) for s in range(SLOTS)]

ITEMS = 2 + 2 + H // 2

PER_LAYER = {
    "x_done": 2 * T, "sd_done": 2 * T, "hn_done": 2 * T, "tp_done": 4 * T, "hh_done": 4 * T,
    "hl_done": 4 * T,
    "hi_done": len(SPLIT_POS), "lo_done": len(SPLIT_POS), "split_used": len(USED_POS), "cmp_used": 4,
    "win_acc": CH * (T - 1), "pj_act": CH * T // 2, "pj_dve": CH * T // 2,
    "lat_sq": 1, "lat_ready": 1, "kpe_ready": 1, "lat_tp": 4, "cols_tp": 1, "lat_hi": 4,
    "lat_lo": 3, "kpe_lo": 1, "cols_ready": 1,
    "kpe_copied": 1, "q_roped": 1, "k_roped": 1, "gate_in": 1, "gate_exp": 1, "gates_ready": 1,
    "v_acc": T, "v_ready": T, "qk_acc": 2 * H, "qf_done": H, "kh_done": H, "q_ready": H, "kl_done": H,
    "sc_done": U, "max_done": U, "exp_done": U, "p_done": U, "t_done": U, "pt_done": U, "pv_done": U,
    "oh_done": H, "ol_done": H,
    "it_tp": ITEMS, "it_act": ITEMS, "it_dve": ITEMS,
    "hb_done": 2, "hid_ready": 2, "kvc_acc": 1, "kch_done": 1, "kvc_ready": 1, "cs_acc": 1,
    "cs_sub": 1, "cs_exp": 1, "pc_done": 1, "pc_tp": 1, "pct_ready": 1,
    "t0_done": 2 * FT, "conv_done": FT, "silu_done": FT, "g_done": FT,
    "gh_done": FT, "gl_done": FT, "out_acc": 2 * (T - 1),
}
CREDIT = {"x_done": T, "hn_done": 1, "lo_done": SLOTS, "split_used": SLOTS}


def at(s, l, n):
    return l * PER_LAYER[s.name] + (n + CREDIT.get(s.name, 0))


def nth(positions, pos):
    return sum(p <= pos for p in positions)


def before_in_slot(pos):
    same = [p for p in RAW_POS if p % SLOTS == pos % SLOTS]
    earlier = [p for p in same if p < pos]
    return (0, earlier[-1]) if earlier else (-1, same[-1])


def split_before_in_slot(pos):
    same = [p for p in SPLIT_POS if p % SLOTS == pos % SLOTS]
    earlier = [p for p in same if p < pos]
    return (0, earlier[-1]) if earlier else (-1, same[-1])


def rope_tables(dim):
    inv = (np.float32(THETA) ** (-np.arange(0, dim, 2, dtype=np.float32) / np.float32(dim))).astype(np.float32)
    ang = np.arange(S, dtype=np.float32)[:, None] * inv[None, :]
    return np.cos(ang).astype(np.float32), np.sin(ang).astype(np.float32)


def shape_constants():
    c, s = rope_tables(ROT)
    nsa = np.concatenate([c, c, -s, s], 1)
    c, s = rope_tables(ROPE)
    mla = np.concatenate([c, c, -s, s], 1)
    rope = np.concatenate([nsa, mla], 1).reshape(T, P, 2 * (ROT + ROPE)).transpose(1, 0, 2)
    table = np.concatenate([np.ones((NOPE, S)), np.concatenate([c, c], 1).T, np.concatenate([-s, s], 1).T], 0)
    table = table * QK ** -0.5
    q = np.arange(P)
    causal = np.where(q[None, :] <= q[:, None], 0.0, NEG)
    end = np.arange(NCP) * CSTRIDE + CLEN - 1
    pos = np.arange(T)[None, :, None] * P + q[:, None, None]
    cmask = np.where((end[None, None, :] <= pos) & (np.arange(NCP) < NC), 0.0, NEG)
    rowok = (pos[:, :, 0] >= CLEN - 1) * 1.0
    f = lambda a: np.ascontiguousarray(a, dtype=np.float32)
    return {"c_rope": f(rope), "c_table": f(table), "c_causal": f(causal), "c_ident": f(np.eye(P)),
            "c_cmask": f(cmask), "c_rowok": f(rowok)}


class Steps:

    def __init__(self, per_layer):
        self.per_layer, self.base, self.n = per_layer, 0, 0

    def layer(self, l):
        self.base, self.n = l * self.per_layer, 0

    def end_layer(self, name):
        assert self.n == self.per_layer, (name, self.n)

    def next(self):
        self.n += 1
        return self.base + self.n

    def loop(self, j, per_turn):
        self.outer = (self.base, self.n)
        self.base, self.n = self.base + self.n + j * per_turn, 0

    def end_loop(self, turns, per_turn):
        assert self.n == per_turn, ("turn", self.n)
        self.base, self.n = self.outer[0], self.outer[1] + turns * per_turn


def hybrid_layers(nc, a, out):
    with ExitStack() as ctx:
        def sb(name, shape, dt=F32, scope=ctx):
            return scope.enter_context(nc.sbuf_tensor(name, shape, dt))

        x = sb("x", [P, T, D])
        ht_hi = sb("ht_hi", [P, KD, S], F32R)
        ht_lo = sb("ht_lo", [P, KD, S], F32R)
        raw = sb("raw", [P, SLOTS, 1024])
        w_hi = sb("w_hi", [P, SLOTS, 1024], F32R)
        w_lo = sb("w_lo", [P, SLOTS, 1024], F32R)
        norm_g = sb("norm_g", [P, D])
        probs = sb("probs", [P, 2, 2, S])
        probs_t = sb("probs_t", [P, 2, S])
        ident = sb("ident", [P, P])
        ident_r = sb("ident_r", [P, P], F32R)
        causal = sb("causal", [P, P])
        causal_r = sb("causal_r", [P, P], F32R)
        table = sb("table", [P, S])
        rope = sb("rope", [P, T, 2 * (ROT + ROPE)])
        cmask = sb("cmask", [P, T, NCP])
        rowok = sb("rowok", [P, T])
        cols = sb("cols", [P, C_END])
        lat_g = sb("lat_g", [P, QR + KVR])
        gate_b = sb("gate_b", [P, H * BR])
        cmp_w2 = sb("cmp_w2", [P, 3, HD])
        eps = sb("eps", [P, 1])
        ms = sb("ms", [P, T])
        sd = sb("sd", [P, T])
        rstd = sb("rstd", [P, T])
        lat_ms = sb("lat_ms", [P, 2 * T])
        lat_sd = sb("lat_sd", [P, 2 * T])
        lat_rstd = sb("lat_rstd", [P, 2 * T])
        nmax = sb("nmax", [P, 4, 2])
        rsum = sb("rsum", [P, 4, 2])
        rinv = sb("rinv", [P, 4, 2])
        rgate = sb("rgate", [P, 4, 2])
        qf = sb("qf", [P, S])
        gate_e = sb("gate_e", [P, T, H * BR])
        gates = sb("gates", [P, T, H * BR])
        hid = sb("hid", [P, 2, G, NCP])
        hid_b = sb("hid_b", [P, 2])
        kc_hi = sb("kc_hi", [P, G, NCP], F32R)
        kc_lo = sb("kc_lo", [P, G, NCP], F32R)
        v_cmp = sb("v_cmp", [P, G, HD])
        cstat = sb("cstat", [P, 3, T, H])
        tmp_pool = sb("tmp_pool", [P, 2, H, ROT])
        kpe_t = sb("kpe_t", [P, 2, T, ROPE])
        kpe_r = sb("kpe_r", [P, T, 2, ROPE])

        attn = ExitStack()
        proj = sb("proj", [P, T, COLS], F32, attn)
        qs = sb("qs", [P, 8, S], F32R, attn)
        ks = sb("ks", [P, 8, S], F32R, attn)
        vm = sb("vm", [P, T, H * VD], F32, attn)
        attn.close()
        ffn = ExitStack()
        g_all = sb("g_all", [P, FT, S], F32, ffn)
        g_hi = sb("g_hi", [P, 2, S], F32R, ffn)
        g_lo = sb("g_lo", [P, 2, S], F32R, ffn)
        conv = sb("conv", [P, 2, 2, S], F32, ffn)
        silu = sb("silu", [P, 2, S], F32, ffn)
        ffn.close()

        rows = probs_t[:, :, :].rearrange("p a (b c) -> p (a b) c", c=P)
        hn = probs[:, :, :, :].rearrange("p s a n -> p s (a n)")
        kcv = vm[:, :, :]
        pct = vm[:, 0:2, :]
        scp = probs[:, 1, :, :].rearrange("p a (t h c) -> p (a t) h c", t=T // 2, h=H)

        ps = ctx.enter_context(nc.psum_tensor("ps", [P, 8, S], F32))

        def sem(name):
            return ctx.enter_context(nc.semaphore(name))

        x_done = sem("x_done")
        sd_done = sem("sd_done")
        hn_done = sem("hn_done")
        tp_done = sem("tp_done")
        hh_done = sem("hh_done")
        hl_done = sem("hl_done")
        hi_done = sem("hi_done")
        lo_done = sem("lo_done")
        split_used = sem("split_used")
        cmp_used = sem("cmp_used")
        win_acc = sem("win_acc")
        pj_act = sem("pj_act")
        pj_dve = sem("pj_dve")
        lat_sq = sem("lat_sq")
        lat_ready = sem("lat_ready")
        kpe_ready = sem("kpe_ready")
        lat_tp = sem("lat_tp")
        cols_tp = sem("cols_tp")
        lat_hi = sem("lat_hi")
        lat_lo = sem("lat_lo")
        kpe_lo = sem("kpe_lo")
        cols_ready = sem("cols_ready")
        kpe_copied = sem("kpe_copied")
        q_roped = sem("q_roped")
        k_roped = sem("k_roped")
        gate_in = sem("gate_in")
        gate_exp = sem("gate_exp")
        gates_ready = sem("gates_ready")
        v_acc = sem("v_acc")
        v_ready = sem("v_ready")
        qk_acc = sem("qk_acc")
        qf_done = sem("qf_done")
        kh_done = sem("kh_done")
        q_ready = sem("q_ready")
        kl_done = sem("kl_done")
        sc_done = sem("sc_done")
        max_done = sem("max_done")
        exp_done = sem("exp_done")
        p_done = sem("p_done")
        t_done = sem("t_done")
        pt_done = sem("pt_done")
        pv_done = sem("pv_done")
        oh_done = sem("oh_done")
        ol_done = sem("ol_done")
        it_tp = sem("it_tp")
        it_act = sem("it_act")
        it_dve = sem("it_dve")
        hb_done = sem("hb_done")
        hid_ready = sem("hid_ready")
        kvc_acc = sem("kvc_acc")
        kch_done = sem("kch_done")
        kvc_ready = sem("kvc_ready")
        cs_acc = sem("cs_acc")
        cs_sub = sem("cs_sub")
        cs_exp = sem("cs_exp")
        pc_done = sem("pc_done")
        pc_tp = sem("pc_tp")
        pct_ready = sem("pct_ready")
        t0_done = sem("t0_done")
        conv_done = sem("conv_done")
        silu_done = sem("silu_done")
        g_done = sem("g_done")
        gh_done = sem("gh_done")
        gl_done = sem("gl_done")
        out_acc = sem("out_acc")
        pj = [pj_act, pj_dve]
        raw_loaded = [sem(f"raw_loaded{s}") for s in range(SLOTS)]
        x_loaded = sem("x_loaded")
        const_loaded = sem("const_loaded")
        g_loaded = sem("g_loaded")
        small_loaded = sem("small_loaded")
        const_ready = sem("const_ready")
        settled = sem("settled")
        out_done = [sem(f"out_done{i}") for i in range(2)]
        act_chain = ctx.enter_context(nc.semaphore("act_chain"))
        dve_chain = ctx.enter_context(nc.semaphore("dve_chain"))
        pool_chain = ctx.enter_context(nc.semaphore("pool_chain"))

        def settle(eng):
            eng.sem_inc(settled, 1)

        block = ctx.enter_context(nc.Block())
        consts = [(ident, "c_ident"), (causal, "c_causal"), (table, "c_table"), (rope, "c_rope"),
                  (cmask, "c_cmask"), (rowok, "c_rowok")]
        SMALL = 9

        def wslot(buf, pos, shape):
            n = int(np.prod(shape))
            v = buf[:, pos % SLOTS, 0:n]
            return v.rearrange("p (a b) -> p a b", b=shape[-1]) if len(shape) == 2 else v

        @block.sync
        def _(sp):
            for t in range(T):
                sp.dma_start(x[:, t, :], a["x"][0, t * P:(t + 1) * P, :]).then_inc(x_loaded, 16)

            def load(l, pos, src, shape, turn=0):
                back, prev = before_in_slot(pos)
                if prev in CMP_POS:
                    sp.wait_ge(cmp_used, at(cmp_used, l, nth(CMP_POS, prev)))
                else:
                    sp.wait_ge(lo_done, at(lo_done, l, back * len(SPLIT_POS) + nth(SPLIT_POS, prev) + turn))
                sp.dma_start(wslot(raw, pos, shape), src).then_inc(raw_loaded[pos % SLOTS], 16)

            with sp.Fori(0, L) as l:
                w_in = a["w_in"][bass.ds(l, 1), :, :].rearrange("o (k p) n -> p (o k) n", p=P)
                for c in range(CH):
                    for kp in range(KD // 2):
                        load(l, POS_WIN + c * KD // 2 + kp, w_in[:, 2 * kp:2 * kp + 2, c * CW:(c + 1) * CW], [2, CW])
                load(l, POS_UKV, a["mla_w_ukv"][bass.ds(l, 1), :, :].rearrange("o p n -> (o p) n"), [H * 2 * NOPE])
                uq = a["mla_w_uq"][bass.ds(l, 1), :, :].rearrange("o (k p) n -> p (o k) n", p=P)
                for k in range(2):
                    load(l, POS_UQ + k, uq[:, k, :], [H * QK])
                w1 = a["nsa_cmp_w1"][bass.ds(l, 1), :, :, :].rearrange("o a (m p) n -> p (o a m) n", p=P)
                for n in range(4):
                    load(l, POS_CMP + n, w1[:, n * MT // 2:(n + 1) * MT // 2, :], [MT // 2, CHID])
                w_out = a["w_out"][bass.ds(l, 1), :, :].rearrange("o (k p) n -> p (o k) n", p=P)
                for k in range(KD):
                    load(l, POS_WOUT + k, w_out[:, k, :], [D])
                up = a["ffn_w_up"][bass.ds(l, 1), :, :].rearrange("o (k p) n -> p (o k) n", p=P)

                def load_up(f, pos, turn):
                    for uv in range(2):
                        load(l, pos + uv, up[:, :, bass.ds(f * P + uv * DFF, P)], [KD, P], turn)

                load_up(0, POS_UP, 0)
                load_up(1, POS_UP + 2, 0)
                with sp.Fori(1, FT // 2) as j:
                    for e in range(2):
                        load_up(2 * j + e, POS_UP + SLOTS + 2 * e, (j - 1) * SLOTS)
                down = a["ffn_w_down"][bass.ds(l, 1), :, :].rearrange("o (k p) n -> (o k) p n", p=P)
                with sp.Fori(0, FT // SLOTS) as j:
                    for e in range(SLOTS):
                        load(l, POS_DOWN + e, down[bass.ds(SLOTS * j + e, 1), :, :].rearrange("k p n -> (k p) n"),
                             [D], j * SLOTS)
                for k in range(FT // SLOTS * SLOTS, FT):
                    load(l, POS_DOWN + k, down[k, :, :], [D])

            for t in range(T):
                sp.wait_ge(hn_done, at(hn_done, L, t + 1))
                sp.dma_start(out[0, t * P:(t + 1) * P, :], hn[:, t % 2, :]).then_inc(out_done[t % 2], 16)
            for slot in out_done:
                sp.wait_ge(slot, 16 * T // 2)

        def slot_loads(pos):
            return sum(p % SLOTS == pos % SLOTS and p <= pos for p in RAW_POS)

        def landed(l, pos, turns=0):
            return (l * LOADS_PER_SLOT[pos % SLOTS] + slot_loads(pos) + turns) * 16

        def split(l, pos, turn=0):
            return at(lo_done, l, nth(SPLIT_POS, pos) + turn)

        def used(l, pos, turn=0):
            return at(split_used, l, nth(USED_POS, pos) + turn)

        def pieces_map(pos):
            if POS_UQ <= pos < POS_UQ + 2:
                d = lambda b: b[:, pos % SLOTS, :].rearrange("p (h c) -> p h c", h=H)
                r = lambda b: b[:, pos % SLOTS, 0:H * QK].rearrange("p (h c) -> p h c", h=H)
                half = ROPE // 2
                return [(d, r, (0, QK), (0, QK)), (d, r, (QK, QK + half), (NOPE + half, QK)),
                        (d, r, (QK + half, P), (NOPE, NOPE + half))]
            n = 2 * CW if pos < POS_UKV else 1024
            whole = lambda b: b[:, pos % SLOTS, 0:n].unsqueeze(1)
            return [(whole, whole, (0, n), (0, n))]

        def split_hi(act, l, pos, turn=0, turns=0):
            act.wait_ge(raw_loaded[(pos) % SLOTS], landed(l, pos, turns))
            back, prev = split_before_in_slot(pos)
            if prev in MLA_POS:
                act.wait_ge(qk_acc, at(qk_acc, l, 2 * H))
            else:
                act.wait_ge(split_used, at(split_used, l, back * len(USED_POS) + nth(USED_POS, prev) + turn))
            for d, r, (d0, d1), (r0, r1) in pieces_map(pos):
                last = nc.scalar.activation(d(w_hi)[:, :, d0:d1], r(raw)[:, :, r0:r1], ACT.Copy)
            last.then_inc(hi_done, 1)

        def split_lo(dve, l, pos, turn=0):
            dve.wait_ge(hi_done, at(hi_done, l, nth(SPLIT_POS, pos) + turn))
            for d, r, (d0, d1), (r0, r1) in pieces_map(pos):
                last = nc.vector.tensor_tensor(d(w_lo)[:, :, d0:d1], r(raw)[:, :, r0:r1],
                                               d(w_hi)[:, :, d0:d1].bitcast(F32), ALU.subtract)
            last.then_inc(lo_done, 1)

        def item_kind(n):
            return ("k", n) if n < 2 else ("c", n - 2) if n < 4 else ("q", n - 4)

        def halves(h):
            top, bottom = slice(0, HD), slice(HD, P)
            return (top, bottom) if h % 2 == 0 else (bottom, top)

        def unit(u):
            if u < U_MLA:
                return u % T, u // T
            return u % T, H // 2 + (u - U_MLA) // T // 2

        @block.gpsimd
        def _(pool):
            ch = Steps(2 * (T + T * BR) + H)
            tt = nc.gpsimd.tensor_tensor

            def rotate(t, v, heads):
                c = rope[:, t, 0:ROT].unsqueeze(1).broadcast_to([P, heads, ROT])
                s = rope[:, t, ROT:2 * ROT].rearrange("p (a b) -> p a b", a=2).unsqueeze(1)\
                    .broadcast_to([P, heads, 2, ROT // 2])
                m0, m1 = tmp_pool[:, 0, 0:heads, :], tmp_pool[:, 1, 0:heads, :]
                tt(m0, v, c, ALU.mult)
                swapped = v.rearrange("p h (a b) -> p h a b", a=2)[:, :, ::-1, :]
                tt(m1.rearrange("p h (a b) -> p h a b", a=2), swapped, s, ALU.mult).then_inc(pool_chain, 1)
                pool.wait_ge(pool_chain, ch.next())
                return tt(v, m0, m1, ALU.add)

            with pool.Fori(0, L) as l:
                ch.layer(l)
                pool.wait_ge(hn_done, at(hn_done, l, 0))
                settle(pool)
                pool.dma_start(norm_g[:, :], a["attn_norm"][bass.ds(l, 1), :].broadcast_to([P, D])).then_inc(g_loaded, 16)
                pool.wait_ge(x_done, at(x_done, l, 1 - T))
                settle(pool)
                bd = lambda v, n: v.broadcast_to([P, n])
                pool.dma_start(lat_g[:, 0:QR], bd(a["mla_q_norm"][bass.ds(l, 1), :], QR)).then_inc(small_loaded, 16)
                pool.dma_start(lat_g[:, QR:QR + KVR], bd(a["mla_kv_norm"][bass.ds(l, 1), :], KVR))\
                    .then_inc(small_loaded, 16)
                pool.dma_start(gate_b[:, :], bd(a["nsa_gate_bias"][bass.ds(l, 1), :], H * BR)).then_inc(small_loaded, 16)
                w2 = a["nsa_cmp_w2"][bass.ds(l, 1), :, :, :].rearrange("o a p n -> p (o a) n")
                pool.dma_start(cmp_w2[:, 0, :], w2[:, 0, :]).then_inc(small_loaded, 16)
                pool.dma_start(cmp_w2[:, 1:3, :], w2).then_inc(small_loaded, 16)
                pool.dma_start(rows[0:2 * FT, 0:TAPS, :], a["ffn_conv_w"][bass.ds(l, 1), :, :]
                               .rearrange("o a (f p) -> f (o a) p", p=P)).then_inc(small_loaded, 16)
                pool.dma_start(rows[0:2 * FT, TAPS, :], a["ffn_conv_b"][bass.ds(l, 1), :]
                               .rearrange("o (f p) -> (o f) p", p=P)).then_inc(small_loaded, 16)
                pool.dma_start(rows[0:2 * MT, TAPS + 1, :].rearrange("m (j d) -> m j d", d=HD),
                               a["nsa_cmp_pos"][bass.ds(l, 1), :, :, :]
                               .rearrange("o a (m j) d -> (o a m) j d", j=2)).then_inc(small_loaded, 16)
                pool.dma_start(rows[0:2, TAPS + 2, :], a["nsa_cmp_b1"][bass.ds(l, 1), :, :]
                               .rearrange("o a n -> (o a) n")).then_inc(small_loaded, 16)
                pool.wait_ge(hn_done, at(hn_done, l, T))
                settle(pool)
                pool.dma_start(norm_g[:, :], a["ffn_norm"][bass.ds(l, 1), :].broadcast_to([P, D])).then_inc(g_loaded, 16)
                pool.wait_ge(kpe_lo, at(kpe_lo, l, 1))
                settle(pool)
                src = ks[NOPE:P, 0:2, :]
                for n in range(1, 4):
                    last = nc.gpsimd.tensor_copy(ks[NOPE:P, 2 * n:2 * n + 2, :], src)
                last.then_inc(kpe_copied, 1)
                pool.wait_ge(kpe_copied, at(kpe_copied, l, 1))
                pool.wait_ge(pj_act, at(pj_act, l, CH * T // 2))
                pool.wait_ge(pj_dve, at(pj_dve, l, CH * T // 2))
                for t in range(T):
                    last = rotate(t, proj[:, t, COL_Q:COL_KV].rearrange("p (h d) -> p h d", h=H)[:, :, 0:ROT], H)
                    last.then_inc(pool_chain, 1)
                    pool.wait_ge(pool_chain, ch.next())
                pool.sem_inc(q_roped, 1)
                tt(gate_e[:, :, :], proj[:, :, COL_GATE:COLS],
                   gate_b[:, :].unsqueeze(1).broadcast_to([P, T, H * BR]), ALU.add).then_inc(gate_in, 1)

                def split_q(n):
                    pool.wait_ge(qf_done, at(qf_done, l, n + 1))
                    settle(pool)
                    i = 2 * (n % 4)
                    nc.gpsimd.tensor_copy(qs[:, i, :], qf[:, :]).then_inc(pool_chain, 1)
                    pool.wait_ge(pool_chain, ch.next())
                    tt(qs[:, i + 1, :], qf[:, :], qs[:, i, :].bitcast(F32), ALU.subtract).then_inc(q_ready, 1)

                split_q(0)
                split_q(1)
                n = 0
                for t in range(T):
                    for b in range(BR):
                        c0 = COL_KV + b * 2 * G * HD
                        last = rotate(t, proj[:, t, c0:c0 + G * HD].rearrange("p (h d) -> p h d", h=G)[:, :, 0:ROT], G)
                        last.then_inc(pool_chain, 1)
                        pool.wait_ge(pool_chain, ch.next())
                    if t < 3:
                        split_q(2 + 2 * t)
                        split_q(3 + 2 * t)
                pool.sem_inc(k_roped, 1)
                ch.end_layer("pool")
            pool.wait_ge(hn_done, at(hn_done, L, 0))
            pool.dma_start(norm_g[:, :], a["final_norm"].rearrange("(o d) -> o d", o=1).broadcast_to([P, D]))\
                .then_inc(g_loaded, 16)

        @block.scalar
        def _(act):
            for tile, name in consts:
                act.dma_start(tile[tuple(slice(None) for _ in tile.shape)], a[name]).then_inc(const_loaded, 16)
            ch = Steps(2 * T + 1)
            activate = nc.scalar.activation

            def norm_stats(l, w, t):
                act.wait_ge(x_done, at(x_done, l, w * T + t + 1 - T))
                activate(ps[:, 2 * t:2 * t + 2, :], x[:, t, :].rearrange("p (a n) -> p a n", a=2), ACT.Square,
                                 scale=D ** -0.5, accum_out=ms[:, t:t + 1]).then_inc(act_chain, 1)
                act.wait_ge(act_chain, ch.next())
                activate(sd[:, t:t + 1], ms[:, t:t + 1], ACT.Sqrt, bias=eps[:, :]).then_inc(sd_done, 1)

            def norm_hi(l, w, t):
                for b in range(2):
                    act.wait_ge(tp_done, at(tp_done, l, 2 * (w * T + t) + b + 1))
                    activate(ht_hi[:, 4 * b:4 * b + 4, t * P:(t + 1) * P],
                             ps[:, 2 * t + b, :].rearrange("p (k n) -> p k n", k=4), ACT.Copy)\
                        .then_inc(hh_done, 1)

            act.wait_ge(const_ready, 4)

            with act.Fori(0, L) as l:
                ch.layer(l)
                norm_stats(l, 0, 0)
                split_hi(act, l, POS_WIN)
                norm_stats(l, 0, 1)
                norm_hi(l, 0, 0)
                split_hi(act, l, POS_WIN + 1)
                split_hi(act, l, POS_WIN + 2)
                norm_stats(l, 0, 2)
                norm_hi(l, 0, 1)
                split_hi(act, l, POS_WIN + 3)
                norm_stats(l, 0, 3)
                norm_hi(l, 0, 2)
                norm_hi(l, 0, 3)

                def evac_chunk(c):
                    for t in range(0, T, 2):
                        act.wait_ge(win_acc, at(win_acc, l, c * (T - 1) + t + 1))
                        activate(proj[:, t, c * CW:(c + 1) * CW], ps[:, 4 * (c % 2) + t, 0:CW], ACT.Copy)\
                            .then_inc(pj_act, 1)

                def win_splits(c):
                    for kp in range(KD // 2):
                        split_hi(act, l, POS_WIN + c * KD // 2 + kp)

                win_splits(1)
                evac_chunk(0)
                act.wait_ge(pj_act, at(pj_act, l, T // 2))
                act.wait_ge(pj_dve, at(pj_dve, l, T // 2))
                for t in range(T):
                    activate(ps[:, t, 0:QR], proj[:, t, 0:QR], ACT.Square, scale=QR ** -0.5,
                             accum_out=lat_ms[:, 2 * t:2 * t + 1])
                    last = activate(ps[:, t, QR:QR + KVR], proj[:, t, QR:QR + KVR], ACT.Square, scale=KVR ** -0.5,
                                    accum_out=lat_ms[:, 2 * t + 1:2 * t + 2])
                last.then_inc(act_chain, 1)
                act.wait_ge(act_chain, ch.next())
                activate(lat_sd[:, :], lat_ms[:, :], ACT.Sqrt, bias=eps[:, :]).then_inc(lat_sq, 1)
                win_splits(2)
                evac_chunk(1)
                win_splits(3)
                split_hi(act, l, POS_UKV)
                evac_chunk(2)
                split_hi(act, l, POS_UQ)
                split_hi(act, l, POS_UQ + 1)
                evac_chunk(3)
                for n in range(3):
                    act.wait_ge(lat_tp, at(lat_tp, l, n + 1))
                    activate(ht_hi[:, LAT + n, :], ps[:, n, :], ACT.Copy).then_inc(lat_hi, 1)
                act.wait_ge(lat_tp, at(lat_tp, l, 4))
                activate(ks[NOPE:P, 0, :], ps[0:2 * ROPE, 3, :], ACT.Copy).then_inc(lat_hi, 1)
                for t in range(T):
                    act.wait_ge(v_acc, at(v_acc, l, t + 1))
                    activate(vm[:, t, :], ps[:, 4 + t, :], ACT.Copy).then_inc(v_ready, 1)

                def k_hi(n, bank):
                    act.wait_ge(qk_acc, at(qk_acc, l, 2 * n + 2))
                    i = 2 * (n % 4)
                    activate(ks[0:NOPE, i, :], ps[0:NOPE, bank, :], ACT.Copy).then_inc(kh_done, 1)

                k_hi(0, 1)
                k_hi(1, 3)
                act.wait_ge(gate_in, at(gate_in, l, 1))
                activate(gates[:, :, :], gate_e[:, :, :], ACT.Exp, scale=-1.0).then_inc(gate_exp, 1)

                def exps(u):
                    i, _ = unit(u)
                    n = (i + 1) * P
                    act.wait_ge(max_done, at(max_done, l, u + 1))
                    if u >= 2:
                        act.wait_ge(t_done, at(t_done, l, u - 1))
                    if u == U_MLA + 1:
                        act.wait_ge(pc_tp, at(pc_tp, l, 1))
                    for s in range(2):
                        last = activate(probs[:, u % 2, s, 0:n], ps[:, 2 * (u % 2) + s, 0:n], ACT.Exp,
                                        bias=nmax[:, u % 4, s:s + 1], accum_out=rsum[:, u % 4, s:s + 1])
                    last.then_inc(exp_done, 1)

                def evac_pt(u):
                    i, _ = unit(u)
                    n = (i + 1) * P
                    act.wait_ge(t_done, at(t_done, l, u + 1))
                    if u >= 1:
                        act.wait_ge(pv_done, at(pv_done, l, u))
                    activate(probs_t[:, :, 0:n], ps[:, 4:6, 0:n], ACT.Copy).then_inc(pt_done, 1)

                def evac_out(pair, bank):
                    done = T * (pair + 1) if pair < H // 2 else U_MLA + 2 * T * (pair - H // 2 + 1)
                    act.wait_ge(pv_done, at(pv_done, l, done))
                    activate(ht_hi[:, pair, :], ps[:, bank, :], ACT.Copy).then_inc(oh_done, 1)

                for s in range(U_MLA + 3):
                    if 0 <= s - 2 < U_MLA:
                        evac_pt(s - 2)
                    if s < U_MLA:
                        exps(s)
                        if s % T in (1, 3) and s + T < U_MLA:
                            k_hi(2 * (s // T) + 2 + (s % T) // 2, 7)
                    if s - 3 >= 0 and (s - 3) % T == T - 1:
                        evac_out((s - 3) // T, 6)

                for n in range(ITEMS):
                    kind, i = item_kind(n)
                    act.wait_ge(it_tp, at(it_tp, l, n + 1))
                    for e in range(2):
                        own = halves(e)[0]
                        if kind == "k":
                            for half in halves(0):
                                ins = activate(ks[half, 2 * (2 * e + i), :], ps[own, n % 4, :], ACT.Copy)
                        elif kind == "c":
                            ins = activate(kcv[0:HD, 2 * i + e, :], ps[own, n % 4, :], ACT.Copy)
                        else:
                            ins = activate(qs[own, 2 * i + e, :], ps[own, n % 4, :], ACT.Copy, scale=HD ** -0.5)
                    ins.then_inc(it_act, 1)
                for kv in range(2):
                    act.wait_ge(hb_done, at(hb_done, l, kv + 1))
                    activate(hid[:, kv, :, 0:NC], ps[:, (4, 7)[kv], 0:G * NC].rearrange("p (g c) -> p g c", g=G),
                             ACT.Gelu_apprx_tanh, bias=hid_b[:, kv:kv + 1]).then_inc(hid_ready, 1)
                act.wait_ge(kvc_acc, at(kvc_acc, l, 1))
                activate(kc_hi[:, :, :], ps[:, 4, 0:G * NCP].rearrange("p (g c) -> p g c", g=G), ACT.Copy)\
                    .then_inc(kch_done, 1)
                act.wait_ge(cs_sub, at(cs_sub, l, 1))
                activate(scp, scp, ACT.Exp).then_inc(cs_exp, 1)
                exps(U_MLA)
                act.wait_ge(pc_tp, at(pc_tp, l, 1))
                activate(pct, ps[:, 4:6, :], ACT.Copy).then_inc(pct_ready, 1)
                for s in range(U_MLA + 1, U + 3):
                    if U_MLA <= s - 2 < U:
                        evac_pt(s - 2)
                    if s < U:
                        exps(s)
                    if s - 3 >= U_MLA and (s - 3 - U_MLA) % (2 * T) == 2 * T - 1:
                        pair = (s - 3 - U_MLA) // (2 * T)
                        evac_out(H // 2 + pair, 6 + pair % 2)
                    if s == U_MLA + 2 * T:
                        for k in range(SLOTS):
                            split_hi(act, l, POS_WOUT + k)
                for k in range(SLOTS, KD):
                    split_hi(act, l, POS_WOUT + k)
                norm_stats(l, 1, 0)
                norm_stats(l, 1, 1)
                norm_hi(l, 1, 0)
                norm_stats(l, 1, 2)
                norm_hi(l, 1, 1)
                split_hi(act, l, POS_UP)
                norm_stats(l, 1, 3)
                norm_hi(l, 1, 2)
                split_hi(act, l, POS_UP + 1)
                norm_hi(l, 1, 3)
                split_hi(act, l, POS_UP + 2)
                split_hi(act, l, POS_UP + 3)

                def up_tail(f, fl, pos_turn):
                    for uv in range(2):
                        act.wait_ge(split_used, used(l, POS_UP + 2 * fl + uv, pos_turn))
                        tap = cols[:, bass.ds(C_TAP + 2 * 2 * FT + f + uv * FT, 1)]
                        bias = cols[:, bass.ds(C_CB + f + uv * FT, 1)]
                        activate(conv[:, fl, uv, :], ps[:, 4 * fl + uv, :], ACT.Identity, bias=bias, scale=tap)\
                            .then_inc(t0_done, 1)
                    act.wait_ge(conv_done, at(conv_done, l, pos_turn // 2 + fl + 1))
                    activate(silu[:, fl, :], conv[:, fl, 0, :], ACT.Silu).then_inc(silu_done, 1)

                with act.Fori(0, FT // 2 - 1) as j:
                    for e in range(2):
                        up_tail(2 * j + e, e, 4 * j)
                        for uv in range(2):
                            p = 2 * e + uv
                            split_hi(act, l, POS_UP + SLOTS + p, SLOTS * j, j)

                def g_split_hi(k, n, turn=0):
                    act.wait_ge(g_done, at(g_done, l, min(n + 1, FT) + turn))
                    if n >= 2:
                        act.wait_ge(split_used, used(l, POS_DOWN + n - 2, turn))
                    activate(g_hi[:, n % 2, :].unsqueeze(1), g_all[:, bass.ds(k, 1), :], ACT.Copy)\
                        .then_inc(gh_done, 1)

                for e in range(2):
                    g_split_hi(e, e)
                for e in range(2):
                    up_tail(FT - 2 + e, e, 2 * (FT - 2))
                    for uv in range(2):
                        split_hi(act, l, POS_DOWN + 2 * e + uv)
                for n in range(SLOTS):
                    g_split_hi(n + 2, n + 2)
                    split_hi(act, l, POS_DOWN + SLOTS + n)
                with act.Fori(0, DOWN_TURNS) as j:
                    for e in range(SLOTS):
                        g_split_hi(SLOTS * j + SLOTS + e + 2, SLOTS + e + 2, SLOTS * j)
                        split_hi(act, l, POS_DOWN + 2 * SLOTS + e, SLOTS * j, j)
                for n in range(SLOTS * (DOWN_TURNS + 1), FT - 2):
                    g_split_hi(n + 2, n + 2)
                    if n + SLOTS < FT:
                        split_hi(act, l, POS_DOWN + n + SLOTS)
                ch.end_layer("act")

            for t in range(T):
                act.wait_ge(x_done, at(x_done, L, t + 1 - T))
                ins = activate(ps[:, 2 * t:2 * t + 2, :], x[:, t, :].rearrange("p (a n) -> p a n", a=2), ACT.Square,
                               scale=D ** -0.5, accum_out=ms[:, t:t + 1])
                ins.then_inc(act_chain, 1)
                act.wait_ge(act_chain, L * ch.per_layer + t + 1)
                activate(sd[:, t:t + 1], ms[:, t:t + 1], ACT.Sqrt, bias=eps[:, :]).then_inc(sd_done, 1)

        @block.vector
        def _(dve):
            ch = Steps(0)
            v = nc.vector
            tt, stt = v.tensor_tensor, v.scalar_tensor_tensor
            ch.per_layer = 2 * T + 3 + U_MLA + 2 * U_NSA + 6 + FT
            dve.wait_ge(const_loaded, 16 * len(consts))
            v.tensor_copy(ident_r[:, :], ident[:, :]).then_inc(const_ready, 1)
            v.tensor_copy(causal_r[:, :], causal[:, :]).then_inc(const_ready, 1)
            v.memset(hid[:, :, :, :], 0.0).then_inc(const_ready, 1)
            v.memset(eps[:, :], EPS).then_inc(const_ready, 1)
            dve.wait_ge(x_loaded, 16 * T)
            dve.sem_inc(x_done, CREDIT["x_done"])
            dve.sem_inc(lo_done, CREDIT["lo_done"])
            dve.sem_inc(hn_done, CREDIT["hn_done"])

            def norm_rows(l, w, t, final=False):
                dve.wait_ge(sd_done, at(sd_done, l, w * T + t + 1))
                v.reciprocal(rstd[:, t:t + 1], sd[:, t:t + 1]).then_inc(dve_chain, 1)
                dve.wait_ge(dve_chain, ch.next())
                if t == 0:
                    dve.wait_ge(g_loaded, (l * 2 + w + 1) * 16)
                if t >= 2:
                    if final:
                        dve.wait_ge(out_done[t % 2], 16 * (t // 2))
                    else:
                        dve.wait_ge(tp_done, at(tp_done, l, 2 * (w * T + t - 2) + 2))
                stt(out=hn[:, t % 2, :], in0=x[:, t, :], scalar=rstd[:, t:t + 1], in1=norm_g[:, :], op0=ALU.mult,
                    op1=ALU.mult).then_inc(hn_done, 1)

            def norm_lo(l, w, t):
                for b in range(2):
                    dve.wait_ge(hh_done, at(hh_done, l, 2 * (w * T + t) + b + 1))
                    r = (slice(None), slice(4 * b, 4 * b + 4), slice(t * P, (t + 1) * P))
                    tt(ht_lo[r], ps[:, 2 * t + b, :].rearrange("p (k n) -> p k n", k=4), ht_hi[r].bitcast(F32),
                       ALU.subtract).then_inc(hl_done, 1)

            def add_x(l, w, t):
                if t < T - 1:
                    dve.wait_ge(out_acc, at(out_acc, l, w * (T - 1) + t + 1))
                else:
                    dve.wait_ge(split_used, used(l, (POS_UP if w == 0 else POS_END) - 1))
                xt = x[:, t, :].rearrange("p (a n) -> p a n", a=2)
                tt(xt, xt, ps[:, 2 * t:2 * t + 2, :], ALU.add).then_inc(x_done, 1)

            with dve.Fori(0, L) as l:
                ch.layer(l)
                norm_rows(l, 0, 0)
                split_lo(dve, l, POS_WIN)
                norm_rows(l, 0, 1)
                norm_lo(l, 0, 0)
                split_lo(dve, l, POS_WIN + 1)
                split_lo(dve, l, POS_WIN + 2)
                norm_rows(l, 0, 2)
                norm_lo(l, 0, 1)
                split_lo(dve, l, POS_WIN + 3)
                norm_rows(l, 0, 3)
                norm_lo(l, 0, 2)
                norm_lo(l, 0, 3)

                def evac_chunk(c):
                    for t in range(1, T, 2):
                        if t < T - 1:
                            dve.wait_ge(win_acc, at(win_acc, l, c * (T - 1) + t + 1))
                        else:
                            dve.wait_ge(split_used, used(l, POS_WIN + (c + 1) * KD // 2 - 1))
                        v.tensor_copy(proj[:, t, c * CW:(c + 1) * CW], ps[:, 4 * (c % 2) + t, 0:CW])\
                            .then_inc(pj_dve, 1)

                def win_splits(c):
                    for kp in range(KD // 2):
                        split_lo(dve, l, POS_WIN + c * KD // 2 + kp)

                win_splits(1)
                evac_chunk(0)
                dve.wait_ge(pj_act, at(pj_act, l, T // 2))
                dve.wait_ge(pj_dve, at(pj_dve, l, T // 2))
                kp = proj[:, :, QR + KVR:COL_Q]
                rc = rope[:, :, 2 * ROT:2 * ROT + ROPE]
                rs = rope[:, :, 2 * ROT + ROPE:].rearrange("p t (a b) -> p t a b", a=2)
                dve.wait_ge(small_loaded, (l + 1) * 16 * SMALL)
                tt(kpe_t[:, 0, :, :], kp, rc, ALU.mult)
                tt(kpe_t[:, 1, :, :].rearrange("p t (a b) -> p t a b", a=2),
                           kp.rearrange("p t (a b) -> p t a b", a=2)[:, :, ::-1, :], rs, ALU.mult).then_inc(dve_chain, 1)
                dve.wait_ge(dve_chain, ch.next())
                twice = lambda n: kpe_t[:, n, :, :].unsqueeze(2).broadcast_to([P, T, 2, ROPE])
                tt(kpe_r[:, :, :, :], twice(0), twice(1), ALU.add).then_inc(kpe_ready, 1)
                dve.wait_ge(lat_sq, at(lat_sq, l, 1))
                v.reciprocal(lat_rstd[:, :], lat_sd[:, :]).then_inc(dve_chain, 1)
                dve.wait_ge(dve_chain, ch.next())
                for t in range(T):
                    stt(out=proj[:, t, 0:QR], in0=proj[:, t, 0:QR], scalar=lat_rstd[:, 2 * t:2 * t + 1],
                        in1=lat_g[:, 0:QR], op0=ALU.mult, op1=ALU.mult)
                    last = stt(out=proj[:, t, QR:QR + KVR], in0=proj[:, t, QR:QR + KVR],
                               scalar=lat_rstd[:, 2 * t + 1:2 * t + 2], in1=lat_g[:, QR:QR + KVR], op0=ALU.mult,
                               op1=ALU.mult)
                last.then_inc(lat_ready, 1)
                win_splits(2)
                evac_chunk(1)
                dve.wait_ge(cols_tp, at(cols_tp, l, 1))
                v.tensor_copy(cols[:, :], ps[:, 4, 0:C_END]).then_inc(cols_ready, 1)
                win_splits(3)
                split_lo(dve, l, POS_UKV)
                evac_chunk(2)
                split_lo(dve, l, POS_UQ)
                split_lo(dve, l, POS_UQ + 1)
                evac_chunk(3)
                for n in range(3):
                    dve.wait_ge(lat_hi, at(lat_hi, l, n + 1))
                    tt(ht_lo[:, LAT + n, :], ps[:, n, :], ht_hi[:, LAT + n, :].bitcast(F32), ALU.subtract)\
                        .then_inc(lat_lo, 1)
                dve.wait_ge(lat_hi, at(lat_hi, l, 4))
                tt(ks[NOPE:P, 1, :], ps[0:2 * ROPE, 3, :], ks[NOPE:P, 0, :].bitcast(F32), ALU.subtract)\
                    .then_inc(kpe_lo, 1)

                def q_rows(n, bank):
                    dve.wait_ge(qk_acc, at(qk_acc, l, 2 * n + 1))
                    if n >= 1:
                        dve.wait_ge(q_ready, at(q_ready, l, n))
                    tt(qf[:, :], ps[:, bank, :], table[:, :], ALU.mult).then_inc(qf_done, 1)

                def k_lo(n, bank):
                    dve.wait_ge(kh_done, at(kh_done, l, n + 1))
                    i = 2 * (n % 4)
                    tt(ks[0:NOPE, i + 1, :], ps[0:NOPE, bank, :], ks[0:NOPE, i, :].bitcast(F32), ALU.subtract)\
                        .then_inc(kl_done, 1)

                q_rows(0, 0)
                k_lo(0, 1)
                q_rows(1, 2)
                k_lo(1, 3)
                dve.wait_ge(gate_exp, at(gate_exp, l, 1))
                v.tensor_scalar(gates[:, :, :], gates[:, :, :], 1.0, None, ALU.add).then_inc(dve_chain, 1)
                dve.wait_ge(dve_chain, ch.next())
                v.reciprocal(gates[:, :, :], gates[:, :, :]).then_inc(gates_ready, 1)

                def row_max(u):
                    i, _ = unit(u)
                    n = (i + 1) * P
                    b = 2 * (u % 2)
                    dve.wait_ge(sc_done, at(sc_done, l, u + 1))
                    v.tensor_reduce(nmax[:, u % 4, :], ps[:, b:b + 2, 0:n], AX, ALU.max, negate=True)\
                        .then_inc(max_done, 1)

                def scale_probs(u):
                    i, _ = unit(u)
                    n = (i + 1) * P
                    dve.wait_ge(exp_done, at(exp_done, l, u + 1))
                    v.reciprocal(rinv[:, u % 4, :], rsum[:, u % 4, :]).then_inc(dve_chain, 1)
                    dve.wait_ge(dve_chain, ch.next())
                    r = rinv
                    if u >= U_MLA:
                        h = (u - U_MLA) // T
                        tt(rgate[:, u % 4, :], rinv[:, u % 4, :], gates[:, i, BR * h + 1:BR * h + 3],
                           ALU.mult).then_inc(dve_chain, 1)
                        dve.wait_ge(dve_chain, ch.next())
                        r = rgate
                    for s in range(2):
                        last = v.tensor_scalar(probs[:, u % 2, s, 0:n], probs[:, u % 2, s, 0:n],
                                               r[:, u % 4, s:s + 1], None, ALU.mult)
                    last.then_inc(p_done, 1)

                def out_lo(pair, bank):
                    dve.wait_ge(oh_done, at(oh_done, l, pair + 1))
                    tt(ht_lo[:, pair, :], ps[:, bank, :], ht_hi[:, pair, :].bitcast(F32), ALU.subtract)\
                        .then_inc(ol_done, 1)

                for s in range(U_MLA + 3):
                    if s < U_MLA:
                        row_max(s)
                    if 0 <= s - 1 < U_MLA:
                        scale_probs(s - 1)
                    if s < U_MLA and s + T < U_MLA:
                        n = 2 * (s // T) + 2 + (s % T) // 2
                        if s % 2 == 0:
                            q_rows(n, 7)
                        else:
                            k_lo(n, 7)
                    if s - 3 >= 0 and (s - 3) % T == T - 1:
                        out_lo((s - 3) // T, 6)

                for n in range(ITEMS):
                    kind, i = item_kind(n)
                    dve.wait_ge(it_act, at(it_act, l, n + 1))
                    for e in range(2):
                        own, other = halves(e)
                        if kind == "k":
                            c = 2 * (2 * e + i)
                            for half in halves(0):
                                ins = tt(ks[half, c + 1, :], ps[own, n % 4, :], ks[own, c, :].bitcast(F32), ALU.subtract)
                        elif kind == "c":
                            ins = v.tensor_copy(kcv[HD:P, 2 * i + e, 0:S - 1], ps[own, n % 4, 1:S])
                        else:
                            ins = stt(out=qs[other, 2 * i + e, :], in0=ps[own, n % 4, :], scalar=HD ** -0.5,
                                      in1=qs[own, 2 * i + e, :].bitcast(F32), op0=ALU.mult, op1=ALU.subtract)
                    ins.then_inc(it_dve, 1)
                for kv in range(2):
                    dve.wait_ge(cmp_used, at(cmp_used, l, 2 * kv + 2))
                    tt(hid_b[:, kv:kv + 1], ps[:, (5, 6)[kv], 0:1], cols[:, C_B1 + kv:C_B1 + kv + 1], ALU.add)\
                        .then_inc(hb_done, 1)
                dve.wait_ge(kch_done, at(kch_done, l, 1))
                tt(kc_lo[:, :, :], ps[:, 4, 0:G * NCP].rearrange("p (g c) -> p g c", g=G),
                   kc_hi[:, :, :].bitcast(F32), ALU.subtract)
                v.tensor_copy(v_cmp[:, :, :], ps[:, 5, 0:G * HD].rearrange("p (g c) -> p g c", g=G))\
                    .then_inc(kvc_ready, 1)
                dve.wait_ge(cs_acc, at(cs_acc, l, 1))
                for b in range(2):
                    t2 = slice(b * T // 2, (b + 1) * T // 2)
                    last = tt(scp[:, t2, :, :], ps[:, 6 + b, :].rearrange("p (t h c) -> p t h c", t=T // 2, h=H),
                              cmask[:, t2, :].unsqueeze(2).broadcast_to([P, T // 2, H, NCP]), ALU.add)
                last.then_inc(dve_chain, 1)
                dve.wait_ge(dve_chain, ch.next())
                sc3 = probs[:, 1, :, :].rearrange("p a n -> p (a n)").rearrange("p (q c) -> p q c", c=NCP)
                st = lambda n: cstat[:, n, :, :].rearrange("p t h -> p (t h)")
                wide = lambda n: st(n).unsqueeze(2).broadcast_to([P, T * H, NCP])
                v.tensor_reduce(st(0), sc3, AX, ALU.max).then_inc(dve_chain, 1)
                dve.wait_ge(dve_chain, ch.next())
                tt(sc3, sc3, wide(0), ALU.subtract).then_inc(cs_sub, 1)
                dve.wait_ge(cs_exp, at(cs_exp, l, 1))
                v.tensor_reduce(st(1), sc3, AX, ALU.add).then_inc(dve_chain, 1)
                dve.wait_ge(dve_chain, ch.next())
                v.reciprocal(st(2), st(1)).then_inc(dve_chain, 1)
                dve.wait_ge(dve_chain, ch.next())
                tt(cstat[:, 0, :, :], cstat[:, 2, :, :], gates[:, :, 0:H * BR:BR], ALU.mult).then_inc(dve_chain, 1)
                dve.wait_ge(dve_chain, ch.next())
                tt(cstat[:, 1, :, :], cstat[:, 0, :, :],
                           rowok[:, :].unsqueeze(2).broadcast_to([P, T, H]), ALU.mult).then_inc(dve_chain, 1)
                dve.wait_ge(dve_chain, ch.next())
                tt(sc3, sc3, wide(1), ALU.mult).then_inc(pc_done, 1)
                for s in range(U_MLA, U + 3):
                    if s < U:
                        row_max(s)
                    if U_MLA <= s - 1 < U:
                        scale_probs(s - 1)
                    if s - 3 >= U_MLA and (s - 3 - U_MLA) % (2 * T) == 2 * T - 1:
                        pair = (s - 3 - U_MLA) // (2 * T)
                        out_lo(H // 2 + pair, 6 + pair % 2)
                    if s == U_MLA + 2 * T + 1:
                        for k in range(SLOTS):
                            split_lo(dve, l, POS_WOUT + k)
                for k in range(SLOTS, KD):
                    split_lo(dve, l, POS_WOUT + k)
                add_x(l, 0, 0)
                norm_rows(l, 1, 0)
                add_x(l, 0, 1)
                norm_rows(l, 1, 1)
                norm_lo(l, 1, 0)
                add_x(l, 0, 2)
                norm_rows(l, 1, 2)
                norm_lo(l, 1, 1)
                split_lo(dve, l, POS_UP)
                add_x(l, 0, 3)
                norm_rows(l, 1, 3)
                norm_lo(l, 1, 2)
                split_lo(dve, l, POS_UP + 1)
                norm_lo(l, 1, 3)
                split_lo(dve, l, POS_UP + 2)
                split_lo(dve, l, POS_UP + 3)

                def up_tail(f, fl, turn):
                    for tap in (1, 0):
                        for uv in range(2):
                            if tap == 1:
                                dve.wait_ge(t0_done, at(t0_done, l, turn + 2 * fl + uv + 1))
                            back = TAPS - 1 - tap
                            c = cols[:, bass.ds(C_TAP + tap * 2 * FT + f + uv * FT, 1)]
                            ins = stt(out=conv[:, fl, uv, back:S], in0=ps[:, 4 * fl + uv, 0:S - back], scalar=c,
                                      in1=conv[:, fl, uv, back:S], op0=ALU.mult, op1=ALU.add)
                        if tap == 1:
                            ins.then_inc(dve_chain, 1)
                            dve.wait_ge(dve_chain, ch.next())
                    ins.then_inc(conv_done, 1)
                    dve.wait_ge(silu_done, at(silu_done, l, turn // 2 + fl + 1))
                    dve.wait_ge(conv_done, at(conv_done, l, turn // 2 + fl + 1))
                    tt(g_all[:, bass.ds(f, 1), :], silu[:, fl, :].unsqueeze(1), conv[:, fl, 1, :].unsqueeze(1),
                       ALU.mult).then_inc(g_done, 1)

                with dve.Fori(0, FT // 2 - 1) as j:
                    ch.loop(j, 2)
                    for e in range(2):
                        up_tail(2 * j + e, e, 4 * j)
                        for uv in range(2):
                            split_lo(dve, l, POS_UP + SLOTS + 2 * e + uv, SLOTS * j)
                    ch.end_loop(FT // 2 - 1, 2)

                def g_split_lo(k, n, turn=0):
                    dve.wait_ge(gh_done, at(gh_done, l, n + 1 + turn))
                    tt(g_lo[:, n % 2, :].unsqueeze(1), g_all[:, bass.ds(k, 1), :],
                       g_hi[:, n % 2, :].unsqueeze(1).bitcast(F32), ALU.subtract).then_inc(gl_done, 1)

                for e in range(2):
                    g_split_lo(e, e)
                for e in range(2):
                    up_tail(FT - 2 + e, e, 2 * (FT - 2))
                    for uv in range(2):
                        split_lo(dve, l, POS_DOWN + 2 * e + uv)
                for n in range(SLOTS):
                    g_split_lo(n + 2, n + 2)
                    split_lo(dve, l, POS_DOWN + SLOTS + n)
                with dve.Fori(0, DOWN_TURNS) as j:
                    for e in range(SLOTS):
                        g_split_lo(SLOTS * j + SLOTS + e + 2, SLOTS + e + 2, SLOTS * j)
                        split_lo(dve, l, POS_DOWN + 2 * SLOTS + e, SLOTS * j)
                for n in range(SLOTS * (DOWN_TURNS + 1), FT - 2):
                    g_split_lo(n + 2, n + 2)
                    if n + SLOTS < FT:
                        split_lo(dve, l, POS_DOWN + n + SLOTS)
                for t in range(T):
                    add_x(l, 1, t)

                ch.end_layer("dve")

            ch.layer(L)
            for t in range(T):
                norm_rows(L, 0, t, final=True)

        @block.tensor
        def _(pe):
            mm = nc.tensor.matmul

            def mm3(o, lhs, rhs, start, stop):
                mm(o, lhs[0], rhs[0], start=start, stop=False)
                mm(o, lhs[0], rhs[1], start=False, stop=False)
                return mm(o, lhs[1], rhs[0], start=False, stop=stop)

            pe.wait_ge(const_ready, 4)
            pe.sem_inc(split_used, CREDIT["split_used"])

            def norm_transpose(l, w, t):
                pe.wait_ge(hn_done, at(hn_done, l, w * T + t + 1))
                for b in range(2):
                    for k in range(4):
                        last = nc.tensor.transpose(ps[:, 2 * t + b, k * P:(k + 1) * P],
                                                   hn[:, t % 2, (4 * b + k) * P:(4 * b + k + 1) * P], ident[:, :])
                    last.then_inc(tp_done, 1)

            with pe.Fori(0, L) as l:
                def win_first(t):
                    pe.wait_ge(hl_done, at(hl_done, l, 2 * t + 2))
                    tk = slice(t * P, (t + 1) * P)
                    for kp in range(KD // 2):
                        if t == 0:
                            pe.wait_ge(lo_done, split(l, POS_WIN + kp))
                        w = [wslot(b, POS_WIN + kp, [2, CW]) for b in (w_hi, w_lo)]
                        for kk in range(2):
                            k = 2 * kp + kk
                            last = mm3(ps[:, t, 0:CW], [ht_hi[:, k, tk], ht_lo[:, k, tk]],
                                       [w[0][:, kk, :], w[1][:, kk, :]], k == 0, k == KD - 1)
                        if t == T - 1:
                            last.then_inc(split_used, 1)
                    if t < T - 1:
                        last.then_inc(win_acc, 1)

                norm_transpose(l, 0, 0)
                norm_transpose(l, 0, 1)
                for t in range(T):
                    win_first(t)
                    if t + 2 < T:
                        norm_transpose(l, 0, t + 2)

                def win_chunk(c):
                    for kp in range(KD // 2):
                        pos = POS_WIN + c * KD // 2 + kp
                        pe.wait_ge(lo_done, split(l, pos))
                        w = [wslot(b, pos, [2, CW]) for b in (w_hi, w_lo)]
                        for kk in range(2):
                            k = 2 * kp + kk
                            for t in range(T):
                                if k == 0 and c >= 2:
                                    pe.wait_ge(pj[t % 2], at(pj[t % 2], l, (c - 2) * T // 2 + t // 2 + 1))
                                tk = slice(t * P, (t + 1) * P)
                                last = mm3(ps[:, 4 * (c % 2) + t, 0:CW], [ht_hi[:, k, tk], ht_lo[:, k, tk]],
                                           [w[0][:, kk, :], w[1][:, kk, :]], k == 0, k == KD - 1)
                                if k == KD - 1 and t < T - 1:
                                    last.then_inc(win_acc, 1)
                        last.then_inc(split_used, 1)

                win_chunk(1)
                pe.wait_ge(pj_act, at(pj_act, l, T // 2 + 1))
                pe.wait_ge(small_loaded, (l + 1) * 16 * SMALL)
                settle(pe)
                for n in range(TAPS + 1):
                    nc.tensor.transpose(ps[:, 4, n * 2 * FT:(n + 1) * 2 * FT], rows[0:2 * FT, n, :],
                                        ident[0:2 * FT, 0:2 * FT])
                nc.tensor.transpose(ps[:, 4, C_POS:C_POS + 2 * MT], rows[0:2 * MT, TAPS + 1, :],
                                    ident[0:2 * MT, 0:2 * MT])
                nc.tensor.transpose(ps[:, 4, C_B1:C_B1 + 2], rows[0:2, TAPS + 2, :], ident[0:2, 0:2])\
                    .then_inc(cols_tp, 1)
                win_chunk(2)
                pe.wait_ge(cols_ready, at(cols_ready, l, 1))
                win_chunk(3)
                pe.wait_ge(lat_ready, at(lat_ready, l, 1))
                pe.wait_ge(kpe_ready, at(kpe_ready, l, 1))
                for n in range(3):
                    pe.wait_ge(pj[n % 2], at(pj[n % 2], l, 2 * T // 2 + n // 2 + 1))
                    c = (QR, 0, P)[n]
                    for t in range(T):
                        last = nc.tensor.transpose(ps[:, n, t * P:(t + 1) * P], proj[:, t, c:c + P], ident[:, :])
                    last.then_inc(lat_tp, 1)
                pe.wait_ge(pj_dve, at(pj_dve, l, 3 * T // 2))
                settle(pe)
                for t in range(T):
                    last = nc.tensor.transpose(ps[0:2 * ROPE, 3, t * P:(t + 1) * P],
                                               kpe_r[:, t, :, :].rearrange("p a b -> p (a b)"), ident[:, :])
                last.then_inc(lat_tp, 1)

                pe.wait_ge(lo_done, split(l, POS_UKV))
                ukv = [b[:, POS_UKV % SLOTS, :].rearrange("p (h c) -> p h c", h=H) for b in (w_hi, w_lo)]
                uq = [[b[:, (POS_UQ + k) % SLOTS, :].rearrange("p (h c) -> p h c", h=H) for b in (w_hi, w_lo)]
                      for k in range(2)]
                lat = lambda n, c: [ht_hi[:, LAT + n, c], ht_lo[:, LAT + n, c]]
                every = slice(0, S)
                pe.wait_ge(lat_lo, at(lat_lo, l, 1))
                for t in range(T):
                    pe.wait_ge(pj[t % 2], at(pj[t % 2], l, 3 * T // 2 + t // 2 + 1))
                    mm3(ps[:, 4 + t, :].rearrange("p (h c) -> p h c", h=H), lat(0, slice(t * P, (t + 1) * P)),
                        [w[:, :, NOPE:2 * NOPE] for w in ukv], True, True).then_inc(v_acc, 1)

                def qk_item(j, bank):
                    h = j // 2
                    if j % 2 == 0:
                        for k in range(2):
                            last = mm3(ps[:, bank, :], [uq[k][0][:, h, :], uq[k][1][:, h, :]], lat(1 + k, every),
                                       k == 0, k == 1)
                    else:
                        last = mm3(ps[:, bank, :], [ukv[0][:, h, :], ukv[1][:, h, :]], lat(0, every), True, True)
                    last.then_inc(qk_acc, 1)

                pe.wait_ge(lo_done, split(l, POS_UQ + 1))
                pe.wait_ge(lat_lo, at(lat_lo, l, 3))
                pe.wait_ge(kpe_lo, at(kpe_lo, l, 1))
                for j in range(4):
                    qk_item(j, j)

                def scores(u):
                    i, pair = unit(u)
                    n = (i + 1) * P
                    qt = slice(i * P, (i + 1) * P)
                    if u >= 2:
                        pe.wait_ge(exp_done, at(exp_done, l, u - 1))
                    for s in range(2):
                        o = ps[:, 2 * (u % 2) + s, 0:n]
                        if u < U_MLA:
                            c = 4 * (pair % 2) + 2 * s
                            mm3(o, [qs[:, c, qt], qs[:, c + 1, qt]], [ks[:, c, 0:n], ks[:, c + 1, 0:n]], True, False)
                        else:
                            h = (u - U_MLA) // T
                            c = 2 * (2 * (h // GROUP) + s)
                            mm(o, qs[:, h, qt], ks[:, c, 0:n], start=True, stop=False)
                            mm(o, qs[:, h, qt], ks[:, c + 1, 0:n], start=False, stop=False)
                        last = mm(ps[:, 2 * (u % 2) + s, qt], ident_r[:, :], causal_r[:, :], start=False, stop=True)
                    last.then_inc(sc_done, 1)

                def turn(u):
                    i, _ = unit(u)
                    pe.wait_ge(p_done, at(p_done, l, u + 1))
                    if u >= 1:
                        pe.wait_ge(pt_done, at(pt_done, l, u))
                    for s in range(2):
                        for b in range(i + 1):
                            last = nc.tensor.transpose(ps[:, 4 + s, b * P:(b + 1) * P],
                                                       probs[:, u % 2, s, b * P:(b + 1) * P], ident[:, :])
                    last.then_inc(t_done, 1)

                def values(u):
                    i, pair = unit(u)
                    qt = slice(i * P, (i + 1) * P)
                    pe.wait_ge(pt_done, at(pt_done, l, u + 1))
                    if u < U_MLA:
                        if i == 0 and pair > 0:
                            pe.wait_ge(ol_done, at(ol_done, l, pair))
                        for s in range(2):
                            o = ps[64 * s:64 * s + VD, 6, qt]
                            for b in range(i + 1):
                                last = mm(o, vm[:, b, (2 * pair + s) * VD:(2 * pair + s + 1) * VD],
                                          probs_t[:, s, b * P:(b + 1) * P], start=b == 0, stop=b == i)
                    else:
                        h = (u - U_MLA) // T
                        g = h // GROUP
                        r = pair - H // 2
                        if i == 0 and h % 2 == 0:
                            if r >= 2:
                                pe.wait_ge(ol_done, at(ol_done, l, pair - 1))
                        o = ps[64 * (h % 2):64 * (h % 2) + HD, 6 + r % 2, qt]
                        m = NCP * (h % GROUP)
                        mm(o, v_cmp[m:m + NCP, g, :], pct[m:m + NCP, g, qt], start=True, stop=False)
                        for s in range(2):
                            c = COL_KV + (s + 1) * 2 * G * HD + G * HD + g * HD
                            for b in range(i + 1):
                                last = mm(o, proj[:, b, c:c + HD], probs_t[:, s, b * P:(b + 1) * P], start=False,
                                          stop=s == 1 and b == i)
                    last.then_inc(pv_done, 1)

                pe.wait_ge(v_ready, at(v_ready, l, T))
                pe.wait_ge(kpe_copied, at(kpe_copied, l, 1))
                for s in range(U_MLA + 3):
                    if s < U_MLA:
                        if s % T == 0:
                            pe.wait_ge(q_ready, at(q_ready, l, 2 * (s // T) + 2))
                            pe.wait_ge(kl_done, at(kl_done, l, 2 * (s // T) + 2))
                        scores(s)
                        if s + T < U_MLA:
                            j = s + 4
                            if s >= 1:
                                if j % 2:
                                    pe.wait_ge(qf_done, at(qf_done, l, (j - 1) // 2 + 1))
                                else:
                                    pe.wait_ge(kl_done, at(kl_done, l, (j - 1) // 2 + 1))
                            qk_item(j, 7)
                    if 0 <= s - 3 < U_MLA:
                        values(s - 3)
                    if 0 <= s - 2 < U_MLA:
                        turn(s - 2)

                pe.wait_ge(q_roped, at(q_roped, l, 1))
                pe.wait_ge(k_roped, at(k_roped, l, 1))
                for n in range(ITEMS):
                    kind, i = item_kind(n)
                    if n >= 4:
                        pe.wait_ge(it_act, at(it_act, l, n - 3))
                        pe.wait_ge(it_dve, at(it_dve, l, n - 3))
                    c = {"k": COL_KV + (1 + i) * 2 * G * HD, "c": COL_KV + i * G * HD, "q": COL_Q + i * P}[kind]
                    for t in range(T):
                        last = nc.tensor.transpose(ps[:, n % 4, t * P:(t + 1) * P], proj[:, t, c:c + P], ident[:, :])
                    last.then_inc(it_tp, 1)
                pe.wait_ge(it_act, at(it_act, l, 4))
                pe.wait_ge(it_dve, at(it_dve, l, 4))
                pe.wait_ge(pt_done, at(pt_done, l, U_MLA))
                pe.wait_ge(ol_done, at(ol_done, l, H // 2))
                for kv in range(2):
                    for half in range(2):
                        pe.wait_ge(raw_loaded[(POS_CMP + 2 * kv + half) % SLOTS], landed(l, POS_CMP + 2 * kv + half))
                        w1 = wslot(raw, POS_CMP + 2 * kv + half, [MT // 2, CHID])
                        for m in range(MT // 2):
                            mt = half * MT // 2 + m
                            tok = kcv[:, 2 * kv:2 * kv + 2, 2 * mt:2 * mt + CSTRIDE * (NC - 1) + 1:CSTRIDE]
                            last = mm(ps[:, (5, 6)[kv], 0:1], w1[:, m, :],
                                      cols[:, C_POS + kv * MT + mt:C_POS + kv * MT + mt + 1],
                                      start=mt == 0, stop=mt == MT - 1)
                            last = mm(ps[:, (4, 7)[kv], 0:G * NC].rearrange("p (g c) -> p g c", g=G), w1[:, m, :],
                                      tok, start=mt == 0, stop=mt == MT - 1)
                        last.then_inc(cmp_used, 1)
                pe.wait_ge(hid_ready, at(hid_ready, l, 2))
                mm(ps[:, 4, 0:G * NCP], cmp_w2[:, 0:2, :].rearrange("p a b -> p (a b)"),
                   hid[:, 0, :, :].rearrange("p g c -> p (g c)"), start=True, stop=True)
                for g in range(G):
                    for m in range(GROUP):
                        last = mm(ps[NCP * m:NCP * (m + 1), 5, g * HD:(g + 1) * HD], hid[:, 1, g, :], cmp_w2[:, 2, :],
                                  start=True, stop=True)
                last.then_inc(kvc_acc, 1)
                pe.wait_ge(kvc_ready, at(kvc_ready, l, 1))
                pe.wait_ge(it_dve, at(it_dve, l, ITEMS))
                for t in range(T):
                    for h in range(H):
                        o = ps[:, 6 + t // 2, ((t % 2) * H + h) * NCP:((t % 2) * H + h + 1) * NCP]
                        mm(o, qs[:, h, t * P:(t + 1) * P], kc_hi[:, h // GROUP, :], start=True, stop=False)
                        last = mm(o, qs[:, h, t * P:(t + 1) * P], kc_lo[:, h // GROUP, :], start=False, stop=True)
                last.then_inc(cs_acc, 1)
                scores(U_MLA)
                scores(U_MLA + 1)
                pe.wait_ge(pc_done, at(pc_done, l, 1))
                for g in range(G):
                    for t in range(T):
                        last = nc.tensor.transpose(ps[:, 4 + g, t * P:(t + 1) * P],
                                                   scp[:, t, g * GROUP:(g + 1) * GROUP, :], ident[:, :])
                last.then_inc(pc_tp, 1)
                pe.wait_ge(pct_ready, at(pct_ready, l, 1))
                for s in range(U_MLA + 2, U + 3):
                    if s < U:
                        scores(s)
                    if U_MLA <= s - 3 < U:
                        values(s - 3)
                    if U_MLA <= s - 2 < U:
                        turn(s - 2)

                def project_out(t, slot_w, lhs, start, stop):
                    tk = slice(t * P, (t + 1) * P)
                    for hf in range(2):
                        last = mm3(ps[:, 2 * t + hf, :], [lhs[0][:, tk], lhs[1][:, tk]],
                                   [b[:, slot_w, hf * HALF:(hf + 1) * HALF] for b in (w_hi, w_lo)], start, stop)
                    return last

                pe.wait_ge(ol_done, at(ol_done, l, H))
                for k in range(KD - SLOTS):
                    pe.wait_ge(lo_done, split(l, POS_WOUT + k))
                    for t in range(T):
                        last = project_out(t, k % SLOTS, [ht_hi[:, k, :], ht_lo[:, k, :]], k == 0, False)
                    last.then_inc(split_used, 1)
                for t in range(T):
                    for k in range(KD - SLOTS, KD):
                        if t == 0:
                            pe.wait_ge(lo_done, split(l, POS_WOUT + k))
                        last = project_out(t, k % SLOTS, [ht_hi[:, k, :], ht_lo[:, k, :]], False, k == KD - 1)
                        if t == T - 1:
                            last.then_inc(split_used, 1)
                    if t < T - 1:
                        last.then_inc(out_acc, 1)
                    if t >= 1:
                        norm_transpose(l, 1, t - 1)
                norm_transpose(l, 1, T - 1)

                def up_half(pos, bank, turn, toks=slice(0, S)):
                    w = [wslot(b, pos, [KD, P]) for b in (w_hi, w_lo)]
                    for k in range(KD):
                        last = mm3(ps[:, bank, toks], [w[0][:, k, :], w[1][:, k, :]],
                                   [ht_hi[:, k, toks], ht_lo[:, k, toks]], k == 0, k == KD - 1)
                    return last

                first, rest = slice(0, S - P), slice(S - P, S)
                for uv in range(2):
                    pe.wait_ge(lo_done, split(l, POS_UP + uv))
                    pe.wait_ge(hl_done, at(hl_done, l, 4 * T - 2))
                    up_half(POS_UP + uv, uv, 0, first)
                pe.wait_ge(hl_done, at(hl_done, l, 4 * T))
                for uv in range(2):
                    up_half(POS_UP + uv, uv, 0, rest).then_inc(split_used, 1)
                for uv in range(2):
                    pe.wait_ge(lo_done, split(l, POS_UP + 2 + uv))
                    up_half(POS_UP + 2 + uv, 4 + uv, 0).then_inc(split_used, 1)
                with pe.Fori(0, FT // 2 - 1) as j:
                    for e in range(2):
                        pe.wait_ge(g_done, at(g_done, l, e + 1 + 2 * j))
                        for uv in range(2):
                            pos = POS_UP + SLOTS + 2 * e + uv
                            pe.wait_ge(lo_done, split(l, pos, SLOTS * j))
                            up_half(pos, 4 * e + uv, SLOTS * j).then_inc(split_used, 1)

                g_pair = [[g_hi[:, slot, :], g_lo[:, slot, :]] for slot in range(2)]

                def down_ready(n, turn=0):
                    pe.wait_ge(lo_done, split(l, POS_DOWN + n, turn))
                    pe.wait_ge(gl_done, at(gl_done, l, n + 1 + turn))

                down_ready(0)
                for t in (1, 3, 0, 2):
                    if t == 0:
                        pe.wait_ge(g_done, at(g_done, l, FT - 1))
                    if t == 2:
                        pe.wait_ge(g_done, at(g_done, l, FT))
                    last = project_out(t, 0, g_pair[0], True, False)
                last.then_inc(split_used, 1)
                for k in range(1, SLOTS):
                    down_ready(k)
                    for t in range(T):
                        last = project_out(t, k, g_pair[k % 2], False, False)
                    last.then_inc(split_used, 1)
                with pe.Fori(0, FT // SLOTS - 1) as j:
                    for e in range(SLOTS):
                        down_ready(SLOTS + e, SLOTS * j)
                        for t in range(T):
                            last = project_out(t, e, g_pair[e % 2], False, False)
                        last.then_inc(split_used, 1)
                for k in range(FT - 2, FT):
                    down_ready(k)
                for t in range(T):
                    for k in range(FT - 2, FT):
                        last = project_out(t, k % SLOTS, g_pair[k % 2], False, k == FT - 1)
                        if t == T - 1:
                            last.then_inc(split_used, 1)
                    if t < T - 1:
                        last.then_inc(out_acc, 1)


_INS = ["x", "attn_norm", "w_in", "mla_q_norm", "mla_kv_norm", "mla_w_uq", "mla_w_ukv", "nsa_gate_bias",
        "nsa_cmp_pos", "nsa_cmp_w1", "nsa_cmp_b1", "nsa_cmp_w2", "w_out", "ffn_norm", "ffn_w_up", "ffn_conv_w",
        "ffn_conv_b", "ffn_w_down", "final_norm"]


def kernel(**inputs):
    import numpy as _np
    import concourse.bacc as _bacc
    from concourse import mybir as _mybir
    from concourse.bass_utils import run_bass_kernel_spmd as _run

    nc = _bacc.Bacc("TRN2", target_bir_lowering=False, num_devices=1)
    arrays, args = {}, {}
    given = {n: _np.ascontiguousarray(inputs[n]) for n in _INS}
    for name, v in {**given, **shape_constants()}.items():
        arrays[f"in_{name}_dram"] = v
        args[name] = nc.dram_tensor(f"in_{name}_dram", v.shape, _mybir.dt.from_np(v.dtype), kind="ExternalInput").ap()
    out = nc.dram_tensor("out_0_dram", (1, S, D), _mybir.dt.float32, kind="ExternalOutput").ap()
    hybrid_layers(nc, args, out)
    r = _run(nc, [arrays], core_ids=[0])
    return r.results[0]["out_0_dram"]
```

```python
from contextlib import ExitStack

import numpy as np

import concourse.bass as bass
from concourse import mybir

F32 = mybir.dt.float32
F32R = mybir.dt.float32r
BF16 = mybir.dt.bfloat16
ALU = mybir.AluOpType
ACT = mybir.ActivationFunctionType
AX = mybir.AxisListType.X

P = 128
D = 1024
S = 512
L = 2
T = S // P
KD = D // P
EPS = 1e-6
NEG = -1e30
THETA = 500000.0

H = 8
QR, KVR, ROPE, NOPE, VD = 256, 128, 32, 64, 64
QK = NOPE + ROPE
HD = 64
ROT = HD // 4
G = 2
BR = 3
GROUP = H // G
CLEN, CSTRIDE, CHID = 32, 16, 128
NC = (S - CLEN) // CSTRIDE + 1
NCP = NC + 1
DFF = 2816
FT = DFF // P
TAPS = 3

COL_Q = QR + KVR + ROPE
COL_KV = COL_Q + H * HD
COL_GATE = COL_KV + BR * 2 * G * HD
COLS = COL_GATE + H * BR
CH = 4
CW = COLS // CH
HALF = D // 2
MT = CLEN * HD // P
LAT = 3
KP_LAST = (1, 2, 3, 0)
CMP_COLS = 2 * NCP
U_MLA = (H // 2) * T
U_NSA = H * T
U = U_MLA + U_NSA

C_TAP, C_CB = 0, TAPS * 2 * FT
C_POS = C_CB + 2 * FT
C_B1 = C_POS + 2 * MT
C_END = C_B1 + 2

SLOTS = 4
POS_WIN = 2
POS_UKV = POS_WIN + CH * KD // 2
POS_UQ = POS_UKV + 1
POS_CMP = POS_UQ + 2
POS_WOUT = -(-(POS_CMP + 4) // SLOTS) * SLOTS
POS_UP = POS_WOUT + KD
POS_DOWN = POS_UP + 2 * FT
POS_END = POS_DOWN + FT
PERIOD = -(-POS_END // SLOTS) * SLOTS
DOWN_TURNS = FT // SLOTS - 2
assert POS_WOUT % SLOTS == 0 and POS_UP % SLOTS == 0 and POS_DOWN % SLOTS == 0
RAW_POS = [p for p in range(POS_WIN, POS_END) if not POS_CMP + 4 <= p < POS_WOUT]
SPLIT_POS = [p for p in RAW_POS if not POS_CMP <= p < POS_CMP + 4]
MLA_POS = [POS_UKV, POS_UQ, POS_UQ + 1]
USED_POS = [p for p in SPLIT_POS if p not in MLA_POS]
CMP_POS = list(range(POS_CMP, POS_CMP + 4))
LOADS_PER_SLOT = [sum(p % SLOTS == s for p in RAW_POS) for s in range(SLOTS)]

ITEMS = [("k", 0), ("q", 0), ("q", 1), ("c", 0), ("c", 1), ("k", 1), ("q", 2), ("q", 3)]
NI = len(ITEMS)
PRE = U_MLA - T

PER_LAYER = {
    "x_done": 2 * T, "sd_done": 2 * T, "hn_done": 2 * T, "tp_done": 4 * T, "hh_done": 4 * T,
    "hl_done": 4 * T,
    "hi_done": len(SPLIT_POS), "lo_done": len(SPLIT_POS), "split_used": len(USED_POS), "cmp_used": 4,
    "win_acc": CH * (T - 1), "pj_act": CH * T // 2, "pj_dve": CH * T // 2,
    "lat_sq": 1, "lat_ready": 1, "kpe_ready": 1, "lat_tp": 4, "cols_tp": 1, "lat_hi": 4,
    "lat_lo": 3, "kpe_lo": 1, "cols_ready": 1,
    "q_roped": 1, "k_roped": 1, "gate_in": 1, "gate_exp": 1, "gates_ready": 1,
    "v_acc": T, "v_ready": T, "qk_acc": 2 * H, "qf_done": H, "qh_done": H, "kh_done": H, "q_ready": H, "kl_done": H,
    "sc_done": U, "max_done": U, "exp_done": U, "p_done": U, "t_done": U, "pt_done": U, "pv_done": U,
    "oh_done": H, "ol_done": H,
    "it_tp": NI, "it_act": NI, "it_dve": NI,
    "pos_ready": 1, "kcz_ready": 1, "hid_out": 1, "hid_tp": 1, "hb_done": 1, "hid_ready": 1, "kvc_acc": 1, "kch_done": 1,
    "kvc_ready": 1, "cs_acc": G, "cs_out": G, "cs_back": 2, "cs_in": 2,
    "cs_sub": 1, "cs_exp": 1, "pc_done": 1, "pc_tp": G, "pct_ready": G,
    "t0_done": 2 * FT, "conv_done": FT, "silu_done": FT, "g_done": FT,
    "gh_done": FT, "gl_done": FT, "out_acc": 2 * (T - 1),
}
CREDIT = {"x_done": T, "hn_done": 1, "lo_done": SLOTS, "split_used": SLOTS}


def at(s, l, n):
    return l * PER_LAYER[s.name] + (n + CREDIT.get(s.name, 0))


def nth(positions, pos):
    return sum(p <= pos for p in positions)


def before_in_slot(pos):
    same = [p for p in RAW_POS if p % SLOTS == pos % SLOTS]
    earlier = [p for p in same if p < pos]
    return (0, earlier[-1]) if earlier else (-1, same[-1])


def split_before_in_slot(pos):
    same = [p for p in SPLIT_POS if p % SLOTS == pos % SLOTS]
    earlier = [p for p in same if p < pos]
    return (0, earlier[-1]) if earlier else (-1, same[-1])


def rope_tables(dim):
    inv = (np.float32(THETA) ** (-np.arange(0, dim, 2, dtype=np.float32) / np.float32(dim))).astype(np.float32)
    ang = np.arange(S, dtype=np.float32)[:, None] * inv[None, :]
    return np.cos(ang).astype(np.float32), np.sin(ang).astype(np.float32)


def shape_constants():
    c, s = rope_tables(ROT)
    nsa = np.concatenate([c, c, -s, s], 1)
    c, s = rope_tables(ROPE)
    mla = np.concatenate([c, c, -s, s], 1)
    rope = np.concatenate([nsa, mla], 1).reshape(T, P, 2 * (ROT + ROPE)).transpose(1, 0, 2)
    table = np.concatenate([np.ones((NOPE, S)), np.concatenate([c, c], 1).T, np.concatenate([-s, s], 1).T], 0)
    table = table * QK ** -0.5
    q = np.arange(P)
    causal = np.where(q[None, :] <= q[:, None], 0.0, NEG)
    end = np.arange(NCP) * CSTRIDE + CLEN - 1
    pos = np.arange(T)[None, :, None] * P + q[:, None, None]
    cmask = np.where((end[None, None, :] <= pos) & (np.arange(NCP) < NC), 0.0, NEG)
    rowok = (pos[:, :, 0] >= CLEN - 1) * 1.0
    f = lambda a: np.ascontiguousarray(a, dtype=np.float32)
    return {"c_rope": f(rope), "c_table": f(table), "c_causal": f(causal), "c_ident": f(np.eye(P)),
            "c_cmask": f(cmask), "c_rowok": f(rowok)}


class Steps:

    def __init__(self, per_layer):
        self.per_layer, self.base, self.n = per_layer, 0, 0

    def layer(self, l):
        self.base, self.n = l * self.per_layer, 0

    def end_layer(self, name):
        assert self.n == self.per_layer, (name, self.n)

    def next(self):
        self.n += 1
        return self.base + self.n

    def loop(self, j, per_turn):
        self.outer = (self.base, self.n)
        self.base, self.n = self.base + self.n + j * per_turn, 0

    def end_loop(self, turns, per_turn):
        assert self.n == per_turn, ("turn", self.n)
        self.base, self.n = self.outer[0], self.outer[1] + turns * per_turn


def hybrid_layers(nc, a, out):
    with ExitStack() as ctx:
        def sb(name, shape, dt=F32, scope=ctx):
            return scope.enter_context(nc.sbuf_tensor(name, shape, dt))

        x = sb("x", [P, T, D])
        under = ExitStack()
        kst = []
        for name in ("k_operand", "v_operand"):
            sb(name + "_below", [P, KD - 2, S], F32, under)
            kst.append(sb(name, [P, MT, CMP_COLS], F32, under))
        under.close()
        ht_hi = sb("ht_hi", [P, KD, S], F32R)
        ht_lo = sb("ht_lo", [P, KD, S], F32R)
        raw = sb("raw", [P, SLOTS, 1024])
        w_hi = sb("w_hi", [P, SLOTS, 1024], F32R)
        w_lo = sb("w_lo", [P, SLOTS, 1024], F32R)
        norm_g = sb("norm_g", [P, D])
        probs = sb("probs", [P, 2, 2, S])
        probs_t = sb("probs_t", [P, 2, S])
        ident = sb("ident", [P, P])
        ident_b = sb("ident_b", [P, P], BF16)
        causal = sb("causal", [P, P])
        causal_b = sb("causal_b", [P, P], BF16)
        table = sb("table", [P, S])
        rope = sb("rope", [P, T, 2 * (ROT + ROPE)])
        cmask = sb("cmask", [P, T, NCP])
        rowok = sb("rowok", [P, T])
        cols = sb("cols", [P, C_END])
        lat_g = sb("lat_g", [P, QR + KVR])
        gate_b = sb("gate_b", [P, H * BR])
        cmp_w2 = sb("cmp_w2", [P, 3, HD])
        eps = sb("eps", [P, 1])
        ms = sb("ms", [P, T])
        sd = sb("sd", [P, T])
        rstd = sb("rstd", [P, T])
        lat_ms = sb("lat_ms", [P, 2 * T])
        lat_sd = sb("lat_sd", [P, 2 * T])
        lat_rstd = sb("lat_rstd", [P, 2 * T])
        nmax = sb("nmax", [P, 4, 2])
        rsum = sb("rsum", [P, 4, 2])
        rinv = sb("rinv", [P, 4, 2])
        rgate = sb("rgate", [P, 4, 2])
        qf = sb("qf", [P, S])
        gate_e = sb("gate_e", [P, T, H * BR])
        gates = sb("gates", [P, T, H * BR])
        hid = sb("hid", [P, 2, G, NCP])
        hid_b = sb("hid_b", [P, 2])
        v_cmp = sb("v_cmp", [P, G, HD])
        cstat = sb("cstat", [P, 3, T, H])
        tmp_pool = sb("tmp_pool", [P, 2, H, ROT])
        kpe_t = sb("kpe_t", [P, 2, T, ROPE])
        kpe_r = sb("kpe_r", [P, T, 2, ROPE])

        attn = ExitStack()
        proj = sb("proj", [P, T, COLS], F32, attn)
        qs = sb("qs", [P, 8, S], F32R, attn)
        ks = sb("ks", [P, 8, S], F32R, attn)
        vm = sb("vm", [P, T, H * VD], F32, attn)
        attn.close()
        ffn = ExitStack()
        g_all = sb("g_all", [P, FT, S], F32, ffn)
        g_hi = sb("g_hi", [P, 2, S], F32R, ffn)
        g_lo = sb("g_lo", [P, 2, S], F32R, ffn)
        conv = sb("conv", [P, 2, 2, S], F32, ffn)
        silu = sb("silu", [P, 2, S], F32, ffn)
        ffn.close()

        rows = probs_t[:, :, :].rearrange("p a (b c) -> p (a b) c", c=P)
        hn = probs[:, :, :, :].rearrange("p s a n -> p s (a n)")
        KCZ = 2 * P - NCP
        kcz_hi, kcz_lo = [b[:, KD - 2, 0:G * KCZ].rearrange("p (g c) -> p g c", g=G) for b in (ht_hi, ht_lo)]
        kc_hi, kc_lo = [b[:, :, P - NCP:P] for b in (kcz_hi, kcz_lo)]
        hid_rows = kpe_t[0:CMP_COLS, :, :, :].rearrange("p a t n -> p a (t n)")
        scp = vm[:, 0:2, :].rearrange("p a (t h c) -> p (a t) h c", t=T // 2, h=H)
        cs_t = vm[:, 2:4, :]

        ps = ctx.enter_context(nc.psum_tensor("ps", [P, 8, S], F32))

        def sem(name):
            return ctx.enter_context(nc.semaphore(name))

        x_done = sem("x_done")
        sd_done = sem("sd_done")
        hn_done = sem("hn_done")
        tp_done = sem("tp_done")
        hh_done = sem("hh_done")
        hl_done = sem("hl_done")
        hi_done = sem("hi_done")
        lo_done = sem("lo_done")
        split_used = sem("split_used")
        cmp_used = sem("cmp_used")
        win_acc = sem("win_acc")
        pj_act = sem("pj_act")
        pj_dve = sem("pj_dve")
        lat_sq = sem("lat_sq")
        lat_ready = sem("lat_ready")
        kpe_ready = sem("kpe_ready")
        lat_tp = sem("lat_tp")
        cols_tp = sem("cols_tp")
        lat_hi = sem("lat_hi")
        lat_lo = sem("lat_lo")
        kpe_lo = sem("kpe_lo")
        cols_ready = sem("cols_ready")
        q_roped = sem("q_roped")
        k_roped = sem("k_roped")
        gate_in = sem("gate_in")
        gate_exp = sem("gate_exp")
        gates_ready = sem("gates_ready")
        v_acc = sem("v_acc")
        v_ready = sem("v_ready")
        qk_acc = sem("qk_acc")
        qf_done = sem("qf_done")
        kh_done = sem("kh_done")
        qh_done = sem("qh_done")
        q_ready = sem("q_ready")
        kl_done = sem("kl_done")
        sc_done = sem("sc_done")
        max_done = sem("max_done")
        exp_done = sem("exp_done")
        p_done = sem("p_done")
        t_done = sem("t_done")
        pt_done = sem("pt_done")
        pv_done = sem("pv_done")
        oh_done = sem("oh_done")
        ol_done = sem("ol_done")
        it_tp = sem("it_tp")
        it_act = sem("it_act")
        it_dve = sem("it_dve")
        pos_ready = sem("pos_ready")
        kcz_ready = sem("kcz_ready")
        hid_out = sem("hid_out")
        hid_tp = sem("hid_tp")
        hb_done = sem("hb_done")
        hid_ready = sem("hid_ready")
        kvc_acc = sem("kvc_acc")
        kch_done = sem("kch_done")
        kvc_ready = sem("kvc_ready")
        cs_acc = sem("cs_acc")
        cs_out = sem("cs_out")
        cs_back = sem("cs_back")
        cs_in = sem("cs_in")
        cs_sub = sem("cs_sub")
        cs_exp = sem("cs_exp")
        pc_done = sem("pc_done")
        pc_tp = sem("pc_tp")
        pct_ready = sem("pct_ready")
        t0_done = sem("t0_done")
        conv_done = sem("conv_done")
        silu_done = sem("silu_done")
        g_done = sem("g_done")
        gh_done = sem("gh_done")
        gl_done = sem("gl_done")
        out_acc = sem("out_acc")
        pj = [pj_act, pj_dve]
        raw_loaded = [sem(f"raw_loaded{s}") for s in range(SLOTS)]
        x_loaded = sem("x_loaded")
        const_loaded = sem("const_loaded")
        g_loaded = sem("g_loaded")
        small_loaded = sem("small_loaded")
        const_ready = sem("const_ready")
        settled = sem("settled")
        out_done = [sem(f"out_done{i}") for i in range(2)]
        act_chain = ctx.enter_context(nc.semaphore("act_chain"))
        dve_chain = ctx.enter_context(nc.semaphore("dve_chain"))
        pool_chain = ctx.enter_context(nc.semaphore("pool_chain"))

        def settle(eng):
            eng.sem_inc(settled, 1)

        block = ctx.enter_context(nc.Block())
        consts = [(ident, "c_ident"), (causal, "c_causal"), (table, "c_table"), (rope, "c_rope"),
                  (cmask, "c_cmask"), (rowok, "c_rowok")]
        SMALL = 9

        def wslot(buf, pos, shape):
            n = int(np.prod(shape))
            v = buf[:, pos % SLOTS, 0:n]
            return v.rearrange("p (a b) -> p a b", b=shape[-1]) if len(shape) == 2 else v

        @block.sync
        def _(sp):
            for t in range(T):
                sp.dma_start(x[:, t, :], a["x"][0, t * P:(t + 1) * P, :]).then_inc(x_loaded, 16)

            def load(l, pos, src, shape, turn=0):
                back, prev = before_in_slot(pos)
                if prev in CMP_POS:
                    sp.wait_ge(cmp_used, at(cmp_used, l, nth(CMP_POS, prev)))
                else:
                    sp.wait_ge(lo_done, at(lo_done, l, back * len(SPLIT_POS) + nth(SPLIT_POS, prev) + turn))
                sp.dma_start(wslot(raw, pos, shape), src).then_inc(raw_loaded[pos % SLOTS], 16)

            with sp.Fori(0, L) as l:
                w_in = a["w_in"][bass.ds(l, 1), :, :].rearrange("o (k p) n -> p (o k) n", p=P)
                for c in range(CH):
                    for n in range(KD // 2):
                        kp = KP_LAST[n] if c == CH - 1 else n
                        load(l, POS_WIN + c * KD // 2 + n, w_in[:, 2 * kp:2 * kp + 2, c * CW:(c + 1) * CW], [2, CW])
                load(l, POS_UKV, a["mla_w_ukv"][bass.ds(l, 1), :, :].rearrange("o p n -> (o p) n"), [H * 2 * NOPE])
                uq = a["mla_w_uq"][bass.ds(l, 1), :, :].rearrange("o (k p) n -> p (o k) n", p=P)
                for k in range(2):
                    load(l, POS_UQ + k, uq[:, k, :], [H * QK])
                w1 = a["nsa_cmp_w1"][bass.ds(l, 1), :, :, :].rearrange("o a (m p) n -> p (o a m) n", p=P)
                for n in range(4):
                    load(l, POS_CMP + n, w1[:, n * MT // 2:(n + 1) * MT // 2, :], [MT // 2, CHID])
                w_out = a["w_out"][bass.ds(l, 1), :, :].rearrange("o (k p) n -> p (o k) n", p=P)
                for k in range(KD):
                    load(l, POS_WOUT + k, w_out[:, k, :], [D])
                up = a["ffn_w_up"][bass.ds(l, 1), :, :].rearrange("o (k p) n -> p (o k) n", p=P)

                def load_up(f, pos, turn):
                    for uv in range(2):
                        load(l, pos + uv, up[:, :, bass.ds(f * P + uv * DFF, P)], [KD, P], turn)

                load_up(0, POS_UP, 0)
                load_up(1, POS_UP + 2, 0)
                with sp.Fori(1, FT // 2) as j:
                    for e in range(2):
                        load_up(2 * j + e, POS_UP + SLOTS + 2 * e, (j - 1) * SLOTS)
                down = a["ffn_w_down"][bass.ds(l, 1), :, :].rearrange("o (k p) n -> (o k) p n", p=P)
                with sp.Fori(0, FT // SLOTS) as j:
                    for e in range(SLOTS):
                        load(l, POS_DOWN + e, down[bass.ds(SLOTS * j + e, 1), :, :].rearrange("k p n -> (k p) n"),
                             [D], j * SLOTS)
                for k in range(FT // SLOTS * SLOTS, FT):
                    load(l, POS_DOWN + k, down[k, :, :], [D])

            for t in range(T):
                sp.wait_ge(hn_done, at(hn_done, L, t + 1))
                sp.dma_start(out[0, t * P:(t + 1) * P, :], hn[:, t % 2, :]).then_inc(out_done[t % 2], 16)
            for slot in out_done:
                sp.wait_ge(slot, 16 * T // 2)

        def slot_loads(pos):
            return sum(p % SLOTS == pos % SLOTS and p <= pos for p in RAW_POS)

        def landed(l, pos, turns=0):
            return (l * LOADS_PER_SLOT[pos % SLOTS] + slot_loads(pos) + turns) * 16

        def split(l, pos, turn=0):
            return at(lo_done, l, nth(SPLIT_POS, pos) + turn)

        def used(l, pos, turn=0):
            return at(split_used, l, nth(USED_POS, pos) + turn)

        def pieces_map(pos):
            if POS_UQ <= pos < POS_UQ + 2:
                d = lambda b: b[:, pos % SLOTS, :].rearrange("p (h c) -> p h c", h=H)
                r = lambda b: b[:, pos % SLOTS, 0:H * QK].rearrange("p (h c) -> p h c", h=H)
                half = ROPE // 2
                return [(d, r, (0, QK), (0, QK)), (d, r, (QK, QK + half), (NOPE + half, QK)),
                        (d, r, (QK + half, P), (NOPE, NOPE + half))]
            n = 2 * CW if pos < POS_UKV else 1024
            whole = lambda b: b[:, pos % SLOTS, 0:n].unsqueeze(1)
            return [(whole, whole, (0, n), (0, n))]

        def split_hi(act, l, pos, turn=0, turns=0):
            act.wait_ge(raw_loaded[(pos) % SLOTS], landed(l, pos, turns))
            back, prev = split_before_in_slot(pos)
            if prev in MLA_POS:
                act.wait_ge(qk_acc, at(qk_acc, l, 2 * H))
            else:
                act.wait_ge(split_used, at(split_used, l, back * len(USED_POS) + nth(USED_POS, prev) + turn))
            for d, r, (d0, d1), (r0, r1) in pieces_map(pos):
                last = nc.scalar.activation(d(w_hi)[:, :, d0:d1], r(raw)[:, :, r0:r1], ACT.Copy)
            last.then_inc(hi_done, 1)

        def split_lo(dve, l, pos, turn=0):
            dve.wait_ge(hi_done, at(hi_done, l, nth(SPLIT_POS, pos) + turn))
            for d, r, (d0, d1), (r0, r1) in pieces_map(pos):
                last = nc.vector.tensor_tensor(d(w_lo)[:, :, d0:d1], r(raw)[:, :, r0:r1],
                                               d(w_hi)[:, :, d0:d1].bitcast(F32), ALU.subtract)
            last.then_inc(lo_done, 1)

        def halves(h):
            top, bottom = slice(0, HD), slice(HD, P)
            return (top, bottom) if h % 2 == 0 else (bottom, top)

        def unit(u):
            if u < U_MLA:
                return u % T, u // T
            return u % T, H // 2 + (u - U_MLA) // T // 2

        def score_banks(u):
            n = (u % T + 1) * P
            if u >= U_MLA and 2 * n <= S:
                return ps[:, 2 * (u % 2), 0:2 * n].rearrange("p (a n) -> p a n", a=2)
            return ps[:, 2 * (u % 2):2 * (u % 2) + 2, 0:n]

        @block.gpsimd
        def _(pool):
            ch = Steps(2 * (T + T * BR))
            tt = nc.gpsimd.tensor_tensor

            def rotate(t, v, heads):
                c = rope[:, t, 0:ROT].unsqueeze(1).broadcast_to([P, heads, ROT])
                s = rope[:, t, ROT:2 * ROT].rearrange("p (a b) -> p a b", a=2).unsqueeze(1)\
                    .broadcast_to([P, heads, 2, ROT // 2])
                m0, m1 = tmp_pool[:, 0, 0:heads, :], tmp_pool[:, 1, 0:heads, :]
                tt(m0, v, c, ALU.mult)
                swapped = v.rearrange("p h (a b) -> p h a b", a=2)[:, :, ::-1, :]
                tt(m1.rearrange("p h (a b) -> p h a b", a=2), swapped, s, ALU.mult).then_inc(pool_chain, 1)
                pool.wait_ge(pool_chain, ch.next())
                return tt(v, m0, m1, ALU.add)

            with pool.Fori(0, L) as l:
                ch.layer(l)
                pool.wait_ge(hn_done, at(hn_done, l, 0))
                settle(pool)
                pool.dma_start(norm_g[:, :], a["attn_norm"][bass.ds(l, 1), :].broadcast_to([P, D])).then_inc(g_loaded, 16)
                pool.wait_ge(x_done, at(x_done, l, 1 - T))
                settle(pool)
                bd = lambda v, n: v.broadcast_to([P, n])
                pool.dma_start(lat_g[:, 0:QR], bd(a["mla_q_norm"][bass.ds(l, 1), :], QR)).then_inc(small_loaded, 16)
                pool.dma_start(lat_g[:, QR:QR + KVR], bd(a["mla_kv_norm"][bass.ds(l, 1), :], KVR))\
                    .then_inc(small_loaded, 16)
                pool.dma_start(gate_b[:, :], bd(a["nsa_gate_bias"][bass.ds(l, 1), :], H * BR)).then_inc(small_loaded, 16)
                w2 = a["nsa_cmp_w2"][bass.ds(l, 1), :, :, :].rearrange("o a p n -> p (o a) n")
                pool.dma_start(cmp_w2[:, 0, :], w2[:, 0, :]).then_inc(small_loaded, 16)
                pool.dma_start(cmp_w2[:, 1:3, :], w2).then_inc(small_loaded, 16)
                pool.dma_start(rows[0:2 * FT, 0:TAPS, :], a["ffn_conv_w"][bass.ds(l, 1), :, :]
                               .rearrange("o a (f p) -> f (o a) p", p=P)).then_inc(small_loaded, 16)
                pool.dma_start(rows[0:2 * FT, TAPS, :], a["ffn_conv_b"][bass.ds(l, 1), :]
                               .rearrange("o (f p) -> (o f) p", p=P)).then_inc(small_loaded, 16)
                pool.dma_start(rows[0:2 * MT, TAPS + 1, :].rearrange("m (j d) -> m j d", d=HD),
                               a["nsa_cmp_pos"][bass.ds(l, 1), :, :, :]
                               .rearrange("o a (m j) d -> (o a m) j d", j=2)).then_inc(small_loaded, 16)
                pool.dma_start(rows[0:2, TAPS + 2, :], a["nsa_cmp_b1"][bass.ds(l, 1), :, :]
                               .rearrange("o a n -> (o a) n")).then_inc(small_loaded, 16)
                pool.wait_ge(hn_done, at(hn_done, l, T))
                settle(pool)
                pool.dma_start(norm_g[:, :], a["ffn_norm"][bass.ds(l, 1), :].broadcast_to([P, D])).then_inc(g_loaded, 16)
                pool.wait_ge(pj_act, at(pj_act, l, CH * T // 2))
                pool.wait_ge(pj_dve, at(pj_dve, l, CH * T // 2))
                tt(gate_e[:, :, :], proj[:, :, COL_GATE:COLS],
                   gate_b[:, :].unsqueeze(1).broadcast_to([P, T, H * BR]), ALU.add).then_inc(gate_in, 1)
                for t in range(T):
                    last = rotate(t, proj[:, t, COL_Q:COL_KV].rearrange("p (h d) -> p h d", h=H)[:, :, 0:ROT], H)
                    last.then_inc(pool_chain, 1)
                    pool.wait_ge(pool_chain, ch.next())
                pool.sem_inc(q_roped, 1)
                for t in range(T):
                    for b in range(BR):
                        c0 = COL_KV + b * 2 * G * HD
                        last = rotate(t, proj[:, t, c0:c0 + G * HD].rearrange("p (h d) -> p h d", h=G)[:, :, 0:ROT], G)
                        last.then_inc(pool_chain, 1)
                        pool.wait_ge(pool_chain, ch.next())
                pool.sem_inc(k_roped, 1)
                for kv in range(2):
                    pos = cols[:, C_POS + kv * MT:C_POS + (kv + 1) * MT].unsqueeze(2).broadcast_to([P, MT, 2])
                    last = nc.gpsimd.tensor_copy(kst[kv][:, :, 2 * NC:CMP_COLS], pos)
                last.then_inc(pos_ready, 1)
                pool.wait_ge(cmp_used, at(cmp_used, l, 4))
                settle(pool)
                for b in (kcz_hi, kcz_lo):
                    last = nc.gpsimd.memset(b.bitcast(F32), 0.0)
                last.then_inc(kcz_ready, 1)
                ch.end_layer("pool")
            pool.wait_ge(hn_done, at(hn_done, L, 0))
            pool.dma_start(norm_g[:, :], a["final_norm"].rearrange("(o d) -> o d", o=1).broadcast_to([P, D]))\
                .then_inc(g_loaded, 16)

        @block.scalar
        def _(act):
            for tile, name in consts:
                act.dma_start(tile[tuple(slice(None) for _ in tile.shape)], a[name]).then_inc(const_loaded, 16)
            ch = Steps(2 * T + 1)
            activate = nc.scalar.activation

            def norm_stats(l, w, t):
                act.wait_ge(x_done, at(x_done, l, w * T + t + 1 - T))
                activate(ps[:, 2 * t:2 * t + 2, :], x[:, t, :].rearrange("p (a n) -> p a n", a=2), ACT.Square,
                                 scale=D ** -0.5, accum_out=ms[:, t:t + 1]).then_inc(act_chain, 1)
                act.wait_ge(act_chain, ch.next())
                activate(sd[:, t:t + 1], ms[:, t:t + 1], ACT.Sqrt, bias=eps[:, :]).then_inc(sd_done, 1)

            def norm_hi(l, w, t):
                for b in range(2):
                    act.wait_ge(tp_done, at(tp_done, l, 2 * (w * T + t) + b + 1))
                    activate(ht_hi[:, 4 * b:4 * b + 4, t * P:(t + 1) * P],
                             ps[:, 2 * t + b, :].rearrange("p (k n) -> p k n", k=4), ACT.Copy)\
                        .then_inc(hh_done, 1)

            act.wait_ge(const_ready, 4)

            with act.Fori(0, L) as l:
                ch.layer(l)
                norm_stats(l, 0, 0)
                split_hi(act, l, POS_WIN)
                norm_stats(l, 0, 1)
                norm_hi(l, 0, 0)
                split_hi(act, l, POS_WIN + 1)
                split_hi(act, l, POS_WIN + 2)
                norm_stats(l, 0, 2)
                norm_hi(l, 0, 1)
                split_hi(act, l, POS_WIN + 3)
                norm_stats(l, 0, 3)
                norm_hi(l, 0, 2)
                norm_hi(l, 0, 3)

                def evac_chunk(c):
                    for t in range(0, T, 2):
                        act.wait_ge(win_acc, at(win_acc, l, c * (T - 1) + t + 1))
                        activate(proj[:, t, c * CW:(c + 1) * CW], ps[:, 4 * (c % 2) + t, 0:CW], ACT.Copy)\
                            .then_inc(pj_act, 1)

                def win_splits(c):
                    for kp in range(KD // 2):
                        split_hi(act, l, POS_WIN + c * KD // 2 + kp)

                win_splits(1)
                evac_chunk(0)
                act.wait_ge(pj_act, at(pj_act, l, T // 2))
                act.wait_ge(pj_dve, at(pj_dve, l, T // 2))
                for t in range(T):
                    activate(ps[:, t, 0:QR], proj[:, t, 0:QR], ACT.Square, scale=QR ** -0.5,
                             accum_out=lat_ms[:, 2 * t:2 * t + 1])
                    last = activate(ps[:, t, QR:QR + KVR], proj[:, t, QR:QR + KVR], ACT.Square, scale=KVR ** -0.5,
                                    accum_out=lat_ms[:, 2 * t + 1:2 * t + 2])
                last.then_inc(act_chain, 1)
                act.wait_ge(act_chain, ch.next())
                activate(lat_sd[:, :], lat_ms[:, :], ACT.Sqrt, bias=eps[:, :]).then_inc(lat_sq, 1)
                win_splits(2)
                evac_chunk(1)
                win_splits(3)
                split_hi(act, l, POS_UKV)
                evac_chunk(2)
                split_hi(act, l, POS_UQ)
                for n in range(3):
                    act.wait_ge(lat_tp, at(lat_tp, l, n + 1))
                    activate(ht_hi[:, LAT + n, :], ps[:, n, :], ACT.Copy).then_inc(lat_hi, 1)
                act.wait_ge(lat_tp, at(lat_tp, l, 4))
                for n in range(4):
                    last = activate(ks[NOPE:P, 2 * n, :], ps[0:2 * ROPE, 3, :], ACT.Copy)
                last.then_inc(lat_hi, 1)
                split_hi(act, l, POS_UQ + 1)
                evac_chunk(3)

                def q_hi(n):
                    act.wait_ge(qf_done, at(qf_done, l, n + 1))
                    activate(qs[:, 2 * (n % 4), :], qf[:, :], ACT.Copy).then_inc(qh_done, 1)

                def k_hi(n, bank):
                    act.wait_ge(qk_acc, at(qk_acc, l, 2 * n + 2))
                    i = 2 * (n % 4)
                    activate(ks[0:NOPE, i, :], ps[0:NOPE, bank, :], ACT.Copy).then_inc(kh_done, 1)

                for n in range(2):
                    q_hi(n)
                    k_hi(n, 2 * n + 1)
                for n in range(T):
                    t = T - 1 - n
                    act.wait_ge(v_acc, at(v_acc, l, n + 1))
                    activate(vm[:, t, :], ps[:, 4 + t, :], ACT.Copy).then_inc(v_ready, 1)

                def exps(u):
                    i, _ = unit(u)
                    n = (i + 1) * P
                    act.wait_ge(max_done, at(max_done, l, u + 1))
                    if u >= 2:
                        act.wait_ge(t_done, at(t_done, l, u - 1))
                    sc = score_banks(u)
                    for s in range(2):
                        last = activate(probs[:, u % 2, s, 0:n], sc[:, s, :], ACT.Exp,
                                        bias=nmax[:, u % 4, s:s + 1], accum_out=rsum[:, u % 4, s:s + 1])
                    last.then_inc(exp_done, 1)

                def evac_pt(u):
                    i, _ = unit(u)
                    n = (i + 1) * P
                    act.wait_ge(t_done, at(t_done, l, u + 1))
                    if u >= 1:
                        act.wait_ge(pv_done, at(pv_done, l, u))
                    activate(probs_t[:, :, 0:n], ps[:, 4:6, 0:n], ACT.Copy).then_inc(pt_done, 1)

                def evac_out(pair, bank):
                    done = T * (pair + 1) if pair < H // 2 else U_MLA + 2 * T * (pair - H // 2 + 1)
                    act.wait_ge(pv_done, at(pv_done, l, done))
                    activate(ht_hi[:, pair, :], ps[:, bank, :], ACT.Copy).then_inc(oh_done, 1)

                def item_hi(n):
                    kind, i = ITEMS[n]
                    act.wait_ge(it_tp, at(it_tp, l, n + 1))
                    for e in range(2):
                        own = halves(e)[0]
                        if kind == "k":
                            for half in halves(0):
                                ins = activate(ks[half, 2 * (2 * i + e), :], ps[own, 7, :], ACT.Copy)
                        elif kind == "q":
                            ins = activate(qs[own, 2 * i + e, :], ps[own, 7, :], ACT.Copy, scale=HD ** -0.5)
                        else:
                            tok = ps[own, 7, :].rearrange("p (c m two) -> p two m c", two=2, m=MT // 2)
                            for part in range(2):
                                ins = activate(kst[i][0:HD, part * MT // 2:(part + 1) * MT // 2, e * NC:(e + 1) * NC],
                                               tok[:, 0, :, part:part + NC], ACT.Copy)
                    ins.then_inc(it_act, 1)

                for s in range(U + 3):
                    if 0 <= s - 2 < U:
                        evac_pt(s - 2)
                    if s < U:
                        exps(s)
                    if s < PRE:
                        n = s // 2 + 2
                        if s % 2 == 0:
                            q_hi(n)
                        else:
                            k_hi(n, 7)
                    if s == 2:
                        act.wait_ge(gate_in, at(gate_in, l, 1))
                        activate(gates[:, :, :], gate_e[:, :, :], ACT.Exp, scale=-1.0).then_inc(gate_exp, 1)
                    if s == PRE:
                        item_hi(0)
                        item_hi(1)
                    if s == PRE + 1:
                        item_hi(2)
                        item_hi(3)
                    if s == PRE + 2:
                        item_hi(4)
                    if s == PRE + 3:
                        act.wait_ge(cmp_used, at(cmp_used, l, 4))
                        activate(hid_rows, ps[0:CMP_COLS, 7, 0:2 * CHID].rearrange("p (a n) -> p a n", a=2), ACT.Copy)                            .then_inc(hid_out, 1)
                    if s == PRE + 4:
                        act.wait_ge(hb_done, at(hb_done, l, 1))
                        for kv in range(2):
                            c = 2 * CHID + kv * CMP_COLS
                            last = activate(hid[:, kv, :, 0:NC],
                                            ps[:, 7, c:c + G * NC].rearrange("p (g c) -> p g c", g=G),
                                            ACT.Gelu_apprx_tanh, bias=hid_b[:, kv:kv + 1])
                        last.then_inc(hid_ready, 1)
                        act.wait_ge(kvc_acc, at(kvc_acc, l, 1))
                        act.wait_ge(kcz_ready, at(kcz_ready, l, 1))
                        activate(kc_hi[:, :, :], ps[:, 7, S - G * NCP:S].rearrange("p (g c) -> p g c", g=G), ACT.Copy)                            .then_inc(kch_done, 1)
                    if s == PRE + 5:
                        item_hi(5)
                        item_hi(6)
                    if s == PRE + 6:
                        item_hi(7)
                    if PRE + 7 <= s < PRE + 7 + G:
                        g = s - PRE - 7
                        act.wait_ge(cs_acc, at(cs_acc, l, g + 1))
                        activate(cs_t[:, g, :], ps[:, 7, :], ACT.Copy).then_inc(cs_out, 1)
                    if s == PRE + 10:
                        act.wait_ge(cs_sub, at(cs_sub, l, 1))
                        activate(scp, scp, ACT.Exp).then_inc(cs_exp, 1)
                    if PRE + 12 <= s < PRE + 12 + G:
                        g = s - PRE - 12
                        act.wait_ge(pc_tp, at(pc_tp, l, g + 1))
                        activate(cs_t[:, g, :], ps[:, 7, :], ACT.Copy).then_inc(pct_ready, 1)
                    if 3 <= s < U_MLA + 3 and (s - 3) % T == T - 1:
                        evac_out((s - 3) // T, 6)
                    if s - 3 >= U_MLA and (s - 3 - U_MLA) % (2 * T) == 2 * T - 1:
                        pair = (s - 3 - U_MLA) // (2 * T)
                        evac_out(H // 2 + pair, 6 + pair % 2)
                    if s == U_MLA + 4 * T:
                        for k in range(SLOTS):
                            split_hi(act, l, POS_WOUT + k)
                for k in range(SLOTS, KD):
                    split_hi(act, l, POS_WOUT + k)
                norm_stats(l, 1, 0)
                norm_stats(l, 1, 1)
                norm_hi(l, 1, 0)
                norm_stats(l, 1, 2)
                norm_hi(l, 1, 1)
                split_hi(act, l, POS_UP)
                norm_stats(l, 1, 3)
                norm_hi(l, 1, 2)
                split_hi(act, l, POS_UP + 1)
                norm_hi(l, 1, 3)
                split_hi(act, l, POS_UP + 2)
                split_hi(act, l, POS_UP + 3)

                def up_tail(f, fl, pos_turn):
                    for uv in range(2):
                        act.wait_ge(split_used, used(l, POS_UP + 2 * fl + uv, pos_turn))
                        tap = cols[:, bass.ds(C_TAP + 2 * 2 * FT + f + uv * FT, 1)]
                        bias = cols[:, bass.ds(C_CB + f + uv * FT, 1)]
                        activate(conv[:, fl, uv, :], ps[:, 4 * fl + uv, :], ACT.Identity, bias=bias, scale=tap)\
                            .then_inc(t0_done, 1)
                    act.wait_ge(conv_done, at(conv_done, l, pos_turn // 2 + fl + 1))
                    activate(silu[:, fl, :], conv[:, fl, 0, :], ACT.Silu).then_inc(silu_done, 1)

                with act.Fori(0, FT // 2 - 1) as j:
                    for e in range(2):
                        up_tail(2 * j + e, e, 4 * j)
                        for uv in range(2):
                            p = 2 * e + uv
                            split_hi(act, l, POS_UP + SLOTS + p, SLOTS * j, j)

                def g_split_hi(k, n, turn=0):
                    act.wait_ge(g_done, at(g_done, l, min(n + 1, FT) + turn))
                    if n >= 2:
                        act.wait_ge(split_used, used(l, POS_DOWN + n - 2, turn))
                    activate(g_hi[:, n % 2, :].unsqueeze(1), g_all[:, bass.ds(k, 1), :], ACT.Copy)\
                        .then_inc(gh_done, 1)

                for e in range(2):
                    g_split_hi(e, e)
                for e in range(2):
                    up_tail(FT - 2 + e, e, 2 * (FT - 2))
                    for uv in range(2):
                        split_hi(act, l, POS_DOWN + 2 * e + uv)
                for n in range(SLOTS):
                    g_split_hi(n + 2, n + 2)
                    split_hi(act, l, POS_DOWN + SLOTS + n)
                with act.Fori(0, DOWN_TURNS) as j:
                    for e in range(SLOTS):
                        g_split_hi(SLOTS * j + SLOTS + e + 2, SLOTS + e + 2, SLOTS * j)
                        split_hi(act, l, POS_DOWN + 2 * SLOTS + e, SLOTS * j, j)
                for n in range(SLOTS * (DOWN_TURNS + 1), FT - 2):
                    g_split_hi(n + 2, n + 2)
                    if n + SLOTS < FT:
                        split_hi(act, l, POS_DOWN + n + SLOTS)
                ch.end_layer("act")

            for t in range(T):
                act.wait_ge(x_done, at(x_done, L, t + 1 - T))
                ins = activate(ps[:, 2 * t:2 * t + 2, :], x[:, t, :].rearrange("p (a n) -> p a n", a=2), ACT.Square,
                               scale=D ** -0.5, accum_out=ms[:, t:t + 1])
                ins.then_inc(act_chain, 1)
                act.wait_ge(act_chain, L * ch.per_layer + t + 1)
                activate(sd[:, t:t + 1], ms[:, t:t + 1], ACT.Sqrt, bias=eps[:, :]).then_inc(sd_done, 1)

        @block.vector
        def _(dve):
            ch = Steps(0)
            v = nc.vector
            tt, stt = v.tensor_tensor, v.scalar_tensor_tensor
            ch.per_layer = 2 * T + 3 + U_MLA + 2 * U_NSA + 5 + FT
            dve.wait_ge(const_loaded, 16 * len(consts))
            v.tensor_copy(ident_b[:, :], ident[:, :]).then_inc(const_ready, 1)
            v.tensor_copy(causal_b[:, :], causal[:, :]).then_inc(const_ready, 1)
            v.memset(hid[:, :, :, :], 0.0).then_inc(const_ready, 1)
            v.memset(eps[:, :], EPS).then_inc(const_ready, 1)
            dve.wait_ge(x_loaded, 16 * T)
            dve.sem_inc(x_done, CREDIT["x_done"])
            dve.sem_inc(lo_done, CREDIT["lo_done"])
            dve.sem_inc(hn_done, CREDIT["hn_done"])

            def norm_rows(l, w, t, final=False):
                dve.wait_ge(sd_done, at(sd_done, l, w * T + t + 1))
                v.reciprocal(rstd[:, t:t + 1], sd[:, t:t + 1]).then_inc(dve_chain, 1)
                dve.wait_ge(dve_chain, ch.next())
                if t == 0:
                    dve.wait_ge(g_loaded, (l * 2 + w + 1) * 16)
                if t >= 2:
                    if final:
                        dve.wait_ge(out_done[t % 2], 16 * (t // 2))
                    else:
                        dve.wait_ge(tp_done, at(tp_done, l, 2 * (w * T + t - 2) + 2))
                stt(out=hn[:, t % 2, :], in0=x[:, t, :], scalar=rstd[:, t:t + 1], in1=norm_g[:, :], op0=ALU.mult,
                    op1=ALU.mult).then_inc(hn_done, 1)

            def norm_lo(l, w, t):
                for b in range(2):
                    dve.wait_ge(hh_done, at(hh_done, l, 2 * (w * T + t) + b + 1))
                    r = (slice(None), slice(4 * b, 4 * b + 4), slice(t * P, (t + 1) * P))
                    tt(ht_lo[r], ps[:, 2 * t + b, :].rearrange("p (k n) -> p k n", k=4), ht_hi[r].bitcast(F32),
                       ALU.subtract).then_inc(hl_done, 1)

            def add_x(l, w, t):
                if t < T - 1:
                    dve.wait_ge(out_acc, at(out_acc, l, w * (T - 1) + t + 1))
                else:
                    dve.wait_ge(split_used, used(l, (POS_UP if w == 0 else POS_END) - 1))
                xt = x[:, t, :].rearrange("p (a n) -> p a n", a=2)
                tt(xt, xt, ps[:, 2 * t:2 * t + 2, :], ALU.add).then_inc(x_done, 1)

            with dve.Fori(0, L) as l:
                ch.layer(l)
                norm_rows(l, 0, 0)
                split_lo(dve, l, POS_WIN)
                norm_rows(l, 0, 1)
                norm_lo(l, 0, 0)
                split_lo(dve, l, POS_WIN + 1)
                split_lo(dve, l, POS_WIN + 2)
                norm_rows(l, 0, 2)
                norm_lo(l, 0, 1)
                split_lo(dve, l, POS_WIN + 3)
                norm_rows(l, 0, 3)
                norm_lo(l, 0, 2)
                norm_lo(l, 0, 3)

                def evac_chunk(c):
                    for t in range(1, T, 2):
                        if t < T - 1:
                            dve.wait_ge(win_acc, at(win_acc, l, c * (T - 1) + t + 1))
                        else:
                            dve.wait_ge(split_used, used(l, POS_WIN + (c + 1) * KD // 2 - 1))
                        v.tensor_copy(proj[:, t, c * CW:(c + 1) * CW], ps[:, 4 * (c % 2) + t, 0:CW])\
                            .then_inc(pj_dve, 1)

                def win_splits(c):
                    for kp in range(KD // 2):
                        split_lo(dve, l, POS_WIN + c * KD // 2 + kp)

                win_splits(1)
                evac_chunk(0)
                dve.wait_ge(pj_act, at(pj_act, l, T // 2))
                dve.wait_ge(pj_dve, at(pj_dve, l, T // 2))
                kp = proj[:, :, QR + KVR:COL_Q]
                rc = rope[:, :, 2 * ROT:2 * ROT + ROPE]
                rs = rope[:, :, 2 * ROT + ROPE:].rearrange("p t (a b) -> p t a b", a=2)
                dve.wait_ge(small_loaded, (l + 1) * 16 * SMALL)
                tt(kpe_t[:, 0, :, :], kp, rc, ALU.mult)
                tt(kpe_t[:, 1, :, :].rearrange("p t (a b) -> p t a b", a=2),
                           kp.rearrange("p t (a b) -> p t a b", a=2)[:, :, ::-1, :], rs, ALU.mult).then_inc(dve_chain, 1)
                dve.wait_ge(dve_chain, ch.next())
                twice = lambda n: kpe_t[:, n, :, :].unsqueeze(2).broadcast_to([P, T, 2, ROPE])
                tt(kpe_r[:, :, :, :], twice(0), twice(1), ALU.add).then_inc(kpe_ready, 1)
                dve.wait_ge(lat_sq, at(lat_sq, l, 1))
                v.reciprocal(lat_rstd[:, :], lat_sd[:, :]).then_inc(dve_chain, 1)
                dve.wait_ge(dve_chain, ch.next())
                for t in range(T):
                    stt(out=proj[:, t, 0:QR], in0=proj[:, t, 0:QR], scalar=lat_rstd[:, 2 * t:2 * t + 1],
                        in1=lat_g[:, 0:QR], op0=ALU.mult, op1=ALU.mult)
                    last = stt(out=proj[:, t, QR:QR + KVR], in0=proj[:, t, QR:QR + KVR],
                               scalar=lat_rstd[:, 2 * t + 1:2 * t + 2], in1=lat_g[:, QR:QR + KVR], op0=ALU.mult,
                               op1=ALU.mult)
                last.then_inc(lat_ready, 1)
                win_splits(2)
                evac_chunk(1)
                dve.wait_ge(cols_tp, at(cols_tp, l, 1))
                v.tensor_copy(cols[:, :], ps[:, 4, 0:C_END]).then_inc(cols_ready, 1)
                win_splits(3)
                split_lo(dve, l, POS_UKV)
                evac_chunk(2)
                split_lo(dve, l, POS_UQ)
                for n in range(3):
                    dve.wait_ge(lat_hi, at(lat_hi, l, n + 1))
                    tt(ht_lo[:, LAT + n, :], ps[:, n, :], ht_hi[:, LAT + n, :].bitcast(F32), ALU.subtract)\
                        .then_inc(lat_lo, 1)
                dve.wait_ge(lat_hi, at(lat_hi, l, 4))
                for n in range(4):
                    last = tt(ks[NOPE:P, 2 * n + 1, :], ps[0:2 * ROPE, 3, :], ks[NOPE:P, 2 * n, :].bitcast(F32),
                              ALU.subtract)
                last.then_inc(kpe_lo, 1)
                split_lo(dve, l, POS_UQ + 1)
                evac_chunk(3)

                def q_rows(n, bank):
                    dve.wait_ge(qk_acc, at(qk_acc, l, 2 * n + 1))
                    if n >= 1:
                        dve.wait_ge(q_ready, at(q_ready, l, n))
                    tt(qf[:, :], ps[:, bank, :], table[:, :], ALU.mult).then_inc(qf_done, 1)

                def q_lo(n):
                    dve.wait_ge(qh_done, at(qh_done, l, n + 1))
                    i = 2 * (n % 4)
                    tt(qs[:, i + 1, :], qf[:, :], qs[:, i, :].bitcast(F32), ALU.subtract).then_inc(q_ready, 1)

                def k_lo(n, bank):
                    dve.wait_ge(kh_done, at(kh_done, l, n + 1))
                    i = 2 * (n % 4)
                    tt(ks[0:NOPE, i + 1, :], ps[0:NOPE, bank, :], ks[0:NOPE, i, :].bitcast(F32), ALU.subtract)\
                        .then_inc(kl_done, 1)

                for n in range(2):
                    q_rows(n, 2 * n)
                    q_lo(n)
                    k_lo(n, 2 * n + 1)

                def row_max(u):
                    i, _ = unit(u)
                    n = (i + 1) * P
                    dve.wait_ge(sc_done, at(sc_done, l, u + 1))
                    v.tensor_reduce(nmax[:, u % 4, :], score_banks(u), AX, ALU.max, negate=True)\
                        .then_inc(max_done, 1)

                def scale_probs(u):
                    i, _ = unit(u)
                    n = (i + 1) * P
                    dve.wait_ge(exp_done, at(exp_done, l, u + 1))
                    v.reciprocal(rinv[:, u % 4, :], rsum[:, u % 4, :]).then_inc(dve_chain, 1)
                    dve.wait_ge(dve_chain, ch.next())
                    r = rinv
                    if u >= U_MLA:
                        h = (u - U_MLA) // T
                        tt(rgate[:, u % 4, :], rinv[:, u % 4, :], gates[:, i, BR * h + 1:BR * h + 3],
                           ALU.mult).then_inc(dve_chain, 1)
                        dve.wait_ge(dve_chain, ch.next())
                        r = rgate
                    for s in range(2):
                        last = v.tensor_scalar(probs[:, u % 2, s, 0:n], probs[:, u % 2, s, 0:n],
                                               r[:, u % 4, s:s + 1], None, ALU.mult)
                    last.then_inc(p_done, 1)

                def out_lo(pair, bank):
                    dve.wait_ge(oh_done, at(oh_done, l, pair + 1))
                    tt(ht_lo[:, pair, :], ps[:, bank, :], ht_hi[:, pair, :].bitcast(F32), ALU.subtract)\
                        .then_inc(ol_done, 1)

                def item_lo(n):
                    kind, i = ITEMS[n]
                    dve.wait_ge(it_act, at(it_act, l, n + 1))
                    for e in range(2):
                        own, other = halves(e)
                        if kind == "k":
                            c = 2 * (2 * i + e)
                            for half in halves(0):
                                ins = tt(ks[half, c + 1, :], ps[own, 7, :], ks[own, c, :].bitcast(F32), ALU.subtract)
                        elif kind == "q":
                            ins = stt(out=qs[other, 2 * i + e, :], in0=ps[own, 7, :], scalar=HD ** -0.5,
                                      in1=qs[own, 2 * i + e, :].bitcast(F32), op0=ALU.mult, op1=ALU.subtract)
                        else:
                            tok = ps[own, 7, :].rearrange("p (c m two) -> p two m c", two=2, m=MT // 2)
                            for part in range(2):
                                ins = v.tensor_copy(kst[i][HD:P, part * MT // 2:(part + 1) * MT // 2,
                                                           e * NC:(e + 1) * NC], tok[:, 1, :, part:part + NC])
                    ins.then_inc(it_dve, 1)

                sc3 = scp.rearrange("p t h c -> p (t h) c")
                st = lambda n: cstat[:, n, :, :].rearrange("p t h -> p (t h)")
                wide = lambda n: st(n).unsqueeze(2).broadcast_to([P, T * H, NCP])

                def cs_mask(b):
                    t2 = slice(b * T // 2, (b + 1) * T // 2)
                    dve.wait_ge(cs_back, at(cs_back, l, b + 1))
                    tt(scp[:, t2, :, :], ps[:, 7, :].rearrange("p (t h c) -> p t h c", t=T // 2, h=H),
                       cmask[:, t2, :].unsqueeze(2).broadcast_to([P, T // 2, H, NCP]), ALU.add).then_inc(cs_in, 1)

                def cs_less_max():
                    dve.wait_ge(cs_in, at(cs_in, l, 2))
                    v.tensor_reduce(st(0), sc3, AX, ALU.max).then_inc(dve_chain, 1)
                    dve.wait_ge(dve_chain, ch.next())
                    tt(sc3, sc3, wide(0), ALU.subtract).then_inc(cs_sub, 1)

                def cs_scale():
                    dve.wait_ge(cs_exp, at(cs_exp, l, 1))
                    v.tensor_reduce(st(1), sc3, AX, ALU.add).then_inc(dve_chain, 1)
                    dve.wait_ge(dve_chain, ch.next())
                    v.reciprocal(st(2), st(1)).then_inc(dve_chain, 1)
                    dve.wait_ge(dve_chain, ch.next())
                    tt(cstat[:, 0, :, :], cstat[:, 2, :, :], gates[:, :, 0:H * BR:BR], ALU.mult).then_inc(dve_chain, 1)
                    dve.wait_ge(dve_chain, ch.next())
                    tt(cstat[:, 1, :, :], cstat[:, 0, :, :],
                       rowok[:, :].unsqueeze(2).broadcast_to([P, T, H]), ALU.mult).then_inc(dve_chain, 1)
                    dve.wait_ge(dve_chain, ch.next())
                    tt(sc3, sc3, wide(1), ALU.mult).then_inc(pc_done, 1)

                for s in range(U + 3):
                    if s < U:
                        row_max(s)
                    if 0 <= s - 1 < U:
                        scale_probs(s - 1)
                    if s < PRE:
                        n = s // 2 + 2
                        if s % 2 == 0:
                            q_rows(n, 7)
                        else:
                            q_lo(n)
                            k_lo(n, 7)
                    if s == 3:
                        dve.wait_ge(gate_exp, at(gate_exp, l, 1))
                        v.tensor_scalar(gates[:, :, :], gates[:, :, :], 1.0, None, ALU.add).then_inc(dve_chain, 1)
                        dve.wait_ge(dve_chain, ch.next())
                        v.reciprocal(gates[:, :, :], gates[:, :, :]).then_inc(gates_ready, 1)
                    if s == PRE:
                        item_lo(0)
                        item_lo(1)
                    if s == PRE + 1:
                        item_lo(2)
                        item_lo(3)
                    if s == PRE + 2:
                        item_lo(4)
                    if s == PRE + 4:
                        dve.wait_ge(hid_tp, at(hid_tp, l, 1))
                        pos = ps[:, 7, 2 * CHID:2 * CHID + 2 * CMP_COLS].rearrange("p (a c) -> p a c", a=2)[:, :, 2 * NC]
                        tt(hid_b[:, :], pos, cols[:, C_B1:C_B1 + 2], ALU.add).then_inc(hb_done, 1)
                        dve.wait_ge(kch_done, at(kch_done, l, 1))
                        tt(kc_lo[:, :, :], ps[:, 7, S - G * NCP:S].rearrange("p (g c) -> p g c", g=G),
                           kc_hi[:, :, :].bitcast(F32), ALU.subtract)
                        v.tensor_copy(v_cmp[:, :, :], ps[:, 7, 0:G * HD].rearrange("p (g c) -> p g c", g=G))\
                            .then_inc(kvc_ready, 1)
                    if s == PRE + 5:
                        item_lo(5)
                        item_lo(6)
                    if s == PRE + 6:
                        item_lo(7)
                    if s == PRE + 9:
                        cs_mask(0)
                        cs_mask(1)
                    if s == PRE + 10:
                        cs_less_max()
                    if s == PRE + 11:
                        cs_scale()
                    if 3 <= s < U_MLA + 3 and (s - 3) % T == T - 1:
                        out_lo((s - 3) // T, 6)
                    if s - 3 >= U_MLA and (s - 3 - U_MLA) % (2 * T) == 2 * T - 1:
                        pair = (s - 3 - U_MLA) // (2 * T)
                        out_lo(H // 2 + pair, 6 + pair % 2)
                    if s == U_MLA + 4 * T + 1:
                        for k in range(SLOTS):
                            split_lo(dve, l, POS_WOUT + k)
                for k in range(SLOTS, KD):
                    split_lo(dve, l, POS_WOUT + k)
                add_x(l, 0, 0)
                norm_rows(l, 1, 0)
                add_x(l, 0, 1)
                norm_rows(l, 1, 1)
                norm_lo(l, 1, 0)
                add_x(l, 0, 2)
                norm_rows(l, 1, 2)
                norm_lo(l, 1, 1)
                split_lo(dve, l, POS_UP)
                add_x(l, 0, 3)
                norm_rows(l, 1, 3)
                norm_lo(l, 1, 2)
                split_lo(dve, l, POS_UP + 1)
                norm_lo(l, 1, 3)
                split_lo(dve, l, POS_UP + 2)
                split_lo(dve, l, POS_UP + 3)

                def up_tail(f, fl, turn):
                    for tap in (1, 0):
                        for uv in range(2):
                            if tap == 1:
                                dve.wait_ge(t0_done, at(t0_done, l, turn + 2 * fl + uv + 1))
                            back = TAPS - 1 - tap
                            c = cols[:, bass.ds(C_TAP + tap * 2 * FT + f + uv * FT, 1)]
                            ins = stt(out=conv[:, fl, uv, back:S], in0=ps[:, 4 * fl + uv, 0:S - back], scalar=c,
                                      in1=conv[:, fl, uv, back:S], op0=ALU.mult, op1=ALU.add)
                        if tap == 1:
                            ins.then_inc(dve_chain, 1)
                            dve.wait_ge(dve_chain, ch.next())
                    ins.then_inc(conv_done, 1)
                    dve.wait_ge(silu_done, at(silu_done, l, turn // 2 + fl + 1))
                    dve.wait_ge(conv_done, at(conv_done, l, turn // 2 + fl + 1))
                    tt(g_all[:, bass.ds(f, 1), :], silu[:, fl, :].unsqueeze(1), conv[:, fl, 1, :].unsqueeze(1),
                       ALU.mult).then_inc(g_done, 1)

                with dve.Fori(0, FT // 2 - 1) as j:
                    ch.loop(j, 2)
                    for e in range(2):
                        up_tail(2 * j + e, e, 4 * j)
                        for uv in range(2):
                            split_lo(dve, l, POS_UP + SLOTS + 2 * e + uv, SLOTS * j)
                    ch.end_loop(FT // 2 - 1, 2)

                def g_split_lo(k, n, turn=0):
                    dve.wait_ge(gh_done, at(gh_done, l, n + 1 + turn))
                    tt(g_lo[:, n % 2, :].unsqueeze(1), g_all[:, bass.ds(k, 1), :],
                       g_hi[:, n % 2, :].unsqueeze(1).bitcast(F32), ALU.subtract).then_inc(gl_done, 1)

                for e in range(2):
                    g_split_lo(e, e)
                for e in range(2):
                    up_tail(FT - 2 + e, e, 2 * (FT - 2))
                    for uv in range(2):
                        split_lo(dve, l, POS_DOWN + 2 * e + uv)
                for n in range(SLOTS):
                    g_split_lo(n + 2, n + 2)
                    split_lo(dve, l, POS_DOWN + SLOTS + n)
                with dve.Fori(0, DOWN_TURNS) as j:
                    for e in range(SLOTS):
                        g_split_lo(SLOTS * j + SLOTS + e + 2, SLOTS + e + 2, SLOTS * j)
                        split_lo(dve, l, POS_DOWN + 2 * SLOTS + e, SLOTS * j)
                for n in range(SLOTS * (DOWN_TURNS + 1), FT - 2):
                    g_split_lo(n + 2, n + 2)
                    if n + SLOTS < FT:
                        split_lo(dve, l, POS_DOWN + n + SLOTS)
                for t in range(T):
                    add_x(l, 1, t)

                ch.end_layer("dve")

            ch.layer(L)
            for t in range(T):
                norm_rows(L, 0, t, final=True)

        @block.tensor
        def _(pe):
            mm = nc.tensor.matmul

            def mm3(o, lhs, rhs, start, stop):
                mm(o, lhs[0], rhs[0], start=start, stop=False)
                mm(o, lhs[0], rhs[1], start=False, stop=False)
                return mm(o, lhs[1], rhs[0], start=False, stop=stop)

            pe.wait_ge(const_ready, 4)
            pe.sem_inc(split_used, CREDIT["split_used"])

            def norm_transpose(l, w, t):
                pe.wait_ge(hn_done, at(hn_done, l, w * T + t + 1))
                for b in range(2):
                    for k in range(4):
                        last = nc.tensor.transpose(ps[:, 2 * t + b, k * P:(k + 1) * P],
                                                   hn[:, t % 2, (4 * b + k) * P:(4 * b + k + 1) * P], ident[:, :])
                    last.then_inc(tp_done, 1)

            with pe.Fori(0, L) as l:
                def win_first(t):
                    pe.wait_ge(hl_done, at(hl_done, l, 2 * t + 2))
                    tk = slice(t * P, (t + 1) * P)
                    for kp in range(KD // 2):
                        if t == 0:
                            pe.wait_ge(lo_done, split(l, POS_WIN + kp))
                        w = [wslot(b, POS_WIN + kp, [2, CW]) for b in (w_hi, w_lo)]
                        for kk in range(2):
                            k = 2 * kp + kk
                            last = mm3(ps[:, t, 0:CW], [ht_hi[:, k, tk], ht_lo[:, k, tk]],
                                       [w[0][:, kk, :], w[1][:, kk, :]], k == 0, k == KD - 1)
                        if t == T - 1:
                            last.then_inc(split_used, 1)
                    if t < T - 1:
                        last.then_inc(win_acc, 1)

                norm_transpose(l, 0, 0)
                norm_transpose(l, 0, 1)
                for t in range(T):
                    win_first(t)
                    if t + 2 < T:
                        norm_transpose(l, 0, t + 2)

                def win_piece(c, n):
                    pos = POS_WIN + c * KD // 2 + n
                    kp = KP_LAST[n] if c == CH - 1 else n
                    pe.wait_ge(lo_done, split(l, pos))
                    w = [wslot(b, pos, [2, CW]) for b in (w_hi, w_lo)]
                    for kk in range(2):
                        k = 2 * kp + kk
                        first, final = n + kk == 0, n == KD // 2 - 1 and kk == 1
                        for t in range(T):
                            if first and c >= 2:
                                pe.wait_ge(pj[t % 2], at(pj[t % 2], l, (c - 2) * T // 2 + t // 2 + 1))
                            tk = slice(t * P, (t + 1) * P)
                            last = mm3(ps[:, 4 * (c % 2) + t, 0:CW], [ht_hi[:, k, tk], ht_lo[:, k, tk]],
                                       [w[0][:, kk, :], w[1][:, kk, :]], first, final)
                            if final and t < T - 1:
                                last.then_inc(win_acc, 1)
                    last.then_inc(split_used, 1)

                for n in range(KD // 2):
                    win_piece(1, n)
                pe.wait_ge(pj_act, at(pj_act, l, T // 2 + 1))
                pe.wait_ge(small_loaded, (l + 1) * 16 * SMALL)
                settle(pe)
                for n in range(TAPS + 1):
                    nc.tensor.transpose(ps[:, 4, n * 2 * FT:(n + 1) * 2 * FT], rows[0:2 * FT, n, :],
                                        ident[0:2 * FT, 0:2 * FT])
                nc.tensor.transpose(ps[:, 4, C_POS:C_POS + 2 * MT], rows[0:2 * MT, TAPS + 1, :],
                                    ident[0:2 * MT, 0:2 * MT])
                nc.tensor.transpose(ps[:, 4, C_B1:C_B1 + 2], rows[0:2, TAPS + 2, :], ident[0:2, 0:2])\
                    .then_inc(cols_tp, 1)
                for n in range(KD // 2):
                    win_piece(2, n)
                pe.wait_ge(cols_ready, at(cols_ready, l, 1))
                win_piece(3, 0)
                win_piece(3, 1)
                pe.wait_ge(lat_ready, at(lat_ready, l, 1))
                pe.wait_ge(kpe_ready, at(kpe_ready, l, 1))
                for n in range(3):
                    pe.wait_ge(pj[n % 2], at(pj[n % 2], l, 2 * T // 2 + n // 2 + 1))
                    c = (QR, 0, P)[n]
                    for t in range(T):
                        last = nc.tensor.transpose(ps[:, n, t * P:(t + 1) * P], proj[:, t, c:c + P], ident[:, :])
                    last.then_inc(lat_tp, 1)
                pe.wait_ge(pj_dve, at(pj_dve, l, 3 * T // 2))
                settle(pe)
                for t in range(T):
                    last = nc.tensor.transpose(ps[0:2 * ROPE, 3, t * P:(t + 1) * P],
                                               kpe_r[:, t, :, :].rearrange("p a b -> p (a b)"), ident[:, :])
                last.then_inc(lat_tp, 1)
                win_piece(3, 2)
                win_piece(3, 3)

                ukv = [b[:, POS_UKV % SLOTS, :].rearrange("p (h c) -> p h c", h=H) for b in (w_hi, w_lo)]
                uq = [[b[:, (POS_UQ + k) % SLOTS, :].rearrange("p (h c) -> p h c", h=H) for b in (w_hi, w_lo)]
                      for k in range(2)]
                lat = lambda n, c: [ht_hi[:, LAT + n, c], ht_lo[:, LAT + n, c]]
                every = slice(0, S)

                def qk_item(j, bank):
                    h = j // 2
                    if j % 2 == 0:
                        for k in range(2):
                            last = mm3(ps[:, bank, :], [uq[k][0][:, h, :], uq[k][1][:, h, :]], lat(1 + k, every),
                                       k == 0, k == 1)
                    else:
                        last = mm3(ps[:, bank, :], [ukv[0][:, h, :], ukv[1][:, h, :]], lat(0, every), True, True)
                    last.then_inc(qk_acc, 1)

                pe.wait_ge(lo_done, split(l, POS_UQ + 1))
                pe.wait_ge(lat_lo, at(lat_lo, l, 3))
                pe.wait_ge(kpe_lo, at(kpe_lo, l, 1))
                for j in range(4):
                    qk_item(j, j)
                for n in range(T):
                    t = T - 1 - n
                    pe.wait_ge(pj[t % 2], at(pj[t % 2], l, 3 * T // 2 + t // 2 + 1))
                    mm3(ps[:, 4 + t, :].rearrange("p (h c) -> p h c", h=H), lat(0, slice(t * P, (t + 1) * P)),
                        [w[:, :, NOPE:2 * NOPE] for w in ukv], True, True).then_inc(v_acc, 1)

                def scores(u):
                    i, pair = unit(u)
                    n = (i + 1) * P
                    qt = slice(i * P, (i + 1) * P)
                    if u >= 2:
                        pe.wait_ge(exp_done, at(exp_done, l, u - 1))
                    sc = score_banks(u)
                    if u < U_MLA:
                        for s in range(2):
                            c = 4 * (pair % 2) + 2 * s
                            mm3(sc[:, s, :], [qs[:, c, qt], qs[:, c + 1, qt]], [ks[:, c, 0:n], ks[:, c + 1, 0:n]],
                                True, False)
                            last = mm(sc[:, s, n - P:n], ident_b[:, :], causal_b[:, :], start=False, stop=True)
                    else:
                        h = (u - U_MLA) // T
                        c = 4 * (h // GROUP)
                        if 2 * n <= S:
                            mm(sc, qs[:, h, qt], ks[:, c:c + 4:2, 0:n], start=True, stop=False)
                            mm(sc, qs[:, h, qt], ks[:, c + 1:c + 4:2, 0:n], start=False, stop=False)
                            last = mm(sc[:, :, n - P:n], ident_b[:, :],
                                      causal_b[:, :].unsqueeze(1).broadcast_to([P, 2, P]), start=False, stop=True)
                        else:
                            for s in range(2):
                                mm(sc[:, s, :], qs[:, h, qt], ks[:, c + 2 * s, 0:n], start=True, stop=False)
                                mm(sc[:, s, :], qs[:, h, qt], ks[:, c + 2 * s + 1, 0:n], start=False, stop=False)
                                last = mm(sc[:, s, n - P:n], ident_b[:, :], causal_b[:, :], start=False, stop=True)
                    last.then_inc(sc_done, 1)

                def turn(u):
                    i, _ = unit(u)
                    pe.wait_ge(p_done, at(p_done, l, u + 1))
                    if u >= 1:
                        pe.wait_ge(pt_done, at(pt_done, l, u))
                    for s in range(2):
                        for b in range(i + 1):
                            last = nc.tensor.transpose(ps[:, 4 + s, b * P:(b + 1) * P],
                                                       probs[:, u % 2, s, b * P:(b + 1) * P], ident[:, :])
                    last.then_inc(t_done, 1)

                def values(u):
                    i, pair = unit(u)
                    qt = slice(i * P, (i + 1) * P)
                    pe.wait_ge(pt_done, at(pt_done, l, u + 1))
                    if u < U_MLA:
                        if i == 0 and pair > 0:
                            pe.wait_ge(ol_done, at(ol_done, l, pair))
                        for s in range(2):
                            o = ps[64 * s:64 * s + VD, 6, qt]
                            for b in range(i + 1):
                                last = mm(o, vm[:, b, (2 * pair + s) * VD:(2 * pair + s + 1) * VD],
                                          probs_t[:, s, b * P:(b + 1) * P], start=b == 0, stop=b == i)
                    else:
                        h = (u - U_MLA) // T
                        g = h // GROUP
                        r = pair - H // 2
                        if i == 0 and h % 2 == 0:
                            if r >= 2:
                                pe.wait_ge(ol_done, at(ol_done, l, pair - 1))
                            elif r == 0:
                                pe.wait_ge(ol_done, at(ol_done, l, H // 2))
                            else:
                                pe.wait_ge(pct_ready, at(pct_ready, l, G))
                        closing = h % 2 == 1 and i == T - 1

                        def compressed(hh, stop):
                            m = NCP * (hh % GROUP)
                            return mm(ps[64 * (hh % 2):64 * (hh % 2) + HD, 6 + r % 2, :], v_cmp[m:m + NCP, g, :],
                                      cs_t[m:m + NCP, g, :], start=False, stop=stop)

                        if closing:
                            if r == 0:
                                pe.wait_ge(pct_ready, at(pct_ready, l, G))
                                settle(pe)
                            compressed(h - 1, True)
                        o = ps[64 * (h % 2):64 * (h % 2) + HD, 6 + r % 2, qt]
                        for s in range(2):
                            c = COL_KV + (s + 1) * 2 * G * HD + G * HD + g * HD
                            for b in range(i + 1):
                                last = mm(o, proj[:, b, c:c + HD], probs_t[:, s, b * P:(b + 1) * P],
                                          start=i + s + b == 0, stop=False)
                        if closing:
                            last = compressed(h, True)
                    last.then_inc(pv_done, 1)

                def item(n):
                    kind, i = ITEMS[n]
                    if n >= 1:
                        pe.wait_ge(it_act, at(it_act, l, n))
                        pe.wait_ge(it_dve, at(it_dve, l, n))
                    settle(pe)
                    for t in range(T):
                        if kind == "k":
                            c = [COL_KV + ((1 + e) * 2 * G + i) * HD for e in range(2)]
                            tk = slice(t * P, (t + 1) * P)
                            nc.tensor.transpose(ps[0:HD, 7, tk], proj[:, t, c[0]:c[0] + HD], ident[:, :])
                            last = mm(ps[HD:P, 7, tk], proj[:, t, c[1]:c[1] + HD], ident[:, :], start=True, stop=True)
                        else:
                            c = {"c": COL_KV + i * G * HD, "q": COL_Q + i * P}[kind]
                            last = nc.tensor.transpose(ps[:, 7, t * P:(t + 1) * P], proj[:, t, c:c + P], ident[:, :])
                    last.then_inc(it_tp, 1)

                def hidden(kv):
                    for half in range(2):
                        pos = POS_CMP + 2 * kv + half
                        pe.wait_ge(raw_loaded[pos % SLOTS], landed(l, pos))
                        w1 = wslot(raw, pos, [MT // 2, CHID])
                        for m in range(MT // 2):
                            mt = half * MT // 2 + m
                            last = mm(ps[0:CMP_COLS, 7, kv * CHID:(kv + 1) * CHID], kst[kv][:, mt, :], w1[:, m, :],
                                      start=mt == 0, stop=mt == MT - 1)
                        last.then_inc(cmp_used, 1)

                def scores_back(b):
                    for t in range(2 * b, 2 * b + 2):
                        for g in range(G):
                            c = (t % 2) * G * P + g * P
                            last = nc.tensor.transpose(ps[:, 7, c:c + P], cs_t[:, g, t * P:(t + 1) * P], ident[:, :])
                    last.then_inc(cs_back, 1)

                for s in range(U + 3):
                    if s < U_MLA and s % T == 0:
                        pe.wait_ge(q_ready, at(q_ready, l, 2 * (s // T) + 2))
                        pe.wait_ge(kl_done, at(kl_done, l, 2 * (s // T) + 2))
                    if s == U_MLA:
                        pe.wait_ge(it_dve, at(it_dve, l, 3))
                    if s == U_MLA + GROUP * T:
                        pe.wait_ge(it_dve, at(it_dve, l, NI))
                    if s < U:
                        scores(s)
                    if s < PRE:
                        j = s + 4
                        if s == 0:
                            pe.wait_ge(v_ready, at(v_ready, l, 1))
                        elif j % 2:
                            pe.wait_ge(qf_done, at(qf_done, l, (j - 1) // 2 + 1))
                        else:
                            pe.wait_ge(kl_done, at(kl_done, l, (j - 1) // 2 + 1))
                        qk_item(j, 7)
                    if s == 1:
                        pe.wait_ge(v_ready, at(v_ready, l, T))
                    if s == PRE:
                        pe.wait_ge(kl_done, at(kl_done, l, H))
                        pe.wait_ge(q_roped, at(q_roped, l, 1))
                        pe.wait_ge(k_roped, at(k_roped, l, 1))
                        item(0)
                    if s == PRE + 1:
                        item(2)
                    if s == PRE + 2:
                        item(4)
                    if s == PRE + 4:
                        pe.wait_ge(hid_out, at(hid_out, l, 1))
                        settle(pe)
                        for kv in range(2):
                            c = 2 * CHID + kv * CMP_COLS
                            last = nc.tensor.transpose(ps[:, 7, c:c + CMP_COLS], hid_rows[:, kv, :],
                                                       ident[0:CMP_COLS, 0:CMP_COLS])
                        last.then_inc(hid_tp, 1)
                    if s == PRE + 5:
                        pe.wait_ge(kvc_ready, at(kvc_ready, l, 1))
                        item(5)
                    if s == PRE + 6:
                        item(7)
                    if s == PRE + 9:
                        pe.wait_ge(cs_out, at(cs_out, l, G))
                        scores_back(0)
                    if 0 <= s - 3 < U:
                        values(s - 3)
                    if 0 <= s - 2 < U:
                        turn(s - 2)
                    if s == PRE:
                        item(1)
                    if s == PRE + 1:
                        item(3)
                    if s == PRE + 2:
                        pe.wait_ge(it_act, at(it_act, l, 5))
                        pe.wait_ge(it_dve, at(it_dve, l, 5))
                        pe.wait_ge(pos_ready, at(pos_ready, l, 1))
                        settle(pe)
                        hidden(0)
                    if s == PRE + 3:
                        hidden(1)
                    if s == PRE + 4:
                        pe.wait_ge(hid_ready, at(hid_ready, l, 1))
                        settle(pe)
                        mm(ps[:, 7, S - G * NCP:S], cmp_w2[:, 0:2, :].rearrange("p a b -> p (a b)"),
                           hid[:, 0, :, :].rearrange("p g c -> p (g c)"), start=True, stop=True)
                        for g in range(G):
                            for m in range(GROUP):
                                last = mm(ps[NCP * m:NCP * (m + 1), 7, g * HD:(g + 1) * HD], hid[:, 1, g, :],
                                          cmp_w2[:, 2, :], start=True, stop=True)
                        last.then_inc(kvc_acc, 1)
                    if s == PRE + 5:
                        item(6)
                    if PRE + 7 <= s < PRE + 7 + G:
                        g = s - PRE - 7
                        if g == 0:
                            pe.wait_ge(it_dve, at(it_dve, l, NI))
                        else:
                            pe.wait_ge(cs_out, at(cs_out, l, g))
                        settle(pe)
                        for m in range(GROUP):
                            q, cz = qs[:, g * GROUP + m, :], slice(P - NCP * (m + 1), 2 * P - NCP * (m + 1))
                            mm(ps[:, 7, :], kcz_hi[:, g, cz], q, start=m == 0, stop=False)
                            last = mm(ps[:, 7, :], kcz_lo[:, g, cz], q, start=False, stop=m == GROUP - 1)
                        last.then_inc(cs_acc, 1)
                    if s == PRE + 9:
                        pe.wait_ge(cs_in, at(cs_in, l, 1))
                        scores_back(1)
                    if PRE + 12 <= s < PRE + 12 + G:
                        g = s - PRE - 12
                        if g == 0:
                            pe.wait_ge(pc_done, at(pc_done, l, 1))
                        else:
                            pe.wait_ge(pct_ready, at(pct_ready, l, g))
                        for t in range(T):
                            last = nc.tensor.transpose(ps[:, 7, t * P:(t + 1) * P],
                                                       scp[:, t, g * GROUP:(g + 1) * GROUP, :], ident[:, :])
                        last.then_inc(pc_tp, 1)

                def project_out(t, slot_w, lhs, start, stop):
                    tk = slice(t * P, (t + 1) * P)
                    for hf in range(2):
                        last = mm3(ps[:, 2 * t + hf, :], [lhs[0][:, tk], lhs[1][:, tk]],
                                   [b[:, slot_w, hf * HALF:(hf + 1) * HALF] for b in (w_hi, w_lo)], start, stop)
                    return last

                pe.wait_ge(ol_done, at(ol_done, l, H))
                for k in range(KD - SLOTS):
                    pe.wait_ge(lo_done, split(l, POS_WOUT + k))
                    for t in range(T):
                        last = project_out(t, k % SLOTS, [ht_hi[:, k, :], ht_lo[:, k, :]], k == 0, False)
                    last.then_inc(split_used, 1)
                for t in range(T):
                    for k in range(KD - SLOTS, KD):
                        if t == 0:
                            pe.wait_ge(lo_done, split(l, POS_WOUT + k))
                        last = project_out(t, k % SLOTS, [ht_hi[:, k, :], ht_lo[:, k, :]], False, k == KD - 1)
                        if t == T - 1:
                            last.then_inc(split_used, 1)
                    if t < T - 1:
                        last.then_inc(out_acc, 1)
                    if t >= 1:
                        norm_transpose(l, 1, t - 1)
                norm_transpose(l, 1, T - 1)

                def up_half(pos, bank, turn, toks=slice(0, S)):
                    w = [wslot(b, pos, [KD, P]) for b in (w_hi, w_lo)]
                    for k in range(KD):
                        last = mm3(ps[:, bank, toks], [w[0][:, k, :], w[1][:, k, :]],
                                   [ht_hi[:, k, toks], ht_lo[:, k, toks]], k == 0, k == KD - 1)
                    return last

                first, rest = slice(0, S - P), slice(S - P, S)
                for uv in range(2):
                    pe.wait_ge(lo_done, split(l, POS_UP + uv))
                    pe.wait_ge(hl_done, at(hl_done, l, 4 * T - 2))
                    up_half(POS_UP + uv, uv, 0, first)
                pe.wait_ge(hl_done, at(hl_done, l, 4 * T))
                for uv in range(2):
                    up_half(POS_UP + uv, uv, 0, rest).then_inc(split_used, 1)
                for uv in range(2):
                    pe.wait_ge(lo_done, split(l, POS_UP + 2 + uv))
                    up_half(POS_UP + 2 + uv, 4 + uv, 0).then_inc(split_used, 1)
                with pe.Fori(0, FT // 2 - 1) as j:
                    for e in range(2):
                        pe.wait_ge(g_done, at(g_done, l, e + 1 + 2 * j))
                        for uv in range(2):
                            pos = POS_UP + SLOTS + 2 * e + uv
                            pe.wait_ge(lo_done, split(l, pos, SLOTS * j))
                            up_half(pos, 4 * e + uv, SLOTS * j).then_inc(split_used, 1)

                g_pair = [[g_hi[:, slot, :], g_lo[:, slot, :]] for slot in range(2)]

                def down_ready(n, turn=0):
                    pe.wait_ge(lo_done, split(l, POS_DOWN + n, turn))
                    pe.wait_ge(gl_done, at(gl_done, l, n + 1 + turn))

                down_ready(0)
                for t in (1, 3, 0, 2):
                    if t == 0:
                        pe.wait_ge(g_done, at(g_done, l, FT - 1))
                    if t == 2:
                        pe.wait_ge(g_done, at(g_done, l, FT))
                    last = project_out(t, 0, g_pair[0], True, False)
                last.then_inc(split_used, 1)
                for k in range(1, SLOTS):
                    down_ready(k)
                    for t in range(T):
                        last = project_out(t, k, g_pair[k % 2], False, False)
                    last.then_inc(split_used, 1)
                with pe.Fori(0, FT // SLOTS - 1) as j:
                    for e in range(SLOTS):
                        down_ready(SLOTS + e, SLOTS * j)
                        for t in range(T):
                            last = project_out(t, e, g_pair[e % 2], False, False)
                        last.then_inc(split_used, 1)
                for k in range(FT - 2, FT):
                    down_ready(k)
                for t in range(T):
                    for k in range(FT - 2, FT):
                        last = project_out(t, k % SLOTS, g_pair[k % 2], False, k == FT - 1)
                        if t == T - 1:
                            last.then_inc(split_used, 1)
                    if t < T - 1:
                        last.then_inc(out_acc, 1)


_INS = ["x", "attn_norm", "w_in", "mla_q_norm", "mla_kv_norm", "mla_w_uq", "mla_w_ukv", "nsa_gate_bias",
        "nsa_cmp_pos", "nsa_cmp_w1", "nsa_cmp_b1", "nsa_cmp_w2", "w_out", "ffn_norm", "ffn_w_up", "ffn_conv_w",
        "ffn_conv_b", "ffn_w_down", "final_norm"]


def kernel(**inputs):
    import numpy as _np
    import concourse.bacc as _bacc
    from concourse import mybir as _mybir
    from concourse.bass_utils import run_bass_kernel_spmd as _run

    nc = _bacc.Bacc("TRN2", target_bir_lowering=False, num_devices=1)
    arrays, args = {}, {}
    given = {n: _np.ascontiguousarray(inputs[n]) for n in _INS}
    for name, v in {**given, **shape_constants()}.items():
        arrays[f"in_{name}_dram"] = v
        args[name] = nc.dram_tensor(f"in_{name}_dram", v.shape, _mybir.dt.from_np(v.dtype), kind="ExternalInput").ap()
    out = nc.dram_tensor("out_0_dram", (1, S, D), _mybir.dt.float32, kind="ExternalOutput").ap()
    hybrid_layers(nc, args, out)
    r = _run(nc, [arrays], core_ids=[0])
    return r.results[0]["out_0_dram"]
```

```python
from contextlib import ExitStack

import numpy as np

import concourse.bass as bass
from concourse import mybir

F32 = mybir.dt.float32
F32R = mybir.dt.float32r
BF16 = mybir.dt.bfloat16
ALU = mybir.AluOpType
ACT = mybir.ActivationFunctionType
AX = mybir.AxisListType.X

P = 128
D = 1024
S = 512
L = 2
T = S // P
KD = D // P
EPS = 1e-6
NEG = -1e30
THETA = 500000.0

H = 8
QR, KVR, ROPE, NOPE, VD = 256, 128, 32, 64, 64
QK = NOPE + ROPE
HD = 64
ROT = HD // 4
G = 2
BR = 3
GROUP = H // G
CLEN, CSTRIDE, CHID = 32, 16, 128
NC = (S - CLEN) // CSTRIDE + 1
NCP = NC + 1
DFF = 2816
FT = DFF // P
TAPS = 3

COL_Q = QR + KVR + ROPE
COL_KV = COL_Q + H * HD
COL_GATE = COL_KV + BR * 2 * G * HD
COLS = COL_GATE + H * BR
CH = 4
CW = COLS // CH
HALF = D // 2
MT = CLEN * HD // P
LAT = 3
KP_LAST = (1, 2, 3, 0)
CMP_COLS = 2 * NCP
U_MLA = (H // 2) * T
U_NSA = H * T
U = U_MLA + U_NSA
LAG = 4
MLA_ORDER = (2, 3, 0, 1)
NSA_ORDER = (2, 3, 1, 0)
PT_FIRST_MLA = (0,)
PT_FIRST_NSA = (0, 1, 2, 3)

C_TAP, C_CB = 0, TAPS * 2 * FT
C_POS = C_CB + 2 * FT
C_B1 = C_POS + 2 * MT
C_END = C_B1 + 2

SLOTS = 4
POS_WIN = 2
POS_UKV = POS_WIN + CH * KD // 2
POS_UQ = POS_UKV + 1
POS_CMP = POS_UQ + 2
POS_WOUT = -(-(POS_CMP + 4) // SLOTS) * SLOTS
POS_UP = POS_WOUT + KD
POS_DOWN = POS_UP + 2 * FT
POS_END = POS_DOWN + FT
PERIOD = -(-POS_END // SLOTS) * SLOTS
DOWN_TURNS = FT // SLOTS - 2
assert POS_WOUT % SLOTS == 0 and POS_UP % SLOTS == 0 and POS_DOWN % SLOTS == 0
assert (POS_UQ + 2) % SLOTS != 0
RAW_POS = [p for p in range(POS_WIN, POS_END) if not POS_CMP + 4 <= p < POS_WOUT]
SPLIT_POS = [p for p in RAW_POS if not POS_CMP <= p < POS_CMP + 4]
MLA_POS = [POS_UKV, POS_UQ, POS_UQ + 1]
USED_POS = [p for p in SPLIT_POS if p not in MLA_POS]
CMP_POS = list(range(POS_CMP, POS_CMP + 4))
LOADS_PER_SLOT = [sum(p % SLOTS == s for p in RAW_POS) for s in range(SLOTS)]

ITEMS = [("c", 0), ("c", 1), ("k", 0), ("q", 0), ("q", 1), ("q", 2), ("q", 3), ("k", 1)]
NI = len(ITEMS)
QK_STEPS = U_MLA - T
ITEM_STEP = [4, 5, 12, 13, 14, 16, 17, 26]
HID_STEP, HIDT_STEP, KVC_STEP = [6, 7], 8, 10
CS_STEP, BACK_STEP, CS_MAX_STEP, CS_SCALE_STEP, PC_STEP = [15, 18], [19, 20], 21, 22, [24, 25]

PER_LAYER = {
    "x_done": 2 * T, "sd_done": 2 * T, "hn_done": 2 * T, "tp_done": 4 * T, "hh_done": 4 * T,
    "hl_done": 4 * T,
    "hi_done": len(SPLIT_POS), "lo_done": len(SPLIT_POS), "split_used": len(USED_POS), "cmp_used": 4,
    "win_acc": CH * (T - 1), "pj_act": CH * T // 2, "pj_dve": CH * T // 2,
    "lat_sq": 1, "lat_ready": 1, "kpe_ready": 1, "lat_tp": 4, "cols_tp": 1, "lat_hi": 4,
    "lat_lo": 3, "kpe_lo": 1, "cols_ready": 1,
    "q_roped": 1, "k_roped": 1, "gate_in": 1, "gate_exp": 1, "gates_ready": 1,
    "v_acc": T, "v_ready": T, "qk_acc": 2 * H, "qf_done": H, "qh_done": H, "kh_done": H, "q_ready": H, "kl_done": H,
    "sc_done": U, "max_done": U, "exp_done": U, "p_done": U, "t_done": U, "pt_done": U, "pv_done": U,
    "oh_done": H, "ol_done": H,
    "k_twice": G, "it_tp": NI, "it_act": NI, "it_dve": NI,
    "pos_ready": 1, "kcz_ready": 1, "hid_out": 2, "hid_tp": 1, "hb_done": 1, "hid_ready": 1, "kvc_acc": 1, "kch_done": 1,
    "kvc_ready": 1, "cs_acc": G, "cs_out": G, "cs_back": 2, "cs_in": 2,
    "cs_sub": 1, "cs_exp": 1, "pc_done": 1, "pc_tp": G, "pct_ready": G,
    "t0_done": 2 * FT, "conv_done": FT, "silu_done": FT, "g_done": FT,
    "gh_done": FT, "gl_done": FT, "out_acc": 2 * (T - 1),
}
CREDIT = {"x_done": T, "hn_done": 1, "lo_done": SLOTS, "split_used": SLOTS}


def at(s, l, n):
    return l * PER_LAYER[s.name] + (n + CREDIT.get(s.name, 0))


def nth(positions, pos):
    return sum(p <= pos for p in positions)


def before_in_slot(pos):
    same = [p for p in RAW_POS if p % SLOTS == pos % SLOTS]
    earlier = [p for p in same if p < pos]
    return (0, earlier[-1]) if earlier else (-1, same[-1])


def split_before_in_slot(pos):
    same = [p for p in SPLIT_POS if p % SLOTS == pos % SLOTS]
    earlier = [p for p in same if p < pos]
    return (0, earlier[-1]) if earlier else (-1, same[-1])


def rope_tables(dim):
    inv = (np.float32(THETA) ** (-np.arange(0, dim, 2, dtype=np.float32) / np.float32(dim))).astype(np.float32)
    ang = np.arange(S, dtype=np.float32)[:, None] * inv[None, :]
    return np.cos(ang).astype(np.float32), np.sin(ang).astype(np.float32)


def shape_constants():
    c, s = rope_tables(ROT)
    nsa = np.concatenate([c, c, -s, s], 1)
    c, s = rope_tables(ROPE)
    mla = np.concatenate([c, c, -s, s], 1)
    rope = np.concatenate([nsa, mla], 1).reshape(T, P, 2 * (ROT + ROPE)).transpose(1, 0, 2)
    table = np.concatenate([np.ones((NOPE, S)), np.concatenate([c, c], 1).T, np.concatenate([-s, s], 1).T], 0)
    table = table * QK ** -0.5
    q = np.arange(P)
    causal = np.where(q[None, :] <= q[:, None], 0.0, NEG)
    end = np.arange(NCP) * CSTRIDE + CLEN - 1
    pos = np.arange(T)[None, :, None] * P + q[:, None, None]
    cmask = np.where((end[None, None, :] <= pos) & (np.arange(NCP) < NC), 0.0, NEG)
    rowok = (pos[:, :, 0] >= CLEN - 1) * 1.0
    f = lambda a: np.ascontiguousarray(a, dtype=np.float32)
    return {"c_rope": f(rope), "c_table": f(table), "c_causal": f(causal), "c_ident": f(np.eye(P)),
            "c_cmask": f(cmask), "c_rowok": f(rowok)}


class Steps:

    def __init__(self, per_layer):
        self.per_layer, self.base, self.n = per_layer, 0, 0

    def layer(self, l):
        self.base, self.n = l * self.per_layer, 0

    def end_layer(self, name):
        assert self.n == self.per_layer, (name, self.n)

    def next(self):
        self.n += 1
        return self.base + self.n

    def loop(self, j, per_turn):
        self.outer = (self.base, self.n)
        self.base, self.n = self.base + self.n + j * per_turn, 0

    def end_loop(self, turns, per_turn):
        assert self.n == per_turn, ("turn", self.n)
        self.base, self.n = self.outer[0], self.outer[1] + turns * per_turn


def hybrid_layers(nc, a, out):
    with ExitStack() as ctx:
        def sb(name, shape, dt=F32, scope=ctx):
            return scope.enter_context(nc.sbuf_tensor(name, shape, dt))

        x = sb("x", [P, T, D])
        under = ExitStack()
        kst = []
        for name in ("k_operand", "v_operand"):
            sb(name + "_below", [P, KD - 2, S], F32, under)
            kst.append(sb(name, [P, MT, CMP_COLS], F32, under))
        under.close()
        ht_hi = sb("ht_hi", [P, KD, S], F32R)
        ht_lo = sb("ht_lo", [P, KD, S], F32R)
        raw = sb("raw", [P, SLOTS, 1024])
        under = ExitStack()
        FREE_SLOT = (POS_UQ + 2) % SLOTS
        if FREE_SLOT:
            sb("probs_t1_below", [P, FREE_SLOT, 1024], F32, under)
        probs_t1 = sb("probs_t1", [P, 2, S], F32, under)
        under.close()
        w_hi = sb("w_hi", [P, SLOTS, 1024], F32R)
        w_lo = sb("w_lo", [P, SLOTS, 1024], F32R)
        probs = sb("probs", [P, 3, 2, S])
        probs_t = sb("probs_t", [P, 2, S])
        ident = sb("ident", [P, P])
        ident_b = sb("ident_b", [P, P], BF16)
        causal = sb("causal", [P, P])
        causal_b = sb("causal_b", [P, P], BF16)
        table = sb("table", [P, S])
        rope = sb("rope", [P, T, 2 * (ROT + ROPE)])
        cmask = sb("cmask", [P, T, NCP])
        rowok = sb("rowok", [P, T])
        cols = sb("cols", [P, C_END])
        lat_g = sb("lat_g", [P, QR + KVR])
        gate_b = sb("gate_b", [P, H * BR])
        cmp_w2 = sb("cmp_w2", [P, 3, HD])
        eps = sb("eps", [P, 1])
        ms = sb("ms", [P, T])
        sd = sb("sd", [P, T])
        rstd = sb("rstd", [P, T])
        lat_ms = sb("lat_ms", [P, 2 * T])
        lat_sd = sb("lat_sd", [P, 2 * T])
        lat_rstd = sb("lat_rstd", [P, 2 * T])
        nmax = sb("nmax", [P, 4, 2])
        rsum = sb("rsum", [P, 4, 2])
        rinv = sb("rinv", [P, 4, 2])
        rgate = sb("rgate", [P, 4, 2])
        qf = sb("qf", [P, S])
        gate_e = sb("gate_e", [P, T, H * BR])
        gates = sb("gates", [P, T, H * BR])
        hid = sb("hid", [P, 2, G, NCP])
        hid_b = sb("hid_b", [P, 2])
        v_cmp = sb("v_cmp", [P, G, HD])
        cstat = sb("cstat", [P, 3, T, H])
        tmp_pool = sb("tmp_pool", [P, 2, H, ROT])
        kpe_t = sb("kpe_t", [P, 2, T, ROPE])
        kpe_r = sb("kpe_r", [P, T, 2, ROPE])

        attn = ExitStack()
        proj = sb("proj", [P, T, COLS], F32, attn)
        qs = sb("qs", [P, 8, S], F32R, attn)
        ks = sb("ks", [P, 8, S], F32R, attn)
        vm = sb("vm", [P, T, H * VD], F32, attn)
        attn.close()
        ffn = ExitStack()
        g_all = sb("g_all", [P, FT, S], F32, ffn)
        g_hi = sb("g_hi", [P, 2, S], F32R, ffn)
        g_lo = sb("g_lo", [P, 2, S], F32R, ffn)
        conv = sb("conv", [P, 2, 2, S], F32, ffn)
        silu = sb("silu", [P, 2, S], F32, ffn)
        ffn.close()

        pts = [probs_t, probs_t1]
        rows = probs_t[:, :, :].rearrange("p a (b c) -> p (a b) c", c=P)
        hn = probs[:, 0:2, :, :].rearrange("p s a n -> p s (a n)")
        norm_g = probs[:, 2, :, :].rearrange("p a n -> p (a n)")
        KCZ = 2 * P - NCP
        kcz_hi, kcz_lo = [b[:, KD - 2, 0:G * KCZ].rearrange("p (g c) -> p g c", g=G) for b in (ht_hi, ht_lo)]
        kc_hi, kc_lo = [b[:, :, P - NCP:P] for b in (kcz_hi, kcz_lo)]
        hid_rows = kpe_t[0:CMP_COLS, :, :, :].rearrange("p a t n -> p a (t n)")
        scp = vm[:, 0:2, :].rearrange("p a (t h c) -> p (a t) h c", t=T // 2, h=H)
        cs_t = [b[:, MT // 2:MT, :].rearrange("p m c -> p (m c)") for b in kst]
        pct = vm[:, 2:4, :]

        ps = ctx.enter_context(nc.psum_tensor("ps", [P, 8, S], F32))

        def sem(name):
            return ctx.enter_context(nc.semaphore(name))

        x_done = sem("x_done")
        sd_done = sem("sd_done")
        hn_done = sem("hn_done")
        tp_done = sem("tp_done")
        hh_done = sem("hh_done")
        hl_done = sem("hl_done")
        hi_done = sem("hi_done")
        lo_done = sem("lo_done")
        split_used = sem("split_used")
        cmp_used = sem("cmp_used")
        win_acc = sem("win_acc")
        pj_act = sem("pj_act")
        pj_dve = sem("pj_dve")
        lat_sq = sem("lat_sq")
        lat_ready = sem("lat_ready")
        kpe_ready = sem("kpe_ready")
        lat_tp = sem("lat_tp")
        cols_tp = sem("cols_tp")
        lat_hi = sem("lat_hi")
        lat_lo = sem("lat_lo")
        kpe_lo = sem("kpe_lo")
        cols_ready = sem("cols_ready")
        q_roped = sem("q_roped")
        k_roped = sem("k_roped")
        gate_in = sem("gate_in")
        gate_exp = sem("gate_exp")
        gates_ready = sem("gates_ready")
        v_acc = sem("v_acc")
        v_ready = sem("v_ready")
        qk_acc = sem("qk_acc")
        qf_done = sem("qf_done")
        kh_done = sem("kh_done")
        qh_done = sem("qh_done")
        q_ready = sem("q_ready")
        kl_done = sem("kl_done")
        sc_done = sem("sc_done")
        max_done = sem("max_done")
        exp_done = sem("exp_done")
        p_done = sem("p_done")
        t_done = sem("t_done")
        pt_done = sem("pt_done")
        pv_done = sem("pv_done")
        oh_done = sem("oh_done")
        ol_done = sem("ol_done")
        it_tp = sem("it_tp")
        it_act = sem("it_act")
        k_twice = sem("k_twice")
        it_dve = sem("it_dve")
        pos_ready = sem("pos_ready")
        kcz_ready = sem("kcz_ready")
        hid_out = sem("hid_out")
        hid_tp = sem("hid_tp")
        hb_done = sem("hb_done")
        hid_ready = sem("hid_ready")
        kvc_acc = sem("kvc_acc")
        kch_done = sem("kch_done")
        kvc_ready = sem("kvc_ready")
        cs_acc = sem("cs_acc")
        cs_out = sem("cs_out")
        cs_back = sem("cs_back")
        cs_in = sem("cs_in")
        cs_sub = sem("cs_sub")
        cs_exp = sem("cs_exp")
        pc_done = sem("pc_done")
        pc_tp = sem("pc_tp")
        pct_ready = sem("pct_ready")
        t0_done = sem("t0_done")
        conv_done = sem("conv_done")
        silu_done = sem("silu_done")
        g_done = sem("g_done")
        gh_done = sem("gh_done")
        gl_done = sem("gl_done")
        out_acc = sem("out_acc")
        pj = [pj_act, pj_dve]
        raw_loaded = [sem(f"raw_loaded{s}") for s in range(SLOTS)]
        x_loaded = [sem(f"x_loaded{t}") for t in range(T)]
        ident_loaded = sem("ident_loaded")
        const_loaded = sem("const_loaded")
        g_loaded = sem("g_loaded")
        small_loaded = sem("small_loaded")
        const_ready = sem("const_ready")
        settled = sem("settled")
        out_done = [sem(f"out_done{i}") for i in range(2)]
        act_chain = ctx.enter_context(nc.semaphore("act_chain"))
        dve_chain = ctx.enter_context(nc.semaphore("dve_chain"))
        pool_chain = ctx.enter_context(nc.semaphore("pool_chain"))

        def settle(eng):
            eng.sem_inc(settled, 1)

        block = ctx.enter_context(nc.Block())
        consts = [(causal, "c_causal"), (table, "c_table"), (rope, "c_rope"),
                  (cmask, "c_cmask"), (rowok, "c_rowok")]
        SMALL = 9

        def wslot(buf, pos, shape):
            n = int(np.prod(shape))
            v = buf[:, pos % SLOTS, 0:n]
            return v.rearrange("p (a b) -> p a b", b=shape[-1]) if len(shape) == 2 else v

        @block.sync
        def _(sp):
            def load_x(t):
                sp.dma_start(x[:, t, :], a["x"][0, t * P:(t + 1) * P, :]).then_inc(x_loaded[t], 16)

            load_x(0)

            def load(l, pos, src, shape, turn=0):
                back, prev = before_in_slot(pos)
                if prev in CMP_POS:
                    sp.wait_ge(cmp_used, at(cmp_used, l, nth(CMP_POS, prev)))
                else:
                    sp.wait_ge(lo_done, at(lo_done, l, back * len(SPLIT_POS) + nth(SPLIT_POS, prev) + turn))
                sp.dma_start(wslot(raw, pos, shape), src).then_inc(raw_loaded[pos % SLOTS], 16)

            for t in range(1, T):
                load_x(t)
            for t in range(T):
                sp.wait_ge(x_loaded[t], 16)
                sp.sem_inc(x_done, 1)

            with sp.Fori(0, L) as l:
                w_in = a["w_in"][bass.ds(l, 1), :, :].rearrange("o (k p) n -> p (o k) n", p=P)
                for c in range(CH):
                    for n in range(KD // 2):
                        kp = KP_LAST[n] if c == CH - 1 else n
                        load(l, POS_WIN + c * KD // 2 + n, w_in[:, 2 * kp:2 * kp + 2, c * CW:(c + 1) * CW], [2, CW])
                load(l, POS_UKV, a["mla_w_ukv"][bass.ds(l, 1), :, :].rearrange("o p n -> (o p) n"), [H * 2 * NOPE])
                uq = a["mla_w_uq"][bass.ds(l, 1), :, :].rearrange("o (k p) n -> p (o k) n", p=P)
                for k in range(2):
                    load(l, POS_UQ + k, uq[:, k, :], [H * QK])
                w1 = a["nsa_cmp_w1"][bass.ds(l, 1), :, :, :].rearrange("o a (m p) n -> p (o a m) n", p=P)
                for n in range(4):
                    load(l, POS_CMP + n, w1[:, n * MT // 2:(n + 1) * MT // 2, :], [MT // 2, CHID])
                w_out = a["w_out"][bass.ds(l, 1), :, :].rearrange("o (k p) n -> p (o k) n", p=P)
                for k in range(KD):
                    load(l, POS_WOUT + k, w_out[:, k, :], [D])
                up = a["ffn_w_up"][bass.ds(l, 1), :, :].rearrange("o (k p) n -> p (o k) n", p=P)

                def load_up(f, pos, turn):
                    for uv in range(2):
                        load(l, pos + uv, up[:, :, bass.ds(f * P + uv * DFF, P)], [KD, P], turn)

                load_up(0, POS_UP, 0)
                load_up(1, POS_UP + 2, 0)
                with sp.Fori(1, FT // 2) as j:
                    for e in range(2):
                        load_up(2 * j + e, POS_UP + SLOTS + 2 * e, (j - 1) * SLOTS)
                down = a["ffn_w_down"][bass.ds(l, 1), :, :].rearrange("o (k p) n -> (o k) p n", p=P)
                with sp.Fori(0, FT // SLOTS) as j:
                    for e in range(SLOTS):
                        load(l, POS_DOWN + e, down[bass.ds(SLOTS * j + e, 1), :, :].rearrange("k p n -> (k p) n"),
                             [D], j * SLOTS)
                for k in range(FT // SLOTS * SLOTS, FT):
                    load(l, POS_DOWN + k, down[k, :, :], [D])

            for t in range(T):
                sp.wait_ge(hn_done, at(hn_done, L, t + 1))
                sp.dma_start(out[0, t * P:(t + 1) * P, :], hn[:, t % 2, :]).then_inc(out_done[t % 2], 16)
            for slot in out_done:
                sp.wait_ge(slot, 16 * T // 2)

        def slot_loads(pos):
            return sum(p % SLOTS == pos % SLOTS and p <= pos for p in RAW_POS)

        def landed(l, pos, turns=0):
            return (l * LOADS_PER_SLOT[pos % SLOTS] + slot_loads(pos) + turns) * 16

        def split(l, pos, turn=0):
            return at(lo_done, l, nth(SPLIT_POS, pos) + turn)

        def used(l, pos, turn=0):
            return at(split_used, l, nth(USED_POS, pos) + turn)

        def pieces_map(pos):
            if POS_UQ <= pos < POS_UQ + 2:
                d = lambda b: b[:, pos % SLOTS, :].rearrange("p (h c) -> p h c", h=H)
                r = lambda b: b[:, pos % SLOTS, 0:H * QK].rearrange("p (h c) -> p h c", h=H)
                half = ROPE // 2
                return [(d, r, (0, QK), (0, QK)), (d, r, (QK, QK + half), (NOPE + half, QK)),
                        (d, r, (QK + half, P), (NOPE, NOPE + half))]
            n = 2 * CW if pos < POS_UKV else 1024
            whole = lambda b: b[:, pos % SLOTS, 0:n].unsqueeze(1)
            return [(whole, whole, (0, n), (0, n))]

        def split_hi(act, l, pos, turn=0, turns=0):
            act.wait_ge(raw_loaded[(pos) % SLOTS], landed(l, pos, turns))
            back, prev = split_before_in_slot(pos)
            if prev in MLA_POS:
                act.wait_ge(qk_acc, at(qk_acc, l, 2 * H))
            else:
                act.wait_ge(split_used, at(split_used, l, back * len(USED_POS) + nth(USED_POS, prev) + turn))
            for d, r, (d0, d1), (r0, r1) in pieces_map(pos):
                last = nc.scalar.activation(d(w_hi)[:, :, d0:d1], r(raw)[:, :, r0:r1], ACT.Copy)
            last.then_inc(hi_done, 1)

        def split_lo(dve, l, pos, turn=0):
            dve.wait_ge(hi_done, at(hi_done, l, nth(SPLIT_POS, pos) + turn))
            for d, r, (d0, d1), (r0, r1) in pieces_map(pos):
                last = nc.vector.tensor_tensor(d(w_lo)[:, :, d0:d1], r(raw)[:, :, r0:r1],
                                               d(w_hi)[:, :, d0:d1].bitcast(F32), ALU.subtract)
            last.then_inc(lo_done, 1)

        def halves(h):
            top, bottom = slice(0, HD), slice(HD, P)
            return (top, bottom) if h % 2 == 0 else (bottom, top)

        def unit(u):
            if u < U_MLA:
                return MLA_ORDER[u % T], u // T
            return NSA_ORDER[u % T], H // 2 + (u - U_MLA) // T // 2

        def score_banks(u):
            n = (unit(u)[0] + 1) * P
            if u >= U_MLA and 2 * n <= S:
                return ps[:, 2 * (u % 2), 0:2 * n].rearrange("p (a n) -> p a n", a=2)
            return ps[:, 2 * (u % 2):2 * (u % 2) + 2, 0:n]

        @block.gpsimd
        def _(pool):
            ch = Steps(2 * (T + T * BR))
            tt = nc.gpsimd.tensor_tensor

            def rotate(t, v, heads):
                c = rope[:, t, 0:ROT].unsqueeze(1).broadcast_to([P, heads, ROT])
                s = rope[:, t, ROT:2 * ROT].rearrange("p (a b) -> p a b", a=2).unsqueeze(1)\
                    .broadcast_to([P, heads, 2, ROT // 2])
                m0, m1 = tmp_pool[:, 0, 0:heads, :], tmp_pool[:, 1, 0:heads, :]
                tt(m0, v, c, ALU.mult)
                swapped = v.rearrange("p h (a b) -> p h a b", a=2)[:, :, ::-1, :]
                tt(m1.rearrange("p h (a b) -> p h a b", a=2), swapped, s, ALU.mult).then_inc(pool_chain, 1)
                pool.wait_ge(pool_chain, ch.next())
                return tt(v, m0, m1, ALU.add)

            with pool.Fori(0, L) as l:
                ch.layer(l)
                pool.wait_ge(hn_done, at(hn_done, l, 0))
                settle(pool)
                pool.dma_start(norm_g[:, :], a["attn_norm"][bass.ds(l, 1), :].broadcast_to([P, D])).then_inc(g_loaded, 16)
                pool.wait_ge(x_done, at(x_done, l, 1 - T))
                settle(pool)
                bd = lambda v, n: v.broadcast_to([P, n])
                pool.dma_start(lat_g[:, 0:QR], bd(a["mla_q_norm"][bass.ds(l, 1), :], QR)).then_inc(small_loaded, 16)
                pool.dma_start(lat_g[:, QR:QR + KVR], bd(a["mla_kv_norm"][bass.ds(l, 1), :], KVR))\
                    .then_inc(small_loaded, 16)
                pool.dma_start(gate_b[:, :], bd(a["nsa_gate_bias"][bass.ds(l, 1), :], H * BR)).then_inc(small_loaded, 16)
                w2 = a["nsa_cmp_w2"][bass.ds(l, 1), :, :, :].rearrange("o a p n -> p (o a) n")
                pool.dma_start(cmp_w2[:, 0, :], w2[:, 0, :]).then_inc(small_loaded, 16)
                pool.dma_start(cmp_w2[:, 1:3, :], w2).then_inc(small_loaded, 16)
                pool.dma_start(rows[0:2 * FT, 0:TAPS, :], a["ffn_conv_w"][bass.ds(l, 1), :, :]
                               .rearrange("o a (f p) -> f (o a) p", p=P)).then_inc(small_loaded, 16)
                pool.dma_start(rows[0:2 * FT, TAPS, :], a["ffn_conv_b"][bass.ds(l, 1), :]
                               .rearrange("o (f p) -> (o f) p", p=P)).then_inc(small_loaded, 16)
                pool.dma_start(rows[0:2 * MT, TAPS + 1, :].rearrange("m (j d) -> m j d", d=HD),
                               a["nsa_cmp_pos"][bass.ds(l, 1), :, :, :]
                               .rearrange("o a (m j) d -> (o a m) j d", j=2)).then_inc(small_loaded, 16)
                pool.dma_start(rows[0:2, TAPS + 2, :], a["nsa_cmp_b1"][bass.ds(l, 1), :, :]
                               .rearrange("o a n -> (o a) n")).then_inc(small_loaded, 16)
                pool.wait_ge(pj_act, at(pj_act, l, CH * T // 2))
                pool.wait_ge(pj_dve, at(pj_dve, l, CH * T // 2))
                tt(gate_e[:, :, :], proj[:, :, COL_GATE:COLS],
                   gate_b[:, :].unsqueeze(1).broadcast_to([P, T, H * BR]), ALU.add).then_inc(gate_in, 1)
                for t in range(T):
                    last = rotate(t, proj[:, t, COL_Q:COL_KV].rearrange("p (h d) -> p h d", h=H)[:, :, 0:ROT], H)
                    last.then_inc(pool_chain, 1)
                    pool.wait_ge(pool_chain, ch.next())
                pool.sem_inc(q_roped, 1)
                for t in range(T):
                    for b in range(BR):
                        c0 = COL_KV + b * 2 * G * HD
                        last = rotate(t, proj[:, t, c0:c0 + G * HD].rearrange("p (h d) -> p h d", h=G)[:, :, 0:ROT], G)
                        last.then_inc(pool_chain, 1)
                        pool.wait_ge(pool_chain, ch.next())
                pool.sem_inc(k_roped, 1)
                for kv in range(2):
                    pos = cols[:, C_POS + kv * MT:C_POS + (kv + 1) * MT].unsqueeze(2).broadcast_to([P, MT, 2])
                    last = nc.gpsimd.tensor_copy(kst[kv][:, :, 2 * NC:CMP_COLS], pos)
                last.then_inc(pos_ready, 1)
                pool.wait_ge(cmp_used, at(cmp_used, l, 4))
                settle(pool)
                for b in (kcz_hi, kcz_lo):
                    last = nc.gpsimd.memset(b.bitcast(F32), 0.0)
                last.then_inc(kcz_ready, 1)
                for g in range(G):
                    pool.wait_ge(it_dve, at(it_dve, l, ITEMS.index(("k", g)) + 1))
                    settle(pool)
                    for e in range(2):
                        own, other = halves(e)
                        c = 2 * (2 * g + e)
                        last = nc.gpsimd.tensor_copy(ks[other, c:c + 2, :], ks[own, c:c + 2, :])
                    last.then_inc(k_twice, 1)
                pool.wait_ge(t_done, at(t_done, l, U))
                settle(pool)
                pool.dma_start(norm_g[:, :], a["ffn_norm"][bass.ds(l, 1), :].broadcast_to([P, D])).then_inc(g_loaded, 16)
                ch.end_layer("pool")
            pool.wait_ge(hn_done, at(hn_done, L, 0))
            pool.dma_start(norm_g[:, :], a["final_norm"].rearrange("(o d) -> o d", o=1).broadcast_to([P, D]))\
                .then_inc(g_loaded, 16)

        @block.scalar
        def _(act):
            act.dma_start(ident[:, :], a["c_ident"]).then_inc(ident_loaded, 16)
            for tile, name in consts:
                act.dma_start(tile[tuple(slice(None) for _ in tile.shape)], a[name]).then_inc(const_loaded, 16)
            ch = Steps(2 * T + 1)
            activate = nc.scalar.activation

            def norm_stats(l, w, t):
                act.wait_ge(x_done, at(x_done, l, w * T + t + 1 - T))
                activate(ps[:, 2 * t:2 * t + 2, :], x[:, t, :].rearrange("p (a n) -> p a n", a=2), ACT.Square,
                                 scale=D ** -0.5, accum_out=ms[:, t:t + 1]).then_inc(act_chain, 1)
                act.wait_ge(act_chain, ch.next())
                activate(sd[:, t:t + 1], ms[:, t:t + 1], ACT.Sqrt, bias=eps[:, :]).then_inc(sd_done, 1)

            def norm_hi(l, w, t):
                for b in range(2):
                    act.wait_ge(tp_done, at(tp_done, l, 2 * (w * T + t) + b + 1))
                    activate(ht_hi[:, 4 * b:4 * b + 4, t * P:(t + 1) * P],
                             ps[:, 2 * t + b, :].rearrange("p (k n) -> p k n", k=4), ACT.Copy)\
                        .then_inc(hh_done, 1)

            act.wait_ge(const_ready, 2)

            with act.Fori(0, L) as l:
                ch.layer(l)
                norm_stats(l, 0, 0)
                split_hi(act, l, POS_WIN)
                norm_stats(l, 0, 1)
                norm_hi(l, 0, 0)
                split_hi(act, l, POS_WIN + 1)
                split_hi(act, l, POS_WIN + 2)
                norm_stats(l, 0, 2)
                norm_hi(l, 0, 1)
                split_hi(act, l, POS_WIN + 3)
                norm_stats(l, 0, 3)
                norm_hi(l, 0, 2)
                norm_hi(l, 0, 3)

                def evac_chunk(c):
                    for t in range(0, T, 2):
                        act.wait_ge(win_acc, at(win_acc, l, c * (T - 1) + t + 1))
                        activate(proj[:, t, c * CW:(c + 1) * CW], ps[:, 4 * (c % 2) + t, 0:CW], ACT.Copy)\
                            .then_inc(pj_act, 1)

                def win_splits(c):
                    for kp in range(KD // 2):
                        split_hi(act, l, POS_WIN + c * KD // 2 + kp)

                win_splits(1)
                evac_chunk(0)
                act.wait_ge(pj_act, at(pj_act, l, T // 2))
                act.wait_ge(pj_dve, at(pj_dve, l, T // 2))
                for t in range(T):
                    activate(ps[:, t, 0:QR], proj[:, t, 0:QR], ACT.Square, scale=QR ** -0.5,
                             accum_out=lat_ms[:, 2 * t:2 * t + 1])
                    last = activate(ps[:, t, QR:QR + KVR], proj[:, t, QR:QR + KVR], ACT.Square, scale=KVR ** -0.5,
                                    accum_out=lat_ms[:, 2 * t + 1:2 * t + 2])
                last.then_inc(act_chain, 1)
                act.wait_ge(act_chain, ch.next())
                activate(lat_sd[:, :], lat_ms[:, :], ACT.Sqrt, bias=eps[:, :]).then_inc(lat_sq, 1)
                win_splits(2)
                evac_chunk(1)
                win_splits(3)
                split_hi(act, l, POS_UKV)
                evac_chunk(2)
                split_hi(act, l, POS_UQ)
                for n in range(3):
                    act.wait_ge(lat_tp, at(lat_tp, l, n + 1))
                    activate(ht_hi[:, LAT + n, :], ps[:, n, :], ACT.Copy).then_inc(lat_hi, 1)
                act.wait_ge(lat_tp, at(lat_tp, l, 4))
                for n in range(4):
                    last = activate(ks[NOPE:P, 2 * n, :], ps[0:2 * ROPE, 3, :], ACT.Copy)
                last.then_inc(lat_hi, 1)
                split_hi(act, l, POS_UQ + 1)
                evac_chunk(3)

                def q_hi(n):
                    act.wait_ge(qf_done, at(qf_done, l, n + 1))
                    activate(qs[:, 2 * (n % 4), :], qf[:, :], ACT.Copy).then_inc(qh_done, 1)

                def k_hi(n, bank):
                    act.wait_ge(qk_acc, at(qk_acc, l, 2 * n + 2))
                    i = 2 * (n % 4)
                    activate(ks[0:NOPE, i, :], ps[0:NOPE, bank, :], ACT.Copy).then_inc(kh_done, 1)

                for n in range(2):
                    q_hi(n)
                    k_hi(n, 2 * n + 1)
                for n in range(T):
                    t = T - 1 - n
                    act.wait_ge(v_acc, at(v_acc, l, n + 1))
                    activate(vm[:, t, :], ps[:, 4 + t, :], ACT.Copy).then_inc(v_ready, 1)

                def exps(u):
                    i, _ = unit(u)
                    n = (i + 1) * P
                    act.wait_ge(max_done, at(max_done, l, u + 1))
                    if u >= 3:
                        act.wait_ge(t_done, at(t_done, l, u - 2))
                    sc = score_banks(u)
                    for s in range(2):
                        last = activate(probs[:, u % 3, s, 0:n], sc[:, s, :], ACT.Exp,
                                        bias=nmax[:, u % 4, s:s + 1], accum_out=rsum[:, u % 4, s:s + 1])
                    last.then_inc(exp_done, 1)

                def evac_pt(u):
                    i, _ = unit(u)
                    n = (i + 1) * P
                    act.wait_ge(t_done, at(t_done, l, u + 1))
                    if u >= 2:
                        act.wait_ge(pv_done, at(pv_done, l, u - 1))
                    activate(pts[u % 2][:, :, 0:n], ps[:, 4:6, 0:n], ACT.Copy).then_inc(pt_done, 1)

                def evac_out(pair, bank):
                    done = T * (pair + 1) if pair < H // 2 else U_MLA + 2 * T * (pair - H // 2 + 1)
                    act.wait_ge(pv_done, at(pv_done, l, done))
                    activate(ht_hi[:, pair, :], ps[:, bank, :], ACT.Copy).then_inc(oh_done, 1)

                def item_hi(n):
                    kind, i = ITEMS[n]
                    act.wait_ge(it_tp, at(it_tp, l, n + 1))
                    for e in range(2):
                        own = halves(e)[0]
                        if kind == "k":
                            ins = activate(ks[own, 2 * (2 * i + e), :], ps[own, 7, :], ACT.Copy)
                        elif kind == "q":
                            ins = activate(qs[own, 2 * i + e, :], ps[own, 7, :], ACT.Copy, scale=HD ** -0.5)
                        else:
                            tok = ps[own, 7, :].rearrange("p (c m two) -> p two m c", two=2, m=MT // 2)
                            for part in range(2):
                                ins = activate(kst[i][0:HD, part * MT // 2:(part + 1) * MT // 2, e * NC:(e + 1) * NC],
                                               tok[:, 0, :, part:part + NC], ACT.Copy)
                    ins.then_inc(it_act, 1)

                for s in range(U + LAG):
                    early = s % T in (PT_FIRST_MLA if s < U_MLA else PT_FIRST_NSA)
                    if early and 0 <= s - 2 < U:
                        evac_pt(s - 2)
                    if s < U:
                        exps(s)
                    if s < QK_STEPS:
                        n = s // 2 + 2
                        if s % 2 == 0:
                            q_hi(n)
                        else:
                            k_hi(n, 7)
                    if s == 2:
                        act.wait_ge(gate_in, at(gate_in, l, 1))
                        activate(gates[:, :, :], gate_e[:, :, :], ACT.Exp, scale=-1.0).then_inc(gate_exp, 1)
                    if LAG <= s < U_MLA + LAG and (s - LAG) % T == T - 1:
                        evac_out((s - LAG) // T, 6)
                    if s - LAG >= U_MLA and (s - LAG - U_MLA) % (2 * T) == 2 * T - 1:
                        pair = (s - LAG - U_MLA) // (2 * T)
                        evac_out(H // 2 + pair, 6 + pair % 2)
                    if not early and 0 <= s - 2 < U:
                        evac_pt(s - 2)
                    if s in ITEM_STEP:
                        item_hi(ITEM_STEP.index(s))
                    if s in HID_STEP:
                        kv = HID_STEP.index(s)
                        act.wait_ge(cmp_used, at(cmp_used, l, 2 * kv + 2))
                        activate(hid_rows[:, kv, :], ps[0:CMP_COLS, 7, 0:CHID], ACT.Copy).then_inc(hid_out, 1)
                    if s == HIDT_STEP:
                        act.wait_ge(hb_done, at(hb_done, l, 1))
                        for kv in range(2):
                            c = kv * CMP_COLS
                            last = activate(hid[:, kv, :, 0:NC],
                                            ps[:, 7, c:c + G * NC].rearrange("p (g c) -> p g c", g=G),
                                            ACT.Gelu_apprx_tanh, bias=hid_b[:, kv:kv + 1])
                        last.then_inc(hid_ready, 1)
                    if s == KVC_STEP:
                        act.wait_ge(kvc_acc, at(kvc_acc, l, 1))
                        act.wait_ge(kcz_ready, at(kcz_ready, l, 1))
                        activate(kc_hi[:, :, :], ps[:, 7, S - G * NCP:S].rearrange("p (g c) -> p g c", g=G), ACT.Copy)\
                            .then_inc(kch_done, 1)
                    if s in CS_STEP:
                        g = CS_STEP.index(s)
                        act.wait_ge(cs_acc, at(cs_acc, l, g + 1))
                        activate(cs_t[g], ps[:, 7, :], ACT.Copy).then_inc(cs_out, 1)
                    if s == CS_MAX_STEP:
                        act.wait_ge(cs_sub, at(cs_sub, l, 1))
                        activate(scp, scp, ACT.Exp).then_inc(cs_exp, 1)
                    if s in PC_STEP:
                        g = PC_STEP.index(s)
                        act.wait_ge(pc_tp, at(pc_tp, l, g + 1))
                        activate(pct[:, g, :], ps[:, 7, :], ACT.Copy).then_inc(pct_ready, 1)
                    if s == U_MLA + 4 * T:
                        split_hi(act, l, POS_WOUT)
                for k in range(1, KD):
                    split_hi(act, l, POS_WOUT + k)
                norm_stats(l, 1, 0)
                norm_stats(l, 1, 1)
                norm_hi(l, 1, 0)
                norm_stats(l, 1, 2)
                norm_hi(l, 1, 1)
                split_hi(act, l, POS_UP)
                norm_stats(l, 1, 3)
                norm_hi(l, 1, 2)
                split_hi(act, l, POS_UP + 1)
                norm_hi(l, 1, 3)
                split_hi(act, l, POS_UP + 2)
                split_hi(act, l, POS_UP + 3)

                def up_tail(f, fl, pos_turn):
                    for uv in range(2):
                        act.wait_ge(split_used, used(l, POS_UP + 2 * fl + uv, pos_turn))
                        tap = cols[:, bass.ds(C_TAP + 2 * 2 * FT + f + uv * FT, 1)]
                        bias = cols[:, bass.ds(C_CB + f + uv * FT, 1)]
                        activate(conv[:, fl, uv, :], ps[:, 4 * fl + uv, :], ACT.Identity, bias=bias, scale=tap)\
                            .then_inc(t0_done, 1)
                    act.wait_ge(conv_done, at(conv_done, l, pos_turn // 2 + fl + 1))
                    activate(silu[:, fl, :], conv[:, fl, 0, :], ACT.Silu).then_inc(silu_done, 1)

                with act.Fori(0, FT // 2 - 1) as j:
                    for e in range(2):
                        up_tail(2 * j + e, e, 4 * j)
                        for uv in range(2):
                            p = 2 * e + uv
                            split_hi(act, l, POS_UP + SLOTS + p, SLOTS * j, j)

                def g_split_hi(k, n, turn=0):
                    act.wait_ge(g_done, at(g_done, l, min(n + 1, FT) + turn))
                    if n >= 2:
                        act.wait_ge(split_used, used(l, POS_DOWN + n - 2, turn))
                    activate(g_hi[:, n % 2, :].unsqueeze(1), g_all[:, bass.ds(k, 1), :], ACT.Copy)\
                        .then_inc(gh_done, 1)

                for e in range(2):
                    g_split_hi(e, e)
                for e in range(2):
                    up_tail(FT - 2 + e, e, 2 * (FT - 2))
                    for uv in range(2):
                        split_hi(act, l, POS_DOWN + 2 * e + uv)
                for n in range(SLOTS):
                    g_split_hi(n + 2, n + 2)
                    split_hi(act, l, POS_DOWN + SLOTS + n)
                with act.Fori(0, DOWN_TURNS) as j:
                    for e in range(SLOTS):
                        g_split_hi(SLOTS * j + SLOTS + e + 2, SLOTS + e + 2, SLOTS * j)
                        split_hi(act, l, POS_DOWN + 2 * SLOTS + e, SLOTS * j, j)
                for n in range(SLOTS * (DOWN_TURNS + 1), FT - 2):
                    g_split_hi(n + 2, n + 2)
                    if n + SLOTS < FT:
                        split_hi(act, l, POS_DOWN + n + SLOTS)
                ch.end_layer("act")

            for t in range(T):
                act.wait_ge(x_done, at(x_done, L, t + 1 - T))
                ins = activate(ps[:, 2 * t:2 * t + 2, :], x[:, t, :].rearrange("p (a n) -> p a n", a=2), ACT.Square,
                               scale=D ** -0.5, accum_out=ms[:, t:t + 1])
                ins.then_inc(act_chain, 1)
                act.wait_ge(act_chain, L * ch.per_layer + t + 1)
                activate(sd[:, t:t + 1], ms[:, t:t + 1], ACT.Sqrt, bias=eps[:, :]).then_inc(sd_done, 1)

        @block.vector
        def _(dve):
            ch = Steps(0)
            v = nc.vector
            tt, stt = v.tensor_tensor, v.scalar_tensor_tensor
            ch.per_layer = 2 * T + 3 + U_MLA + 2 * U_NSA + 5 + FT
            dve.sem_inc(lo_done, CREDIT["lo_done"])
            dve.sem_inc(hn_done, CREDIT["hn_done"])
            v.memset(hid[:, :, :, :], 0.0).then_inc(const_ready, 1)
            v.memset(eps[:, :], EPS).then_inc(const_ready, 1)
            dve.wait_ge(ident_loaded, 16)
            v.tensor_copy(ident_b[:, :], ident[:, :]).then_inc(const_ready, 1)

            def norm_rows(l, w, t, final=False):
                dve.wait_ge(sd_done, at(sd_done, l, w * T + t + 1))
                v.reciprocal(rstd[:, t:t + 1], sd[:, t:t + 1]).then_inc(dve_chain, 1)
                dve.wait_ge(dve_chain, ch.next())
                if t == 0:
                    dve.wait_ge(g_loaded, (l * 2 + w + 1) * 16)
                if t >= 2:
                    if final:
                        dve.wait_ge(out_done[t % 2], 16 * (t // 2))
                    else:
                        dve.wait_ge(tp_done, at(tp_done, l, 2 * (w * T + t - 2) + 2))
                stt(out=hn[:, t % 2, :], in0=x[:, t, :], scalar=rstd[:, t:t + 1], in1=norm_g[:, :], op0=ALU.mult,
                    op1=ALU.mult).then_inc(hn_done, 1)

            def norm_lo(l, w, t):
                for b in range(2):
                    dve.wait_ge(hh_done, at(hh_done, l, 2 * (w * T + t) + b + 1))
                    r = (slice(None), slice(4 * b, 4 * b + 4), slice(t * P, (t + 1) * P))
                    tt(ht_lo[r], ps[:, 2 * t + b, :].rearrange("p (k n) -> p k n", k=4), ht_hi[r].bitcast(F32),
                       ALU.subtract).then_inc(hl_done, 1)

            def add_x(l, w, t):
                if t < T - 1:
                    dve.wait_ge(out_acc, at(out_acc, l, w * (T - 1) + t + 1))
                else:
                    dve.wait_ge(split_used, used(l, (POS_UP if w == 0 else POS_END) - 1))
                xt = x[:, t, :].rearrange("p (a n) -> p a n", a=2)
                tt(xt, xt, ps[:, 2 * t:2 * t + 2, :], ALU.add).then_inc(x_done, 1)

            with dve.Fori(0, L) as l:
                ch.layer(l)
                norm_rows(l, 0, 0)
                split_lo(dve, l, POS_WIN)
                norm_rows(l, 0, 1)
                norm_lo(l, 0, 0)
                split_lo(dve, l, POS_WIN + 1)
                split_lo(dve, l, POS_WIN + 2)
                norm_rows(l, 0, 2)
                norm_lo(l, 0, 1)
                split_lo(dve, l, POS_WIN + 3)
                norm_rows(l, 0, 3)
                norm_lo(l, 0, 2)
                norm_lo(l, 0, 3)

                def evac_chunk(c):
                    for t in range(1, T, 2):
                        if t < T - 1:
                            dve.wait_ge(win_acc, at(win_acc, l, c * (T - 1) + t + 1))
                        else:
                            dve.wait_ge(split_used, used(l, POS_WIN + (c + 1) * KD // 2 - 1))
                        v.tensor_copy(proj[:, t, c * CW:(c + 1) * CW], ps[:, 4 * (c % 2) + t, 0:CW])\
                            .then_inc(pj_dve, 1)

                def win_splits(c):
                    for kp in range(KD // 2):
                        split_lo(dve, l, POS_WIN + c * KD // 2 + kp)

                win_splits(1)
                dve.wait_ge(const_loaded, 16 * len(consts))
                v.tensor_copy(causal_b[:, :], causal[:, :])
                evac_chunk(0)
                dve.wait_ge(pj_act, at(pj_act, l, T // 2))
                dve.wait_ge(pj_dve, at(pj_dve, l, T // 2))
                kp = proj[:, :, QR + KVR:COL_Q]
                rc = rope[:, :, 2 * ROT:2 * ROT + ROPE]
                rs = rope[:, :, 2 * ROT + ROPE:].rearrange("p t (a b) -> p t a b", a=2)
                dve.wait_ge(small_loaded, (l + 1) * 16 * SMALL)
                tt(kpe_t[:, 0, :, :], kp, rc, ALU.mult)
                tt(kpe_t[:, 1, :, :].rearrange("p t (a b) -> p t a b", a=2),
                           kp.rearrange("p t (a b) -> p t a b", a=2)[:, :, ::-1, :], rs, ALU.mult).then_inc(dve_chain, 1)
                dve.wait_ge(dve_chain, ch.next())
                twice = lambda n: kpe_t[:, n, :, :].unsqueeze(2).broadcast_to([P, T, 2, ROPE])
                tt(kpe_r[:, :, :, :], twice(0), twice(1), ALU.add).then_inc(kpe_ready, 1)
                dve.wait_ge(lat_sq, at(lat_sq, l, 1))
                v.reciprocal(lat_rstd[:, :], lat_sd[:, :]).then_inc(dve_chain, 1)
                dve.wait_ge(dve_chain, ch.next())
                for t in range(T):
                    stt(out=proj[:, t, 0:QR], in0=proj[:, t, 0:QR], scalar=lat_rstd[:, 2 * t:2 * t + 1],
                        in1=lat_g[:, 0:QR], op0=ALU.mult, op1=ALU.mult)
                    last = stt(out=proj[:, t, QR:QR + KVR], in0=proj[:, t, QR:QR + KVR],
                               scalar=lat_rstd[:, 2 * t + 1:2 * t + 2], in1=lat_g[:, QR:QR + KVR], op0=ALU.mult,
                               op1=ALU.mult)
                last.then_inc(lat_ready, 1)
                win_splits(2)
                evac_chunk(1)
                dve.wait_ge(cols_tp, at(cols_tp, l, 1))
                v.tensor_copy(cols[:, :], ps[:, 4, 0:C_END]).then_inc(cols_ready, 1)
                win_splits(3)
                split_lo(dve, l, POS_UKV)
                evac_chunk(2)
                split_lo(dve, l, POS_UQ)
                for n in range(3):
                    dve.wait_ge(lat_hi, at(lat_hi, l, n + 1))
                    tt(ht_lo[:, LAT + n, :], ps[:, n, :], ht_hi[:, LAT + n, :].bitcast(F32), ALU.subtract)\
                        .then_inc(lat_lo, 1)
                dve.wait_ge(lat_hi, at(lat_hi, l, 4))
                for n in range(4):
                    last = tt(ks[NOPE:P, 2 * n + 1, :], ps[0:2 * ROPE, 3, :], ks[NOPE:P, 2 * n, :].bitcast(F32),
                              ALU.subtract)
                last.then_inc(kpe_lo, 1)
                split_lo(dve, l, POS_UQ + 1)
                evac_chunk(3)

                def q_rows(n, bank):
                    dve.wait_ge(qk_acc, at(qk_acc, l, 2 * n + 1))
                    if n >= 1:
                        dve.wait_ge(q_ready, at(q_ready, l, n))
                    tt(qf[:, :], ps[:, bank, :], table[:, :], ALU.mult).then_inc(qf_done, 1)

                def q_lo(n):
                    dve.wait_ge(qh_done, at(qh_done, l, n + 1))
                    i = 2 * (n % 4)
                    tt(qs[:, i + 1, :], qf[:, :], qs[:, i, :].bitcast(F32), ALU.subtract).then_inc(q_ready, 1)

                def k_lo(n, bank):
                    dve.wait_ge(kh_done, at(kh_done, l, n + 1))
                    i = 2 * (n % 4)
                    tt(ks[0:NOPE, i + 1, :], ps[0:NOPE, bank, :], ks[0:NOPE, i, :].bitcast(F32), ALU.subtract)\
                        .then_inc(kl_done, 1)

                for n in range(2):
                    q_rows(n, 2 * n)
                    q_lo(n)
                    k_lo(n, 2 * n + 1)

                def row_max(u):
                    i, _ = unit(u)
                    n = (i + 1) * P
                    dve.wait_ge(sc_done, at(sc_done, l, u + 1))
                    v.tensor_reduce(nmax[:, u % 4, :], score_banks(u), AX, ALU.max, negate=True)\
                        .then_inc(max_done, 1)

                def scale_probs(u):
                    i, _ = unit(u)
                    n = (i + 1) * P
                    dve.wait_ge(exp_done, at(exp_done, l, u + 1))
                    v.reciprocal(rinv[:, u % 4, :], rsum[:, u % 4, :]).then_inc(dve_chain, 1)
                    dve.wait_ge(dve_chain, ch.next())
                    r = rinv
                    if u >= U_MLA:
                        h = (u - U_MLA) // T
                        tt(rgate[:, u % 4, :], rinv[:, u % 4, :], gates[:, i, BR * h + 1:BR * h + 3],
                           ALU.mult).then_inc(dve_chain, 1)
                        dve.wait_ge(dve_chain, ch.next())
                        r = rgate
                    for s in range(2):
                        last = v.tensor_scalar(probs[:, u % 3, s, 0:n], probs[:, u % 3, s, 0:n],
                                               r[:, u % 4, s:s + 1], None, ALU.mult)
                    last.then_inc(p_done, 1)

                def out_lo(pair, bank):
                    dve.wait_ge(oh_done, at(oh_done, l, pair + 1))
                    tt(ht_lo[:, pair, :], ps[:, bank, :], ht_hi[:, pair, :].bitcast(F32), ALU.subtract)\
                        .then_inc(ol_done, 1)

                def item_lo(n):
                    kind, i = ITEMS[n]
                    dve.wait_ge(it_act, at(it_act, l, n + 1))
                    for e in range(2):
                        own, other = halves(e)
                        if kind == "k":
                            c = 2 * (2 * i + e)
                            ins = tt(ks[own, c + 1, :], ps[own, 7, :], ks[own, c, :].bitcast(F32), ALU.subtract)
                        elif kind == "q":
                            ins = stt(out=qs[other, 2 * i + e, :], in0=ps[own, 7, :], scalar=HD ** -0.5,
                                      in1=qs[own, 2 * i + e, :].bitcast(F32), op0=ALU.mult, op1=ALU.subtract)
                        else:
                            tok = ps[own, 7, :].rearrange("p (c m two) -> p two m c", two=2, m=MT // 2)
                            for part in range(2):
                                ins = v.tensor_copy(kst[i][HD:P, part * MT // 2:(part + 1) * MT // 2,
                                                           e * NC:(e + 1) * NC], tok[:, 1, :, part:part + NC])
                    ins.then_inc(it_dve, 1)

                sc3 = scp.rearrange("p t h c -> p (t h) c")
                st = lambda n: cstat[:, n, :, :].rearrange("p t h -> p (t h)")
                wide = lambda n: st(n).unsqueeze(2).broadcast_to([P, T * H, NCP])

                def cs_mask(b):
                    t2 = slice(b * T // 2, (b + 1) * T // 2)
                    dve.wait_ge(cs_back, at(cs_back, l, b + 1))
                    tt(scp[:, t2, :, :], ps[:, 7, :].rearrange("p (t h c) -> p t h c", t=T // 2, h=H),
                       cmask[:, t2, :].unsqueeze(2).broadcast_to([P, T // 2, H, NCP]), ALU.add).then_inc(cs_in, 1)

                def cs_less_max():
                    dve.wait_ge(cs_in, at(cs_in, l, 2))
                    v.tensor_reduce(st(0), sc3, AX, ALU.max).then_inc(dve_chain, 1)
                    dve.wait_ge(dve_chain, ch.next())
                    tt(sc3, sc3, wide(0), ALU.subtract).then_inc(cs_sub, 1)

                def cs_scale():
                    dve.wait_ge(cs_exp, at(cs_exp, l, 1))
                    v.tensor_reduce(st(1), sc3, AX, ALU.add).then_inc(dve_chain, 1)
                    dve.wait_ge(dve_chain, ch.next())
                    v.reciprocal(st(2), st(1)).then_inc(dve_chain, 1)
                    dve.wait_ge(dve_chain, ch.next())
                    tt(cstat[:, 0, :, :], cstat[:, 2, :, :], gates[:, :, 0:H * BR:BR], ALU.mult).then_inc(dve_chain, 1)
                    dve.wait_ge(dve_chain, ch.next())
                    tt(cstat[:, 1, :, :], cstat[:, 0, :, :],
                       rowok[:, :].unsqueeze(2).broadcast_to([P, T, H]), ALU.mult).then_inc(dve_chain, 1)
                    dve.wait_ge(dve_chain, ch.next())
                    tt(sc3, sc3, wide(1), ALU.mult).then_inc(pc_done, 1)

                for s in range(U + LAG):
                    if s < U:
                        row_max(s)
                    if s - 1 in ITEM_STEP:
                        item_lo(ITEM_STEP.index(s - 1))
                    if s == HIDT_STEP + 1:
                        dve.wait_ge(hid_tp, at(hid_tp, l, 1))
                        pos = ps[:, 7, 0:2 * CMP_COLS].rearrange("p (a c) -> p a c", a=2)[:, :, 2 * NC]
                        tt(hid_b[:, :], pos, cols[:, C_B1:C_B1 + 2], ALU.add).then_inc(hb_done, 1)
                    if s == KVC_STEP + 1:
                        dve.wait_ge(kch_done, at(kch_done, l, 1))
                        tt(kc_lo[:, :, :], ps[:, 7, S - G * NCP:S].rearrange("p (g c) -> p g c", g=G),
                           kc_hi[:, :, :].bitcast(F32), ALU.subtract)
                        v.tensor_copy(v_cmp[:, :, :], ps[:, 7, 0:G * HD].rearrange("p (g c) -> p g c", g=G))\
                            .then_inc(kvc_ready, 1)
                    if s - 1 in BACK_STEP:
                        cs_mask(BACK_STEP.index(s - 1))
                    if 0 <= s - 1 < U:
                        scale_probs(s - 1)
                    if s == CS_MAX_STEP:
                        cs_less_max()
                    if s == CS_SCALE_STEP:
                        cs_scale()
                    if s < QK_STEPS:
                        n = s // 2 + 2
                        if s % 2 == 0:
                            q_rows(n, 7)
                        else:
                            k_lo(n, 7)
                            q_lo(n)
                    if s == 3:
                        dve.wait_ge(gate_exp, at(gate_exp, l, 1))
                        v.tensor_scalar(gates[:, :, :], gates[:, :, :], 1.0, None, ALU.add).then_inc(dve_chain, 1)
                        dve.wait_ge(dve_chain, ch.next())
                        v.reciprocal(gates[:, :, :], gates[:, :, :]).then_inc(gates_ready, 1)
                    if LAG <= s < U_MLA + LAG and (s - LAG) % T == T - 1:
                        out_lo((s - LAG) // T, 6)
                    if s - LAG >= U_MLA and (s - LAG - U_MLA) % (2 * T) == 2 * T - 1:
                        pair = (s - LAG - U_MLA) // (2 * T)
                        out_lo(H // 2 + pair, 6 + pair % 2)
                    if s == U_MLA + 4 * T + 1:
                        split_lo(dve, l, POS_WOUT)
                for k in range(1, KD):
                    split_lo(dve, l, POS_WOUT + k)
                add_x(l, 0, 0)
                norm_rows(l, 1, 0)
                add_x(l, 0, 1)
                norm_rows(l, 1, 1)
                norm_lo(l, 1, 0)
                add_x(l, 0, 2)
                norm_rows(l, 1, 2)
                norm_lo(l, 1, 1)
                split_lo(dve, l, POS_UP)
                add_x(l, 0, 3)
                norm_rows(l, 1, 3)
                norm_lo(l, 1, 2)
                split_lo(dve, l, POS_UP + 1)
                norm_lo(l, 1, 3)
                split_lo(dve, l, POS_UP + 2)
                split_lo(dve, l, POS_UP + 3)

                def up_tail(f, fl, turn):
                    for tap in (1, 0):
                        for uv in range(2):
                            if tap == 1:
                                dve.wait_ge(t0_done, at(t0_done, l, turn + 2 * fl + uv + 1))
                            back = TAPS - 1 - tap
                            c = cols[:, bass.ds(C_TAP + tap * 2 * FT + f + uv * FT, 1)]
                            ins = stt(out=conv[:, fl, uv, back:S], in0=ps[:, 4 * fl + uv, 0:S - back], scalar=c,
                                      in1=conv[:, fl, uv, back:S], op0=ALU.mult, op1=ALU.add)
                        if tap == 1:
                            ins.then_inc(dve_chain, 1)
                            dve.wait_ge(dve_chain, ch.next())
                    ins.then_inc(conv_done, 1)
                    dve.wait_ge(silu_done, at(silu_done, l, turn // 2 + fl + 1))
                    dve.wait_ge(conv_done, at(conv_done, l, turn // 2 + fl + 1))
                    tt(g_all[:, bass.ds(f, 1), :], silu[:, fl, :].unsqueeze(1), conv[:, fl, 1, :].unsqueeze(1),
                       ALU.mult).then_inc(g_done, 1)

                with dve.Fori(0, FT // 2 - 1) as j:
                    ch.loop(j, 2)
                    for e in range(2):
                        up_tail(2 * j + e, e, 4 * j)
                        for uv in range(2):
                            split_lo(dve, l, POS_UP + SLOTS + 2 * e + uv, SLOTS * j)
                    ch.end_loop(FT // 2 - 1, 2)

                def g_split_lo(k, n, turn=0):
                    dve.wait_ge(gh_done, at(gh_done, l, n + 1 + turn))
                    tt(g_lo[:, n % 2, :].unsqueeze(1), g_all[:, bass.ds(k, 1), :],
                       g_hi[:, n % 2, :].unsqueeze(1).bitcast(F32), ALU.subtract).then_inc(gl_done, 1)

                for e in range(2):
                    g_split_lo(e, e)
                for e in range(2):
                    up_tail(FT - 2 + e, e, 2 * (FT - 2))
                    for uv in range(2):
                        split_lo(dve, l, POS_DOWN + 2 * e + uv)
                for n in range(SLOTS):
                    g_split_lo(n + 2, n + 2)
                    split_lo(dve, l, POS_DOWN + SLOTS + n)
                with dve.Fori(0, DOWN_TURNS) as j:
                    for e in range(SLOTS):
                        g_split_lo(SLOTS * j + SLOTS + e + 2, SLOTS + e + 2, SLOTS * j)
                        split_lo(dve, l, POS_DOWN + 2 * SLOTS + e, SLOTS * j)
                for n in range(SLOTS * (DOWN_TURNS + 1), FT - 2):
                    g_split_lo(n + 2, n + 2)
                    if n + SLOTS < FT:
                        split_lo(dve, l, POS_DOWN + n + SLOTS)
                for t in range(T):
                    add_x(l, 1, t)

                ch.end_layer("dve")

            ch.layer(L)
            for t in range(T):
                norm_rows(L, 0, t, final=True)

        @block.tensor
        def _(pe):
            mm = nc.tensor.matmul

            def mm3(o, lhs, rhs, start, stop):
                mm(o, lhs[0], rhs[0], start=start, stop=False)
                mm(o, lhs[0], rhs[1], start=False, stop=False)
                return mm(o, lhs[1], rhs[0], start=False, stop=stop)

            pe.wait_ge(const_ready, 3)
            pe.sem_inc(split_used, CREDIT["split_used"])

            def norm_transpose(l, w, t):
                pe.wait_ge(hn_done, at(hn_done, l, w * T + t + 1))
                for b in range(2):
                    for k in range(4):
                        last = nc.tensor.transpose(ps[:, 2 * t + b, k * P:(k + 1) * P],
                                                   hn[:, t % 2, (4 * b + k) * P:(4 * b + k + 1) * P], ident[:, :])
                    last.then_inc(tp_done, 1)

            with pe.Fori(0, L) as l:
                def win_first(t):
                    pe.wait_ge(hl_done, at(hl_done, l, 2 * t + 2))
                    tk = slice(t * P, (t + 1) * P)
                    for kp in range(KD // 2):
                        if t == 0:
                            pe.wait_ge(lo_done, split(l, POS_WIN + kp))
                        w = [wslot(b, POS_WIN + kp, [2, CW]) for b in (w_hi, w_lo)]
                        for kk in range(2):
                            k = 2 * kp + kk
                            last = mm3(ps[:, t, 0:CW], [ht_hi[:, k, tk], ht_lo[:, k, tk]],
                                       [w[0][:, kk, :], w[1][:, kk, :]], k == 0, k == KD - 1)
                        if t == T - 1:
                            last.then_inc(split_used, 1)
                    if t < T - 1:
                        last.then_inc(win_acc, 1)

                norm_transpose(l, 0, 0)
                norm_transpose(l, 0, 1)
                for t in range(T):
                    win_first(t)
                    if t + 2 < T:
                        norm_transpose(l, 0, t + 2)

                def win_piece(c, n):
                    pos = POS_WIN + c * KD // 2 + n
                    kp = KP_LAST[n] if c == CH - 1 else n
                    pe.wait_ge(lo_done, split(l, pos))
                    w = [wslot(b, pos, [2, CW]) for b in (w_hi, w_lo)]
                    for kk in range(2):
                        k = 2 * kp + kk
                        first, final = n + kk == 0, n == KD // 2 - 1 and kk == 1
                        for t in range(T):
                            if first and c >= 2:
                                pe.wait_ge(pj[t % 2], at(pj[t % 2], l, (c - 2) * T // 2 + t // 2 + 1))
                            tk = slice(t * P, (t + 1) * P)
                            last = mm3(ps[:, 4 * (c % 2) + t, 0:CW], [ht_hi[:, k, tk], ht_lo[:, k, tk]],
                                       [w[0][:, kk, :], w[1][:, kk, :]], first, final)
                            if final and t < T - 1:
                                last.then_inc(win_acc, 1)
                    last.then_inc(split_used, 1)

                for n in range(KD // 2):
                    win_piece(1, n)
                win_piece(2, 0)
                pe.wait_ge(pj_act, at(pj_act, l, T // 2 + 1))
                pe.wait_ge(small_loaded, (l + 1) * 16 * SMALL)
                settle(pe)
                for n in range(TAPS + 1):
                    nc.tensor.transpose(ps[:, 4, n * 2 * FT:(n + 1) * 2 * FT], rows[0:2 * FT, n, :],
                                        ident[0:2 * FT, 0:2 * FT])
                nc.tensor.transpose(ps[:, 4, C_POS:C_POS + 2 * MT], rows[0:2 * MT, TAPS + 1, :],
                                    ident[0:2 * MT, 0:2 * MT])
                nc.tensor.transpose(ps[:, 4, C_B1:C_B1 + 2], rows[0:2, TAPS + 2, :], ident[0:2, 0:2])\
                    .then_inc(cols_tp, 1)
                for n in range(1, KD // 2):
                    win_piece(2, n)
                pe.wait_ge(cols_ready, at(cols_ready, l, 1))
                win_piece(3, 0)
                win_piece(3, 1)
                pe.wait_ge(lat_ready, at(lat_ready, l, 1))
                pe.wait_ge(kpe_ready, at(kpe_ready, l, 1))
                for n in range(3):
                    pe.wait_ge(pj[n % 2], at(pj[n % 2], l, 2 * T // 2 + n // 2 + 1))
                    c = (QR, 0, P)[n]
                    for t in range(T):
                        last = nc.tensor.transpose(ps[:, n, t * P:(t + 1) * P], proj[:, t, c:c + P], ident[:, :])
                    last.then_inc(lat_tp, 1)
                pe.wait_ge(pj_dve, at(pj_dve, l, 3 * T // 2))
                settle(pe)
                for t in range(T):
                    last = nc.tensor.transpose(ps[0:2 * ROPE, 3, t * P:(t + 1) * P],
                                               kpe_r[:, t, :, :].rearrange("p a b -> p (a b)"), ident[:, :])
                last.then_inc(lat_tp, 1)
                win_piece(3, 2)
                win_piece(3, 3)

                ukv = [b[:, POS_UKV % SLOTS, :].rearrange("p (h c) -> p h c", h=H) for b in (w_hi, w_lo)]
                uq = [[b[:, (POS_UQ + k) % SLOTS, :].rearrange("p (h c) -> p h c", h=H) for b in (w_hi, w_lo)]
                      for k in range(2)]
                lat = lambda n, c: [ht_hi[:, LAT + n, c], ht_lo[:, LAT + n, c]]
                every = slice(0, S)

                def qk_item(j, bank):
                    h = j // 2
                    if j % 2 == 0:
                        for k in range(2):
                            last = mm3(ps[:, bank, :], [uq[k][0][:, h, :], uq[k][1][:, h, :]], lat(1 + k, every),
                                       k == 0, k == 1)
                    else:
                        last = mm3(ps[:, bank, :], [ukv[0][:, h, :], ukv[1][:, h, :]], lat(0, every), True, True)
                    last.then_inc(qk_acc, 1)

                pe.wait_ge(lo_done, split(l, POS_UQ + 1))
                pe.wait_ge(lat_lo, at(lat_lo, l, 3))
                pe.wait_ge(kpe_lo, at(kpe_lo, l, 1))
                for j in range(4):
                    qk_item(j, j)
                for n in range(T):
                    t = T - 1 - n
                    pe.wait_ge(pj[t % 2], at(pj[t % 2], l, 3 * T // 2 + t // 2 + 1))
                    mm3(ps[:, 4 + t, :].rearrange("p (h c) -> p h c", h=H), lat(0, slice(t * P, (t + 1) * P)),
                        [w[:, :, NOPE:2 * NOPE] for w in ukv], True, True).then_inc(v_acc, 1)

                def scores(u):
                    i, pair = unit(u)
                    n = (i + 1) * P
                    qt = slice(i * P, (i + 1) * P)
                    if u >= 2:
                        pe.wait_ge(exp_done, at(exp_done, l, u - 1))
                    sc = score_banks(u)
                    if u < U_MLA:
                        for s in range(2):
                            c = 4 * (pair % 2) + 2 * s
                            mm3(sc[:, s, :], [qs[:, c, qt], qs[:, c + 1, qt]], [ks[:, c, 0:n], ks[:, c + 1, 0:n]],
                                True, False)
                            last = mm(sc[:, s, n - P:n], ident_b[:, :], causal_b[:, :], start=False, stop=True)
                    else:
                        h = (u - U_MLA) // T
                        c = 4 * (h // GROUP)
                        if 2 * n <= S:
                            mm(sc, qs[:, h, qt], ks[:, c:c + 4:2, 0:n], start=True, stop=False)
                            mm(sc, qs[:, h, qt], ks[:, c + 1:c + 4:2, 0:n], start=False, stop=False)
                            last = mm(sc[:, :, n - P:n], ident_b[:, :],
                                      causal_b[:, :].unsqueeze(1).broadcast_to([P, 2, P]), start=False, stop=True)
                        else:
                            for s in range(2):
                                mm(sc[:, s, :], qs[:, h, qt], ks[:, c + 2 * s, 0:n], start=True, stop=False)
                                mm(sc[:, s, :], qs[:, h, qt], ks[:, c + 2 * s + 1, 0:n], start=False, stop=False)
                                last = mm(sc[:, s, n - P:n], ident_b[:, :], causal_b[:, :], start=False, stop=True)
                    last.then_inc(sc_done, 1)

                def turn(u):
                    i, _ = unit(u)
                    pe.wait_ge(p_done, at(p_done, l, u + 1))
                    if u >= 1:
                        pe.wait_ge(pt_done, at(pt_done, l, u))
                    for s in range(2):
                        for b in range(i + 1):
                            last = nc.tensor.transpose(ps[:, 4 + s, b * P:(b + 1) * P],
                                                       probs[:, u % 3, s, b * P:(b + 1) * P], ident[:, :])
                    last.then_inc(t_done, 1)

                def values(u):
                    i, pair = unit(u)
                    qt = slice(i * P, (i + 1) * P)
                    pe.wait_ge(pt_done, at(pt_done, l, u + 1))
                    if u < U_MLA:
                        if u % T == 0 and pair > 0:
                            pe.wait_ge(ol_done, at(ol_done, l, pair))
                        for s in range(2):
                            o = ps[64 * s:64 * s + VD, 6, qt]
                            for b in range(i + 1):
                                last = mm(o, vm[:, b, (2 * pair + s) * VD:(2 * pair + s + 1) * VD],
                                          pts[u % 2][:, s, b * P:(b + 1) * P], start=b == 0, stop=b == i)
                    else:
                        h = (u - U_MLA) // T
                        g = h // GROUP
                        r = pair - H // 2
                        if u % T == 0 and h % 2 == 0:
                            if r >= 2:
                                pe.wait_ge(ol_done, at(ol_done, l, pair - 1))
                            elif r == 0:
                                pe.wait_ge(ol_done, at(ol_done, l, H // 2))
                            else:
                                pe.wait_ge(it_dve, at(it_dve, l, NI))
                        closing = h % 2 == 1 and u % T == T - 1

                        def compressed(hh, stop):
                            m = NCP * (hh % GROUP)
                            return mm(ps[64 * (hh % 2):64 * (hh % 2) + HD, 6 + r % 2, :], v_cmp[m:m + NCP, g, :],
                                      pct[m:m + NCP, g, :], start=False, stop=stop)

                        if closing:
                            if r == 0:
                                pe.wait_ge(pct_ready, at(pct_ready, l, G))
                                settle(pe)
                            compressed(h - 1, True)
                        o = ps[64 * (h % 2):64 * (h % 2) + HD, 6 + r % 2, qt]
                        for s in range(2):
                            c = COL_KV + (s + 1) * 2 * G * HD + G * HD + g * HD
                            for b in range(i + 1):
                                last = mm(o, proj[:, b, c:c + HD], pts[u % 2][:, s, b * P:(b + 1) * P],
                                          start=u % T + s + b == 0, stop=False)
                        if closing:
                            last = compressed(h, True)
                    last.then_inc(pv_done, 1)

                def item(n):
                    kind, i = ITEMS[n]
                    if n >= 1:
                        pe.wait_ge(it_act, at(it_act, l, n))
                        pe.wait_ge(it_dve, at(it_dve, l, n))
                    settle(pe)
                    for t in range(T):
                        if kind == "k":
                            c = [COL_KV + ((1 + e) * 2 * G + i) * HD for e in range(2)]
                            tk = slice(t * P, (t + 1) * P)
                            nc.tensor.transpose(ps[0:HD, 7, tk], proj[:, t, c[0]:c[0] + HD], ident[:, :])
                            last = mm(ps[HD:P, 7, tk], proj[:, t, c[1]:c[1] + HD], ident[:, :], start=True, stop=True)
                        else:
                            c = {"c": COL_KV + i * G * HD, "q": COL_Q + i * P}[kind]
                            last = nc.tensor.transpose(ps[:, 7, t * P:(t + 1) * P], proj[:, t, c:c + P], ident[:, :])
                    last.then_inc(it_tp, 1)

                def hidden(kv):
                    for half in range(2):
                        pos = POS_CMP + 2 * kv + half
                        pe.wait_ge(raw_loaded[pos % SLOTS], landed(l, pos))
                        w1 = wslot(raw, pos, [MT // 2, CHID])
                        for m in range(MT // 2):
                            mt = half * MT // 2 + m
                            last = mm(ps[0:CMP_COLS, 7, 0:CHID], kst[kv][:, mt, :], w1[:, m, :],
                                      start=mt == 0, stop=mt == MT - 1)
                        last.then_inc(cmp_used, 1)

                def project_out(t, slot_w, lhs, start, stop):
                    tk = slice(t * P, (t + 1) * P)
                    for hf in range(2):
                        last = mm3(ps[:, 2 * t + hf, :], [lhs[0][:, tk], lhs[1][:, tk]],
                                   [b[:, slot_w, hf * HALF:(hf + 1) * HALF] for b in (w_hi, w_lo)], start, stop)
                    return last

                def scores_back(b):
                    for t in range(2 * b, 2 * b + 2):
                        for g in range(G):
                            c = (t % 2) * G * P + g * P
                            last = nc.tensor.transpose(ps[:, 7, c:c + P], cs_t[g][:, t * P:(t + 1) * P], ident[:, :])
                    last.then_inc(cs_back, 1)

                for s in range(U + LAG):
                    if s < U_MLA and s % T == 0:
                        pe.wait_ge(q_ready, at(q_ready, l, 2 * (s // T) + 2))
                        pe.wait_ge(kl_done, at(kl_done, l, 2 * (s // T) + 2))
                    if s == U_MLA:
                        pe.wait_ge(it_dve, at(it_dve, l, 5))
                        pe.wait_ge(k_twice, at(k_twice, l, 1))
                    if s == U_MLA + GROUP * T:
                        pe.wait_ge(k_twice, at(k_twice, l, 2))
                    if s < U:
                        scores(s)
                    if s == 1:
                        pe.wait_ge(v_ready, at(v_ready, l, T))
                    if s in (U + 1, U + 2):
                        pe.wait_ge(exp_done, at(exp_done, l, U))
                        pe.wait_ge(lo_done, split(l, POS_WOUT))
                        project_out(s - U - 1, 0, [ht_hi[:, 0, :], ht_lo[:, 0, :]], True, False)
                    if 0 <= s - LAG < U:
                        values(s - LAG)
                    if s < QK_STEPS:
                        j = s + 4
                        if s == 0:
                            pe.wait_ge(v_ready, at(v_ready, l, 1))
                        elif j % 2:
                            pe.wait_ge(qf_done, at(qf_done, l, (j - 1) // 2 + 1))
                        else:
                            pe.wait_ge(kl_done, at(kl_done, l, (j - 1) // 2 + 1))
                        if s - 1 in ITEM_STEP:
                            pe.wait_ge(it_dve, at(it_dve, l, ITEM_STEP.index(s - 1) + 1))
                        if s - 1 in HID_STEP:
                            pe.wait_ge(hid_out, at(hid_out, l, HID_STEP.index(s - 1) + 1))
                        if s - 1 == HIDT_STEP:
                            pe.wait_ge(hid_ready, at(hid_ready, l, 1))
                        if s - 1 == KVC_STEP:
                            pe.wait_ge(kvc_ready, at(kvc_ready, l, 1))
                        qk_item(j, 7)
                    if 0 <= s - 2 < U:
                        turn(s - 2)
                    if T <= s <= QK_STEPS:
                        n = min(s, QK_STEPS - 1) // 2 + 2
                        if s % 2 == 0 and s < QK_STEPS:
                            pe.wait_ge(qf_done, at(qf_done, l, n + 1))
                        else:
                            pe.wait_ge(kl_done, at(kl_done, l, n + 1))
                    if s == ITEM_STEP[0]:
                        pe.wait_ge(q_roped, at(q_roped, l, 1))
                        pe.wait_ge(k_roped, at(k_roped, l, 1))
                    if s in ITEM_STEP:
                        n = ITEM_STEP.index(s)
                        if n == NI - 1:
                            pe.wait_ge(pct_ready, at(pct_ready, l, G))
                        if s - 1 in CS_STEP:
                            pe.wait_ge(cs_out, at(cs_out, l, CS_STEP.index(s - 1) + 1))
                        item(n)
                    if s in HID_STEP:
                        if s == HID_STEP[0]:
                            pe.wait_ge(it_act, at(it_act, l, 2))
                            pe.wait_ge(it_dve, at(it_dve, l, 2))
                            pe.wait_ge(pos_ready, at(pos_ready, l, 1))
                        settle(pe)
                        hidden(HID_STEP.index(s))
                    if s == HIDT_STEP:
                        pe.wait_ge(hid_out, at(hid_out, l, 2))
                        settle(pe)
                        for kv in range(2):
                            c = kv * CMP_COLS
                            last = nc.tensor.transpose(ps[:, 7, c:c + CMP_COLS], hid_rows[:, kv, :],
                                                       ident[0:CMP_COLS, 0:CMP_COLS])
                        last.then_inc(hid_tp, 1)
                    if s == KVC_STEP:
                        pe.wait_ge(hid_ready, at(hid_ready, l, 1))
                        settle(pe)
                        mm(ps[:, 7, S - G * NCP:S], cmp_w2[:, 0:2, :].rearrange("p a b -> p (a b)"),
                           hid[:, 0, :, :].rearrange("p g c -> p (g c)"), start=True, stop=True)
                        for g in range(G):
                            for m in range(GROUP):
                                last = mm(ps[NCP * m:NCP * (m + 1), 7, g * HD:(g + 1) * HD], hid[:, 1, g, :],
                                          cmp_w2[:, 2, :], start=True, stop=True)
                        last.then_inc(kvc_acc, 1)
                    if s in CS_STEP:
                        g = CS_STEP.index(s)
                        n = sum(t < s for t in ITEM_STEP)
                        pe.wait_ge(it_dve, at(it_dve, l, n))
                        pe.wait_ge(kvc_ready, at(kvc_ready, l, 1))
                        settle(pe)
                        for m in range(GROUP):
                            q, cz = qs[:, g * GROUP + m, :], slice(P - NCP * (m + 1), 2 * P - NCP * (m + 1))
                            mm(ps[:, 7, :], kcz_hi[:, g, cz], q, start=m == 0, stop=False)
                            last = mm(ps[:, 7, :], kcz_lo[:, g, cz], q, start=False, stop=m == GROUP - 1)
                        last.then_inc(cs_acc, 1)
                    if s in BACK_STEP:
                        b = BACK_STEP.index(s)
                        if b == 0:
                            pe.wait_ge(cs_out, at(cs_out, l, G))
                        else:
                            pe.wait_ge(cs_in, at(cs_in, l, 1))
                        scores_back(b)
                    if s in PC_STEP:
                        g = PC_STEP.index(s)
                        if g == 0:
                            pe.wait_ge(pc_done, at(pc_done, l, 1))
                        else:
                            pe.wait_ge(pct_ready, at(pct_ready, l, g))
                        for t in range(T):
                            last = nc.tensor.transpose(ps[:, 7, t * P:(t + 1) * P],
                                                       scp[:, t, g * GROUP:(g + 1) * GROUP, :], ident[:, :])
                        last.then_inc(pc_tp, 1)

                for k in range(KD - SLOTS):
                    pe.wait_ge(lo_done, split(l, POS_WOUT + k))
                    for t in range(2 if k == 0 else 0, T):
                        if k == 0 and t == T - 1:
                            pe.wait_ge(ol_done, at(ol_done, l, H))
                        last = project_out(t, k % SLOTS, [ht_hi[:, k, :], ht_lo[:, k, :]], k == 0, False)
                    last.then_inc(split_used, 1)
                for t in range(T):
                    for k in range(KD - SLOTS, KD):
                        if t == 0:
                            pe.wait_ge(lo_done, split(l, POS_WOUT + k))
                        last = project_out(t, k % SLOTS, [ht_hi[:, k, :], ht_lo[:, k, :]], False, k == KD - 1)
                        if t == T - 1:
                            last.then_inc(split_used, 1)
                    if t < T - 1:
                        last.then_inc(out_acc, 1)
                    if t >= 1:
                        norm_transpose(l, 1, t - 1)
                norm_transpose(l, 1, T - 1)

                def up_half(pos, bank, turn, toks=slice(0, S)):
                    w = [wslot(b, pos, [KD, P]) for b in (w_hi, w_lo)]
                    for k in range(KD):
                        last = mm3(ps[:, bank, toks], [w[0][:, k, :], w[1][:, k, :]],
                                   [ht_hi[:, k, toks], ht_lo[:, k, toks]], k == 0, k == KD - 1)
                    return last

                first, rest = slice(0, S - P), slice(S - P, S)
                for uv in range(2):
                    pe.wait_ge(lo_done, split(l, POS_UP + uv))
                    pe.wait_ge(hl_done, at(hl_done, l, 4 * T - 2))
                    up_half(POS_UP + uv, uv, 0, first)
                pe.wait_ge(hl_done, at(hl_done, l, 4 * T))
                for uv in range(2):
                    up_half(POS_UP + uv, uv, 0, rest).then_inc(split_used, 1)
                for uv in range(2):
                    pe.wait_ge(lo_done, split(l, POS_UP + 2 + uv))
                    up_half(POS_UP + 2 + uv, 4 + uv, 0).then_inc(split_used, 1)
                with pe.Fori(0, FT // 2 - 1) as j:
                    for e in range(2):
                        pe.wait_ge(g_done, at(g_done, l, e + 1 + 2 * j))
                        for uv in range(2):
                            pos = POS_UP + SLOTS + 2 * e + uv
                            pe.wait_ge(lo_done, split(l, pos, SLOTS * j))
                            up_half(pos, 4 * e + uv, SLOTS * j).then_inc(split_used, 1)

                g_pair = [[g_hi[:, slot, :], g_lo[:, slot, :]] for slot in range(2)]

                def down_ready(n, turn=0):
                    pe.wait_ge(lo_done, split(l, POS_DOWN + n, turn))
                    pe.wait_ge(gl_done, at(gl_done, l, n + 1 + turn))

                down_ready(0)
                for t in (1, 3, 0, 2):
                    if t == 0:
                        pe.wait_ge(g_done, at(g_done, l, FT - 1))
                    if t == 2:
                        pe.wait_ge(g_done, at(g_done, l, FT))
                    last = project_out(t, 0, g_pair[0], True, False)
                last.then_inc(split_used, 1)
                for k in range(1, SLOTS):
                    down_ready(k)
                    for t in range(T):
                        last = project_out(t, k, g_pair[k % 2], False, False)
                    last.then_inc(split_used, 1)
                with pe.Fori(0, FT // SLOTS - 1) as j:
                    for e in range(SLOTS):
                        down_ready(SLOTS + e, SLOTS * j)
                        for t in range(T):
                            last = project_out(t, e, g_pair[e % 2], False, False)
                        last.then_inc(split_used, 1)
                for k in range(FT - 2, FT):
                    down_ready(k)
                for t in range(T):
                    for k in range(FT - 2, FT):
                        last = project_out(t, k % SLOTS, g_pair[k % 2], False, k == FT - 1)
                        if t == T - 1:
                            last.then_inc(split_used, 1)
                    if t < T - 1:
                        last.then_inc(out_acc, 1)


_INS = ["x", "attn_norm", "w_in", "mla_q_norm", "mla_kv_norm", "mla_w_uq", "mla_w_ukv", "nsa_gate_bias",
        "nsa_cmp_pos", "nsa_cmp_w1", "nsa_cmp_b1", "nsa_cmp_w2", "w_out", "ffn_norm", "ffn_w_up", "ffn_conv_w",
        "ffn_conv_b", "ffn_w_down", "final_norm"]


def kernel(**inputs):
    import numpy as _np
    import concourse.bacc as _bacc
    from concourse import mybir as _mybir
    from concourse.bass_utils import run_bass_kernel_spmd as _run

    nc = _bacc.Bacc("TRN2", target_bir_lowering=False, num_devices=1)
    arrays, args = {}, {}
    given = {n: _np.ascontiguousarray(inputs[n]) for n in _INS}
    for name, v in {**given, **shape_constants()}.items():
        arrays[f"in_{name}_dram"] = v
        args[name] = nc.dram_tensor(f"in_{name}_dram", v.shape, _mybir.dt.from_np(v.dtype), kind="ExternalInput").ap()
    out = nc.dram_tensor("out_0_dram", (1, S, D), _mybir.dt.float32, kind="ExternalOutput").ap()
    hybrid_layers(nc, args, out)
    r = _run(nc, [arrays], core_ids=[0])
    return r.results[0]["out_0_dram"]
```
